# Optimizing a Trainium2 kernel written in Bass

```python
import math
import jax, jax.numpy as jnp
from jax import lax
import numpy as np

D_MODEL = 1024
BATCH = 1
SEQ = 128
DEPTH = 2
DEC_BATCH = 1
DEC_SEQ = 1024
PAST_LEN = 128

GRID_W = 64
N_MIXERS = 2
N_HYENA = (DEPTH + 1) // 2
N_SSD = DEPTH // 2
RMS_EPS = 1e-6
HY_SHORT_W = 3
HY_EMB = 33
HY_BANDS = (HY_EMB - 1) // 2
HY_HIDDEN = 64
HY_SHORT_DECAY_FRAC = 0.3
HY_LONG_DECAY_FRAC = 1.5
HY_DECAY_TARGET = 1e-2
HY_MAX_DECAY = math.log(HY_DECAY_TARGET) / HY_SHORT_DECAY_FRAC
HY_MIN_DECAY = math.log(HY_DECAY_TARGET) / HY_LONG_DECAY_FRAC
SSD_D_INNER = 2 * D_MODEL
SSD_HEAD_DIM = 64
SSD_HEADS = SSD_D_INNER // SSD_HEAD_DIM
SSD_GROUPS = 4
SSD_STATE = 128
SSD_CONV_W = 5
SSD_CHUNK = 128
SSD_XBC = SSD_D_INNER + 2 * SSD_GROUPS * SSD_STATE
SSD_IN = SSD_D_INNER + SSD_XBC + 2 * SSD_HEADS
N_EXPERTS = 16
EXPERT_FF = 1024
EC_FACTOR = 2

kernel_name = 'hybrid_hyena_ssd_expert_choice_dit_step'

def _rmsnorm(x, g):
    x32 = x.astype(jnp.float32)
    y = x32 * lax.rsqrt(jnp.mean(x32 * x32, axis=-1, keepdims=True) + RMS_EPS)
    return y.astype(x.dtype) * g

def _adaln(cond, ada_w, ada_b):
    m = jax.nn.silu(cond) @ ada_w + ada_b
    return jnp.split(m[:, None, :], 6, axis=-1)

def _modulate(h, shift, scale):
    return h * (1 + scale) + shift

def _dwconv(x, w, b):
    k, ch = w.shape
    y = lax.conv_general_dilated(x, w[:, None, :].astype(x.dtype), window_strides=(1,),
                                 padding=[(k // 2, k // 2)],
                                 dimension_numbers=('NWC', 'WIO', 'NWC'),
                                 feature_group_count=ch)
    return y + b

def _sincos_2d(rows, cols, d):
    q = d // 4
    omega = 1.0 / (10000.0 ** (jnp.arange(q, dtype=jnp.float32) / q))
    t = jnp.arange(rows * cols)
    er = (t // cols).astype(jnp.float32)[:, None] * omega[None, :]
    ec = (t % cols).astype(jnp.float32)[:, None] * omega[None, :]
    return jnp.concatenate([jnp.sin(er), jnp.cos(er), jnp.sin(ec), jnp.cos(ec)], axis=-1)

def _hyena_filters(length, f_w1, f_b1, f_w2, f_b2, f_w3, f_freq):
    t = jnp.linspace(0.0, 1.0, length, dtype=jnp.float32)[:, None]
    w = 2.0 * math.pi * jnp.arange(length, dtype=jnp.float32)[:, None] / length
    f = jnp.linspace(1e-4, HY_BANDS - 1, HY_BANDS, dtype=jnp.float32)[None, :]
    z = jnp.concatenate([t, jnp.cos(f * w), -jnp.sin(f * w)], axis=-1)
    h = jnp.sin(f_freq * (z @ f_w1 + f_b1))
    h = jnp.sin(f_freq * (h @ f_w2 + f_b2))
    h = (h @ f_w3).astype(jnp.float32)
    deltas = jnp.linspace(HY_MIN_DECAY, HY_MAX_DECAY, D_MODEL, dtype=jnp.float32)
    window = jnp.exp(-t * jnp.abs(deltas)[None, :])
    return h[:, :D_MODEL] * window, h[:, D_MODEL:] * window

def _bidir_long_conv(u, h_fwd, h_bwd, bias):
    b, length, ch = u.shape
    n = 2 * length
    k = jnp.concatenate([h_fwd, jnp.zeros((1, ch), jnp.float32), h_bwd[1:][::-1]], axis=0)
    kf = jnp.fft.rfft(k, n=n, axis=0)
    u32 = u.astype(jnp.float32)
    uf = jnp.fft.rfft(u32, n=n, axis=1)
    y = jnp.fft.irfft(uf * kf[None], n=n, axis=1)[:, :length]
    return (y + u32 * bias.astype(jnp.float32)).astype(u.dtype)

def _hyena_mixer(h, in_w, in_b, short_w, short_b, f_w1, f_b1, f_w2, f_b2, f_w3, f_freq, f_bias, out_w):
    length = h.shape[1]
    u = _dwconv(h @ in_w + in_b, short_w, short_b)
    x0 = u[..., :D_MODEL]
    x1 = u[..., D_MODEL:2 * D_MODEL]
    v = u[..., 2 * D_MODEL:]
    h_fwd, h_bwd = _hyena_filters(length, f_w1, f_b1, f_w2, f_b2, f_w3, f_freq)
    v = _bidir_long_conv(v * x1, h_fwd, h_bwd, f_bias)
    return (v * x0) @ out_w

def _ssd_scan(x, dt, a, bm, cm, init):
    b, length = x.shape[:2]
    nc = length // SSD_CHUNK
    q, g, r = SSD_CHUNK, SSD_GROUPS, SSD_HEADS // SSD_GROUPS
    x = x.reshape(b, nc, q, g, r, SSD_HEAD_DIM)
    dt = dt.reshape(b, nc, q, g, r)
    bm = bm.reshape(b, nc, q, g, SSD_STATE)
    cm = cm.reshape(b, nc, q, g, SSD_STATE)
    a_cum = jnp.cumsum(dt * a.reshape(g, r), axis=2)
    xdt = x * dt[..., None]
    seg = a_cum[:, :, :, None] - a_cum[:, :, None, :]
    causal = jnp.tril(jnp.ones((q, q), dtype=bool))[None, None, :, :, None, None]
    decay = jnp.exp(jnp.where(causal, seg, -jnp.inf))
    cb = jnp.einsum('bclgn,bcsgn->bclsg', cm, bm)
    y_diag = jnp.einsum('bclsgr,bcsgrp->bclgrp', cb[..., None] * decay, xdt)
    decay_end = jnp.exp(a_cum[:, :, -1:] - a_cum)
    chunk_states = jnp.einsum('bcsgn,bcsgrp->bcgrpn', bm, xdt * decay_end[..., None])
    chunk_decay = jnp.exp(a_cum[:, :, -1])

    def step(s, inp):
        st, dec = inp
        return s * dec[..., None, None] + st, s

    init_g = init.astype(jnp.float32).reshape(b, g, r, SSD_HEAD_DIM, SSD_STATE)
    final, starts = lax.scan(step, init_g, (jnp.moveaxis(chunk_states, 1, 0), jnp.moveaxis(chunk_decay, 1, 0)))
    starts = jnp.moveaxis(starts, 0, 1)
    y_off = jnp.einsum('bclgn,bcgrpn->bclgrp', cm, starts) * jnp.exp(a_cum)[..., None]
    y = (y_diag + y_off).reshape(b, length, SSD_HEADS, SSD_HEAD_DIM)
    return y, final.reshape(b, SSD_HEADS, SSD_HEAD_DIM, SSD_STATE)

def _flip(t):
    return jnp.flip(t, axis=1)

def _ssd_mixer(h, init_f, init_b, in_w, conv_w, conv_b, dt_bias, a_log, d_skip, norm_g, out_w):
    b, length, _ = h.shape
    proj = h @ in_w
    z = proj[..., :SSD_D_INNER]
    xbc = jax.nn.silu(_dwconv(proj[..., SSD_D_INNER:SSD_D_INNER + SSD_XBC], conv_w, conv_b))
    dt_raw = proj[..., SSD_D_INNER + SSD_XBC:]
    gn = SSD_GROUPS * SSD_STATE
    xh = xbc[..., :SSD_D_INNER].reshape(b, length, SSD_HEADS, SSD_HEAD_DIM).astype(jnp.float32)
    bm = xbc[..., SSD_D_INNER:SSD_D_INNER + gn].reshape(b, length, SSD_GROUPS, SSD_STATE).astype(jnp.float32)
    cm = xbc[..., SSD_D_INNER + gn:].reshape(b, length, SSD_GROUPS, SSD_STATE).astype(jnp.float32)
    dt = jax.nn.softplus(dt_raw.astype(jnp.float32).reshape(b, length, 2, SSD_HEADS) + dt_bias.astype(jnp.float32))
    a = -jnp.exp(a_log.astype(jnp.float32))
    y_f, s_f = _ssd_scan(xh, dt[:, :, 0], a[0], bm, cm, init_f)
    y_b, s_b = _ssd_scan(_flip(xh), _flip(dt[:, :, 1]), a[1], _flip(bm), _flip(cm), init_b)
    y = y_f + _flip(y_b) + d_skip.astype(jnp.float32)[:, None] * xh
    y = y.reshape(b, length, SSD_D_INNER) * jax.nn.silu(z.astype(jnp.float32))
    y = _rmsnorm(y, norm_g).astype(h.dtype)
    return y @ out_w, s_f, s_b

def _expert_choice_ffn(h, w_router, w_gate, w_up, w_down):
    b, length, _ = h.shape
    cap = EC_FACTOR * length // N_EXPERTS
    aff = jax.nn.softmax((h @ w_router).astype(jnp.float32), axis=-1)
    gate, idx = lax.top_k(jnp.swapaxes(aff, 1, 2), cap)
    bi = jnp.arange(b)[:, None, None]
    xe = h[bi, idx]
    hid = jax.nn.silu(jnp.einsum('becd,edf->becf', xe, w_gate)) * jnp.einsum('becd,edf->becf', xe, w_up)
    ye = jnp.einsum('becf,efd->becd', hid, w_down)
    return jnp.zeros_like(h).at[bi, idx].add((gate[..., None] * ye).astype(h.dtype))

def setup_inputs(seed: int = 0) -> dict:
    key = jax.random.key(seed)
    ks = iter(jax.random.split(key, 48))

    def nrm(shape, scale):
        return jax.random.normal(next(ks), shape, jnp.float32) * scale

    dt0 = jnp.exp(jax.random.uniform(next(ks), (N_SSD, 2, SSD_HEADS), jnp.float32,
                                     math.log(1e-3), math.log(1e-1)))
    return {
        'x_prompt': nrm((BATCH, SEQ, D_MODEL), 1.0),
        'x_sample': nrm((DEC_BATCH, DEC_SEQ, D_MODEL), 1.0),
        'state_ssd': nrm((DEC_BATCH, N_SSD, 2, SSD_HEADS, SSD_HEAD_DIM, SSD_STATE), 0.1),
        'c': nrm((DEC_BATCH, D_MODEL), 1.0),
        'c_ctx': nrm((D_MODEL,), 1.0),
        'norm_g': 1.0 + nrm((DEPTH, 2, D_MODEL), 0.05),
        'ada_w': nrm((DEPTH, D_MODEL, 6 * D_MODEL), 0.5 * D_MODEL ** -0.5),
        'ada_b': nrm((DEPTH, 6 * D_MODEL), 0.01),
        'hy_in_w': nrm((N_HYENA, D_MODEL, 3 * D_MODEL), D_MODEL ** -0.5),
        'hy_in_b': nrm((N_HYENA, 3 * D_MODEL), 0.01),
        'hy_short_w': nrm((N_HYENA, HY_SHORT_W, 3 * D_MODEL), HY_SHORT_W ** -0.5),
        'hy_short_b': nrm((N_HYENA, 3 * D_MODEL), 0.01),
        'hy_f_w1': nrm((N_HYENA, HY_EMB, HY_HIDDEN), HY_EMB ** -0.5),
        'hy_f_b1': nrm((N_HYENA, HY_HIDDEN), 0.1),
        'hy_f_w2': nrm((N_HYENA, HY_HIDDEN, HY_HIDDEN), HY_HIDDEN ** -0.5),
        'hy_f_b2': nrm((N_HYENA, HY_HIDDEN), 0.1),
        'hy_f_w3': nrm((N_HYENA, HY_HIDDEN, 2 * D_MODEL), 0.1 * HY_HIDDEN ** -0.5),
        'hy_f_freq': 1.0 + nrm((N_HYENA, HY_HIDDEN), 0.05),
        'hy_f_bias': nrm((N_HYENA, D_MODEL), 1.0),
        'hy_out_w': nrm((N_HYENA, D_MODEL, D_MODEL), D_MODEL ** -0.5),
        'ssd_in_w': nrm((N_SSD, D_MODEL, SSD_IN), D_MODEL ** -0.5),
        'ssd_conv_w': nrm((N_SSD, SSD_CONV_W, SSD_XBC), SSD_CONV_W ** -0.5),
        'ssd_conv_b': nrm((N_SSD, SSD_XBC), 0.01),
        'ssd_dt_bias': dt0 + jnp.log(-jnp.expm1(-dt0)),
        'ssd_A_log': jnp.log(jax.random.uniform(next(ks), (N_SSD, 2, SSD_HEADS), jnp.float32, 1.0, 16.0)),
        'ssd_D': 1.0 + nrm((N_SSD, SSD_HEADS), 0.05),
        'ssd_norm_g': 1.0 + nrm((N_SSD, SSD_D_INNER), 0.05),
        'ssd_out_w': nrm((N_SSD, SSD_D_INNER, D_MODEL), SSD_D_INNER ** -0.5),
        'moe_router': nrm((DEPTH, D_MODEL, N_EXPERTS), D_MODEL ** -0.5),
        'moe_w_gate': nrm((DEPTH, N_EXPERTS, D_MODEL, EXPERT_FF), D_MODEL ** -0.5),
        'moe_w_up': nrm((DEPTH, N_EXPERTS, D_MODEL, EXPERT_FF), D_MODEL ** -0.5),
        'moe_w_down': nrm((DEPTH, N_EXPERTS, EXPERT_FF, D_MODEL), EXPERT_FF ** -0.5),
        'final_norm_g': 1.0 + nrm((D_MODEL,), 0.05),
    }

def reference(x_prompt, x_sample, state_ssd, c, c_ctx, norm_g, ada_w, ada_b,
              hy_in_w, hy_in_b, hy_short_w, hy_short_b, hy_f_w1, hy_f_b1, hy_f_w2, hy_f_b2,
              hy_f_w3, hy_f_freq, hy_f_bias, hy_out_w,
              ssd_in_w, ssd_conv_w, ssd_conv_b, ssd_dt_bias, ssd_A_log, ssd_D, ssd_norm_g, ssd_out_w,
              moe_router, moe_w_gate, moe_w_up, moe_w_down, final_norm_g):
    rows = x_sample.shape[1] // GRID_W
    xp = x_prompt
    xs = x_sample + _sincos_2d(rows, GRID_W, D_MODEL).astype(x_sample.dtype)[None]
    new_ssd = []
    for i in range(DEPTH):
        sh1p, sc1p, g1p, sh2p, sc2p, g2p = _adaln(c_ctx[None, :], ada_w[i], ada_b[i])
        sh1s, sc1s, g1s, sh2s, sc2s, g2s = _adaln(c, ada_w[i], ada_b[i])
        hp = _modulate(_rmsnorm(xp, norm_g[i, 0]), sh1p, sc1p)
        hs = _modulate(_rmsnorm(xs, norm_g[i, 0]), sh1s, sc1s)
        j = i // N_MIXERS
        if i % N_MIXERS == 0:
            hy = (hy_in_w[j], hy_in_b[j], hy_short_w[j], hy_short_b[j], hy_f_w1[j], hy_f_b1[j],
                  hy_f_w2[j], hy_f_b2[j], hy_f_w3[j], hy_f_freq[j], hy_f_bias[j], hy_out_w[j])
            mp = _hyena_mixer(hp, *hy)
            ms = _hyena_mixer(hs, *hy)
        else:
            sp = (ssd_in_w[j], ssd_conv_w[j], ssd_conv_b[j], ssd_dt_bias[j], ssd_A_log[j],
                  ssd_D[j], ssd_norm_g[j], ssd_out_w[j])
            zeros = jnp.zeros((xp.shape[0], SSD_HEADS, SSD_HEAD_DIM, SSD_STATE), jnp.float32)
            mp, s_f, s_b = _ssd_mixer(hp, zeros, zeros, *sp)
            new_ssd.append(jnp.stack([s_f, s_b], axis=1))
            ms, _, _ = _ssd_mixer(hs, state_ssd[:, j, 0], state_ssd[:, j, 1], *sp)
        xp = xp + g1p * mp
        xs = xs + g1s * ms
        moe = (moe_router[i], moe_w_gate[i], moe_w_up[i], moe_w_down[i])
        xp = xp + g2p * _expert_choice_ffn(_modulate(_rmsnorm(xp, norm_g[i, 1]), sh2p, sc2p), *moe)
        xs = xs + g2s * _expert_choice_ffn(_modulate(_rmsnorm(xs, norm_g[i, 1]), sh2s, sc2s), *moe)
    y_prompt = _rmsnorm(xp, final_norm_g)
    y_sample = _rmsnorm(xs, final_norm_g)
    new_state_ssd = jnp.stack(new_ssd, axis=1)
    return (y_prompt, y_sample, new_state_ssd)


_drawn_inputs = setup_inputs


def setup_inputs(seed=0):
    import zlib

    import numpy as np

    out = dict(_drawn_inputs(seed))
    spreads = {}
    factors = {'state_ssd': 3.582,
     'hy_in_b': 4.124,
     'hy_short_b': 4.477,
     'hy_f_freq': 3.306,
     'ssd_conv_b': 3.818,
     'ssd_D': 8.0,
     'ssd_norm_g': 3.925}
    for name, (base, spread) in spreads.items():
        noise = np.random.default_rng([zlib.crc32(name.encode()), seed]).standard_normal(out[name].shape)
        drawn = base * np.exp(spread * noise) if base else spread * noise
        out[name] = __import__('jax').numpy.asarray(drawn.astype(out[name].dtype))
    for name, factor in factors.items():
        out[name] = (out[name] * factor).astype(out[name].dtype)
    return out
```

```python
from contextlib import ExitStack

import numpy as np

import concourse.bass as bass
from concourse import mybir

F32 = mybir.dt.float32
U32 = mybir.dt.uint32
ALU = mybir.AluOpType
ACT = mybir.ActivationFunctionType
AX = mybir.AxisListType

P = 128
D = 1024
KD = D // P
TILES = 9
CTX_ROWS = 128
LAT = 1024
TOK = CTX_ROWS + LAT
CTX, LATENT = 0, 1
EPS = 1e-6
HALF = 512
HY_HID = 64
HY_EMB = 33
NFFT = 2 * LAT
HEADS = 32
HEAD = 64
INNER = 2 * D
GROUPS = 4
XBC_TILES = 24
Z_TILES = 16
EXPERTS = 16
CAP_LAT = 2 * LAT // EXPERTS
CAP_CTX = 2 * CTX_ROWS // EXPERTS
SLOTS = CAP_LAT + CAP_CTX
GAPPED = TOK + 2
LAT_AT = CTX_ROWS + 2
V_G1, V_A2, V_B2, V_G2 = range(4)


def vec_row(layer, cond, which):
    return (layer * 2 + cond) * 4 + which


class Chain:

    def __init__(self, eng, sem, base=0):
        self.eng, self.sem, self.base, self.n = eng, sem, base, 0

    def step(self, ins):
        ins.then_inc(self.sem, 1)
        self.n += 1
        return self.base + self.n

    def link(self, ins):
        self.eng.wait_ge(self.sem, self.step(ins))


class Mem:

    def __init__(self, nc, ctx, prefix=""):
        self.nc, self.ctx, self.prefix, self.sems = nc, ctx, prefix, []
        ctx.callback(self.clear)

    def clear(self):
        self.nc.clear_and_free_semaphores(self.sems)
        self.nc.all_engine_barrier()

    def sb(self, name, shape, dt=F32):
        return self.ctx.enter_context(self.nc.sbuf_tensor(self.prefix + name, shape, dt))

    def psum(self, name="banks"):
        return self.ctx.enter_context(self.nc.psum_tensor(self.prefix + name, [P, 8, HALF], F32))

    def sem(self, name):
        self.sems.append(self.nc.alloc_semaphore(name=self.prefix + name))
        return self.sems[-1]


def phase_modulation(nc, io, keep):
    ada = io["ada_w"].rearrange("l (k p) n -> p l k n", p=P)
    RING = 3
    COLUMNS = 6 * D // HALF
    with ExitStack() as ctx:
        m = Mem(nc, ctx, "mod_")
        cond_rows = m.sb("cond_rows", [16, P])
        cond_t = m.sb("cond_t", [P, KD, 2])
        w = m.sb("w", [P, RING, KD, HALF])
        bias = m.sb("bias", [2, 2 * 6 * D])
        rows = m.sb("rows", [2, 2 * 6 * D])
        a_rows = m.sb("a_rows", [2, 2, D])
        gains = m.sb("gains", [2, 2, D])
        mrows = m.sb("mrows", [96, 2, P])
        stage = m.sb("stage", [P, 4, P])
        pb = m.psum()
        s_c = m.sem("cond_in")
        s_stage = m.sem("stage_in")
        s_bias = m.sem("bias_in")
        s_w = [m.sem(f"w_in{i}") for i in range(RING)]
        s_ct = m.sem("cond_transposed")
        s_silu = m.sem("cond_ready")
        s_acc = m.sem("piece_summed")
        s_row = m.sem("piece_in_rows")
        s_dve = m.sem("dve")
        s_arow = m.sem("a_rows_ready")
        s_out = m.sem("rows_in_dram")
        s_back = m.sem("rows_back")
        s_tr = m.sem("param_transposed")
        s_done = m.sem("params_kept")
        mod_dram = io["mod_dram"]
        vec_dram = io["vec_dram"]

        with nc.Block() as block:

            @block.sync
            def _(sp):
                sp.dma_start(cond_rows[0:8, :], io["c_ctx"].rearrange("(k p) -> k p", p=P)).then_inc(s_c, 16)
                sp.dma_start(cond_rows[8:16, :], io["c"][0].rearrange("(k p) -> k p", p=P)).then_inc(s_c, 16)
                for r in range(RING):
                    sp.dma_start(w[:, r, :, :], ada[:, 0, :, r * HALF:(r + 1) * HALF]).then_inc(s_w[r], 16)
                for layer in range(2):
                    with sp.Fori(0 if layer else 1, COLUMNS // RING) as i:
                        for r in range(RING):
                            sp.wait_ge(s_acc, i * RING + (layer * COLUMNS + r - RING + 1))
                            sp.dma_start(w[:, r, :, :], ada[:, layer, :, bass.ds((i * RING + r) * HALF, HALF)]
                                         ).then_inc(s_w[r], 16)
                sp.wait_ge(s_row, 2 * COLUMNS)
                sp.dma_start(mod_dram, rows[:, :]).then_inc(s_out, 16)
                sp.wait_ge(s_arow, 2)
                for layer in range(2):
                    for which, src in ((V_G1, 2), (V_B2, 3), (V_G2, 5)):
                        sp.dma_start(vec_dram[layer, :, which, :],
                                     rows[:, (layer * 6 + src) * D:(layer * 6 + src + 1) * D]).then_inc(s_out, 16)
                    sp.dma_start(vec_dram[layer, :, V_A2, :], a_rows[:, layer, :]).then_inc(s_out, 16)
                sp.wait_ge(s_out, 16 * 9)
                for c in range(2):
                    sp.dma_start(mrows[:, c, :], mod_dram[c].rearrange("(r p) -> r p", p=P)).then_inc(s_back, 16)

            @block.scalar
            def _(act):
                for c in range(2):
                    act.dma_start(bias[c:c + 1, :], io["ada_b"].rearrange("(a l) n -> a (l n)", a=1)).then_inc(s_bias, 16)
                    act.dma_start(gains[c:c + 1, :, :], io["norm_g"][:, 1, :].rearrange("(a l) d -> a l d", a=1)
                                  ).then_inc(s_bias, 16)
                for n, (src, at, cnt) in enumerate(keep["param_rows"]):
                    act.dma_start(stage[at[1]:at[1] + cnt, at[0], :], src).then_inc(s_stage, 16)
                for h in range(2):
                    act.dma_start(keep["d_skip"][h * HEAD:(h + 1) * HEAD, :],
                                  bass.AP(io["ssd_D"].tensor, h, [[0, HEAD], [2, Z_TILES]]),
                                  allow_slow_non_contiguous=True).then_inc(s_stage, 16)
                act.wait_ge(s_ct, 1)
                for c in range(2):
                    act.activation(cond_t[:, :, c], pb[:, 0, 8 * c:8 * c + 8], ACT.Silu).then_inc(s_silu, 1)

            @block.tensor
            def _(pe):
                pe.wait_ge(keep["s_const"], 16)
                pe.wait_ge(s_c, 32)
                pe.transpose(pb[:, 0, 0:16], cond_rows[:, :], keep["ident"][0:16, 0:16]).then_inc(s_ct, 1)
                pe.wait_ge(s_silu, 2)
                for layer in range(2):
                    with pe.Fori(0, COLUMNS // RING) as i:
                        for r in range(RING):
                            pe.wait_ge(s_w[r], (i + (layer * COLUMNS // RING + 1)) * 16)
                            pe.wait_ge(s_row, i * RING + (COLUMNS + r - RING + 1 if layer else 0))
                            for k in range(KD):
                                ins = pe.matmul(pb[0:2, 1 + r, :], cond_t[:, k, :], w[:, r, k, :],
                                                start=(k == 0), stop=(k == KD - 1))
                            ins.then_inc(s_acc, 1)
                pe.wait_ge(s_stage, 16 * (len(keep["param_rows"]) + 2))
                for n, cnt in enumerate(keep["param_counts"]):
                    pe.transpose(pb[:, 4 + n // 4, (n % 4) * P:(n % 4) * P + cnt], stage[0:cnt, n, :],
                                 keep["ident"][0:cnt, 0:cnt]).then_inc(s_tr, 1)
                pe.wait_ge(s_back, 32)
                for c in range(2):
                    pe.transpose(pb[:, 6, c * P:c * P + 96], mrows[:, c, :], keep["ident"][0:96, 0:96]).then_inc(s_tr, 1)

            @block.vector
            def _(dve):
                ch = Chain(dve, s_dve)
                ch.link(dve.memset(keep["eps"][:, :], EPS))
                dve.wait_ge(s_bias, 64)
                for layer in range(2):
                    with dve.Fori(0, COLUMNS // RING) as i:
                        for r in range(RING):
                            dve.wait_ge(s_acc, i * RING + (layer * COLUMNS + r + 1))
                            at = bass.ds((i * RING + (layer * COLUMNS + r)) * HALF, HALF)
                            dve.tensor_tensor(rows[:, at], pb[0:2, 1 + r, :], bias[:, at], ALU.add).then_inc(s_row, 1)
                dve.wait_ge(s_row, 2 * COLUMNS)
                for layer in range(2):
                    dve.scalar_tensor_tensor(a_rows[:, layer, :], rows[:, (layer * 6 + 4) * D:(layer * 6 + 5) * D],
                                             1.0, gains[:, layer, :], ALU.add, ALU.mult).then_inc(s_arow, 1)
                dve.wait_ge(s_tr, 6)
                for n, cnt in enumerate(keep["param_counts"]):
                    dve.tensor_copy(keep["prm"][:, n, 0:cnt], pb[:, 4 + n // 4, (n % 4) * P:(n % 4) * P + cnt]
                                    ).then_inc(s_done, 1)
                for c in range(2):
                    dve.tensor_copy(keep["mod"][:, c, :], pb[:, 6, c * P:c * P + 96]).then_inc(s_done, 1)
                dve.wait_ge(s_done, 6)
                for layer in range(2):
                    for c in range(2):
                        ch.link(dve.scalar_tensor_tensor(
                            keep["gain1"][:, layer, c, :], keep["mod"][:, c, layer * 48 + 8:layer * 48 + 16], 1.0,
                            keep["prm"][:, 3, layer * 8:layer * 8 + 8], ALU.add, ALU.mult))


def phase_norm(nc, io, keep, layer):
    x_rows = io["x_dram"].rearrange("(t p) d -> t p d", p=P)
    with ExitStack() as ctx:
        m = Mem(nc, ctx, f"norm{layer}_")
        xr = m.sb("x", [P, 2, D])
        pos = m.sb("pos", [P, 2, D])
        xn = m.sb("xn", [P, 2, D])
        junk = m.sb("junk", [P, D])
        st = m.sb("stats", [P, 2, 3])
        pb = m.psum()
        s_x = [m.sem(f"x_in{b}") for b in range(2)]
        s_pos = [m.sem(f"pos_in{b}") for b in range(2)]
        s_add = m.sem("x_added")
        s_st = [m.sem(f"x_stored{b}") for b in range(2)]
        s_sq = m.sem("squared")
        s_rt = m.sem("root")
        s_rc = m.sem("reciprocal")
        s_xn = m.sem("scaled")
        s_tr = m.sem("transposed")
        s_ea = m.sem("evicted_act")
        s_ed = m.sem("evicted_dve")
        hT = keep["hT"]

        def src(t):
            if layer:
                return x_rows[t]
            return io["x_prompt"][0] if t == 0 else io["x_sample"][0, (t - 1) * P:t * P, :]

        def args(t, k):
            c = CTX if t == 0 else LATENT
            return keep["gain1"][:, layer, c, k:k + 1], keep["mod"][:, c, layer * 48 + k:layer * 48 + k + 1]

        with nc.Block() as block:

            @block.sync
            def _(sp):
                for t in range(TILES):
                    b, u = t % 2, t // 2
                    if t >= 2:
                        sp.wait_ge(s_xn, t - 1)
                        if not layer:
                            sp.wait_ge(s_st[b], 16 * u)
                    sp.dma_start(xr[:, b, :], src(t)).then_inc(s_x[b], 16)
                    if not layer and t:
                        sp.dma_start(pos[:, b, :], io["pos"][(t - 1) * P:t * P, :]).then_inc(s_pos[b], 16)
                if not layer:
                    for b in range(2):
                        sp.wait_ge(s_st[b], 16 * (5 - b))

            @block.gpsimd
            def _(pool):
                if not layer:
                    for t in range(TILES):
                        pool.wait_ge(s_x[0], 16) if t == 0 else pool.wait_ge(s_add, t)
                        pool.dma_start(x_rows[t], xr[:, t % 2, :]).then_inc(s_st[t % 2], 16)

            @block.scalar
            def _(act):
                def tile_stats(t):
                    b = t % 2
                    if layer or t == 0:
                        act.wait_ge(s_x[b], 16 * (t // 2 + 1))
                    else:
                        act.wait_ge(s_add, t)
                    if t:
                        act.wait_ge(s_sq, t)
                    if t >= 2:
                        act.wait_ge(s_rc, t - 1)
                    act.activation(junk[:, :], xr[:, b, :], ACT.Square, accum_out=st[:, b, 0:1]).then_inc(s_sq, 1)
                    act.wait_ge(s_sq, t + 1)
                    act.activation(st[:, b, 1:2], st[:, b, 0:1], ACT.Sqrt, bias=keep["eps"][:, 0:1], scale=1.0 / D
                                   ).then_inc(s_rt, 1)

                def tile_evict(t):
                    act.wait_ge(s_tr, t + 1)
                    for k in range(0, 4):
                        gain, shift = args(t, k)
                        act.activation(hT[:, k, t * P:(t + 1) * P], pb[:, 2 * (t % 2) + k // 4, (k % 4) * P:(k % 4 + 1) * P],
                                       ACT.Identity, bias=shift, scale=gain).then_inc(s_ea, 1)

                for t in range(TILES):
                    tile_stats(t)
                    if t:
                        tile_evict(t - 1)
                tile_evict(TILES - 1)

            @block.tensor
            def _(pe):
                for t in range(TILES):
                    pe.wait_ge(s_xn, t + 1)
                    if t >= 2:
                        pe.wait_ge(s_ea, 4 * (t - 1))
                        pe.wait_ge(s_ed, 4 * (t - 1))
                    for k in range(KD):
                        ins = pe.transpose(pb[:, 2 * (t % 2) + k // 4, (k % 4) * P:(k % 4 + 1) * P],
                                           xn[:, t % 2, k * P:(k + 1) * P], keep["ident"][:, :])
                    ins.then_inc(s_tr, 1)

            @block.vector
            def _(dve):
                def tile_scale(t):
                    b = t % 2
                    if not layer and t:
                        dve.wait_ge(s_x[b], 16 * (t // 2 + 1))
                        dve.wait_ge(s_pos[b], 16 * ((t + 1) // 2))
                        dve.tensor_tensor(xr[:, b, :], xr[:, b, :], pos[:, b, :], ALU.add).then_inc(s_add, 1)
                    dve.wait_ge(s_rt, t + 1)
                    dve.reciprocal(st[:, b, 2:3], st[:, b, 1:2]).then_inc(s_rc, 1)
                    dve.wait_ge(s_rc, t + 1)
                    if t >= 2:
                        dve.wait_ge(s_tr, t - 1)
                    dve.tensor_scalar(xn[:, b, :], xr[:, b, :], st[:, b, 2:3], None, ALU.mult).then_inc(s_xn, 1)

                def tile_evict(t):
                    dve.wait_ge(s_tr, t + 1)
                    for k in range(4, KD):
                        gain, shift = args(t, k)
                        dve.tensor_scalar(hT[:, k, t * P:(t + 1) * P], pb[:, 2 * (t % 2) + k // 4, (k % 4) * P:(k % 4 + 1) * P],
                                          gain, shift, ALU.mult, ALU.add).then_inc(s_ed, 1)

                for t in range(TILES):
                    tile_scale(t)
                    if t:
                        tile_evict(t - 1)
                tile_evict(TILES - 1)


def phase_hyena_in(nc, io, keep):
    win = io["hy_in_w"][0].rearrange("(k p) (s j c) -> p k s j c", p=P, s=3, c=P)
    PARTS = (1, 2, 0)
    with ExitStack() as ctx:
        m = Mem(nc, ctx, "hyin_")
        w = m.sb("w", [P, 2, KD, 3, P])
        pad = m.sb("pad", [P, 2, GAPPED + 2])
        mid = m.sb("mid", [P, 2, GAPPED])
        out = m.sb("out", [P, 3, GAPPED])
        u = m.sb("u", [P, 2, GAPPED])
        u_rows = m.sb("u_rows", [P, 2, TILES, P])
        pb = m.psum()
        s_w = [m.sem(f"w_in{b}") for b in range(2)]
        s_mm = m.sem("projected")
        s_zero = m.sem("pads_zero")
        s_ev = m.sem("padded")
        s_mid = m.sem("mid_tap")
        s_cv = m.sem("convolved")
        s_dve = m.sem("dve")
        s_u = m.sem("u_ready")
        s_tr = m.sem("u_transposed")
        s_ur = m.sem("u_rows_ready")
        s_x0 = [m.sem(f"x0_stored{b}") for b in range(2)]
        s_us = [m.sem(f"u_stored{b}") for b in range(2)]
        prm, hT = keep["prm"], keep["hT"]
        x0_dram, u_dram = io["x0_dram"], io["u_dram"]

        def bank(b, n):
            return 3 * ((b + n) % 2)

        with nc.Block() as block:

            @block.sync
            def _(sp):
                for b in range(2):
                    for part in PARTS:
                        sp.dma_start(w[:, b, :, part, :], win[:, :, part, b, :]).then_inc(s_w[b], 16)
                with sp.Fori(1, 4) as i:
                    for b in range(2):
                        sp.wait_ge(s_mm, i * 6 - 3 * (1 - b))
                        for part in PARTS:
                            sp.dma_start(w[:, b, :, part, :], win[:, :, part, i * 2 + b, :]).then_inc(s_w[b], 16)

            @block.tensor
            def _(pe):
                def project(b, i):
                    pe.wait_ge(s_w[b], i * 48 + 48)
                    for n, part in enumerate(PARTS):
                        if b == 0 and n < 2:
                            pe.wait_ge(s_ev, i * 6)
                        else:
                            pe.wait_ge(s_ev, i * 6 + (3 * b + n - 1))
                        for piece, (at, width) in enumerate(((0, CTX_ROWS), (CTX_ROWS, HALF), (CTX_ROWS + HALF, HALF))):
                            for k in range(KD):
                                ins = pe.matmul(pb[:, bank(b, n) + piece, 0:width], w[:, b, k, part, :],
                                                hT[:, k, at:at + width], start=(k == 0), stop=(k == KD - 1))
                        ins.then_inc(s_mm, 1)

                def turn(b, i):
                    pe.wait_ge(s_u, i * 2 + (b + 1))
                    for go, tiles in enumerate(((0, 4), (4, 8), (8, 9))):
                        pe.wait_ge(s_ur, i * 6 + (3 * b + (0 if go < 2 else 1)))
                        for t in range(*tiles):
                            at = t * P + (2 if t else 0)
                            ins = pe.transpose(pb[:, 6 + go % 2, (t % 4) * P:(t % 4 + 1) * P], u[:, b, at:at + P],
                                               keep["ident"][:, :])
                        ins.then_inc(s_tr, 1)

                with pe.Fori(0, 4) as i:
                    project(0, i)
                    project(1, i)
                    turn(0, i)
                    turn(1, i)

            @block.scalar
            def _(act):
                def evict(b, n, i):
                    q = 3 * b + n
                    act.wait_ge(s_mm, i * 6 + (q + 1))
                    act.wait_ge(s_cv, i * 6 if q < 2 else i * 6 + (q - 1))
                    pd = q % 2
                    part = PARTS[n]
                    col = 72 + part * 8
                    bias = prm[:, 2, bass.ds(i * 2 + (col + b), 1)]
                    act.activation(pad[:, pd, 1:1 + CTX_ROWS], pb[:, bank(b, n), 0:CTX_ROWS], ACT.Identity, bias=bias)
                    act.activation(pad[:, pd, LAT_AT + 1:LAT_AT + 1 + LAT].rearrange("p (a c) -> p a c", c=HALF),
                                   pb[:, bank(b, n) + 1:bank(b, n) + 3, :], ACT.Identity, bias=bias).then_inc(s_ev, 1)
                    act.wait_ge(s_ev, i * 6 + (q + 1))
                    act.activation(mid[:, pd, :], pad[:, pd, 1:1 + GAPPED], ACT.Identity,
                                   bias=prm[:, 2, bass.ds(i * 2 + (96 + part * 8 + b), 1)],
                                   scale=prm[:, 2, bass.ds(i * 2 + (24 + part * 8 + b), 1)]).then_inc(s_mid, 1)

                def evict_u(b, i):
                    for go, tiles in enumerate(((0, 4), (4, 8), (8, 9))):
                        act.wait_ge(s_tr, i * 6 + (3 * b + go + 1))
                        if go == 0:
                            act.wait_ge(s_us[b], i * 16)
                        act.activation(u_rows[:, b, tiles[0]:tiles[1], :],
                                       pb[:, 6 + go % 2, 0:(tiles[1] - tiles[0]) * P].rearrange("p (a c) -> p a c", c=P),
                                       ACT.Copy).then_inc(s_ur, 1)

                act.wait_ge(s_zero, 6)
                with act.Fori(0, 4) as i:
                    for b in range(2):
                        for n in range(3):
                            evict(b, n, i)
                    evict_u(0, i)
                    evict_u(1, i)

            @block.vector
            def _(dve):
                for b in range(2):
                    for at in (0, CTX_ROWS + 1, GAPPED + 1):
                        w_ = 2 if at == CTX_ROWS + 1 else 1
                        dve.memset(pad[:, b, at:at + w_], 0.0).then_inc(s_zero, 1)
                with dve.Fori(0, 4) as i:
                    ch = Chain(dve, s_dve, i * 6)
                    for b in range(2):
                        for n, part in enumerate(PARTS):
                            q = 3 * b + n
                            pd = q % 2
                            dve.wait_ge(s_mid, i * 6 + (q + 1))
                            first = prm[:, 2, bass.ds(i * 2 + (part * 8 + b), 1)]
                            last = prm[:, 2, bass.ds(i * 2 + (48 + part * 8 + b), 1)]
                            ch.link(dve.scalar_tensor_tensor(mid[:, pd, :], pad[:, pd, 0:GAPPED], first, mid[:, pd, :],
                                                             ALU.mult, ALU.add))
                            if n == 2:
                                if b == 0:
                                    dve.wait_ge(s_x0[1], i * 16)
                                else:
                                    dve.wait_ge(s_x0[0], i * 16 + 16)
                            dve.scalar_tensor_tensor(out[:, n, :], pad[:, pd, 2:2 + GAPPED], last, mid[:, pd, :],
                                                     ALU.mult, ALU.add).then_inc(s_cv, 1)
                            if n == 1:
                                dve.wait_ge(s_cv, i * 6 + (q + 1))
                                dve.wait_ge(s_tr, i * 6)
                                dve.tensor_tensor(u[:, b, :], out[:, 0, :], out[:, 1, :], ALU.mult).then_inc(s_u, 1)

            @block.gpsimd
            def _(pool):
                with pool.Fori(0, 4) as i:
                    for b in range(2):
                        pool.wait_ge(s_cv, i * 6 + (3 * b + 3))
                        pool.dma_start(x0_dram[i * 2 + b], out[:, 2, :]).then_inc(s_x0[b], 16)
                    for b in range(2):
                        pool.wait_ge(s_ur, i * 6 + 3 * (b + 1))
                        pool.dma_start(u_dram[:, :, bass.ds((i * 2 + b) * P, P)], u_rows[:, b, :, :]).then_inc(s_us[b], 16)
                for b in range(2):
                    pool.wait_ge(s_x0[b], 64)
                    pool.wait_ge(s_us[b], 64)


TAPS = 2 * LAT + 2 * CTX_ROWS
TAP_TILES = TAPS // P
ROUND = 1.5 * 2.0 ** 23
TWO_PI_HI = 6.28125
TWO_PI_LO = float(2 * np.pi - 6.28125)
PI_IN = 3.1415925


def phase_filter(nc, io, keep):
    with ExitStack() as ctx:
        m = Mem(nc, ctx, "filt_")
        z = m.sb("z", [HY_EMB, TAPS])
        w1 = m.sb("w1", [HY_EMB, HY_HID])
        w2 = m.sb("w2", [HY_HID, HY_HID])
        col = m.sb("columns", [HY_HID, 5])
        arg = m.sb("arg", [HY_HID, TAPS])
        turns = m.sb("turns", [HY_HID, TAPS])
        h1 = m.sb("h1", [HY_HID, TAPS])
        pb = m.psum()
        s_in = m.sem("loaded")
        s_mm = m.sem("layer_done")
        s_dve = m.sem("dve")
        s_arg = m.sem("angle_ready")
        s_sin = m.sem("sine_ready")
        filt = keep["filt"]
        pieces = [(a, min(HALF, TAPS - a)) for a in range(0, TAPS, HALF)]

        with nc.Block() as block:

            @block.sync
            def _(sp):
                sp.dma_start(z[:, :], io["zfeat"]).then_inc(s_in, 16)
                sp.dma_start(w1[:, :], io["hy_f_w1"][0]).then_inc(s_in, 16)
                sp.dma_start(w2[:, :], io["hy_f_w2"][0]).then_inc(s_in, 16)
                for n, name in enumerate(("hy_f_b1", "hy_f_b2", "hy_f_freq")):
                    sp.dma_start(col[:, n:n + 1], io[name].rearrange("a h -> h a")).then_inc(s_in, 16)

            @block.tensor
            def _(pe):
                pe.wait_ge(s_in, 96)
                for layer, (w, src) in enumerate(((w1, z), (w2, h1))):
                    if layer:
                        pe.wait_ge(s_sin, 1)
                    for n, (at, width) in enumerate(pieces):
                        pe.matmul(pb[0:HY_HID, n, 0:width], w[:, :], src[:, at:at + width], start=True, stop=True
                                  ).then_inc(s_mm, 1)

            @block.scalar
            def _(act):
                for layer, dst in enumerate((h1, filt)):
                    act.wait_ge(s_arg, layer + 1)
                    act.activation(dst[0:HY_HID, :], arg[:, :], ACT.Sin).then_inc(s_sin, 1)

            @block.vector
            def _(dve):
                ch = Chain(dve, s_dve)
                dve.wait_ge(s_in, 96)
                for n in range(2):
                    ch.link(dve.tensor_tensor(col[:, 3 + n:4 + n], col[:, n:n + 1], col[:, 2:3], ALU.mult))
                for layer in range(2):
                    if layer:
                        dve.wait_ge(s_sin, 1)
                    for n, (at, width) in enumerate(pieces):
                        dve.wait_ge(s_mm, layer * len(pieces) + n + 1)
                        last = ch.step(dve.tensor_scalar(arg[:, at:at + width], pb[0:HY_HID, n, 0:width], col[:, 2:3],
                                                         col[:, 3 + layer:4 + layer], ALU.mult, ALU.add))
                    dve.wait_ge(s_dve, last)
                    ch.link(dve.tensor_scalar(turns[:, :], arg[:, :], 1 / (2 * np.pi), ROUND, ALU.mult, ALU.add))
                    ch.link(dve.tensor_scalar(turns[:, :], turns[:, :], ROUND, None, ALU.subtract))
                    ch.link(dve.scalar_tensor_tensor(arg[:, :], turns[:, :], -TWO_PI_HI, arg[:, :], ALU.mult, ALU.add))
                    ch.link(dve.scalar_tensor_tensor(arg[:, :], turns[:, :], -TWO_PI_LO, arg[:, :], ALU.mult, ALU.add))
                    dve.tensor_scalar(arg[:, :], arg[:, :], PI_IN, -PI_IN, ALU.min, ALU.max).then_inc(s_arg, 1)


SQ = float(np.sqrt(0.5))
RE, IM = 0, 1
BLOCKS = 9
CTX_BLOCK = 8
CT_HALF = HALF // P


def phase_long_conv(nc, io, keep):
    FW = 2 * 256 + 9 * 256
    with ExitStack() as ctx:
        m = Mem(nc, ctx, "conv_")
        fwd = m.sb("fwd", [P, 2, FW])
        inv04 = m.sb("inv04", [P, 2, 2, 256])
        inv = m.sb("inv", [P, 3, 4, HALF])
        negt = m.sb("negt", [P, TAP_TILES])
        delta = m.sb("delta", [P, HALF])
        w3 = m.sb("w3", [HY_HID, 2, HALF])
        fbias = m.sb("fbias", [1, HALF])
        win = m.sb("window", [P, 2, HALF])
        ut = m.sb("u", [P, TILES, HALF])
        taps = m.sb("taps", [P, 2 * BLOCKS, HALF])
        z = m.sb("z", [P, 8, 2, HALF])
        tmp = m.sb("tmp", [P, 4, HALF])
        kf = m.sb("kf", [P, BLOCKS, 2, HALF])
        zflat = z[:, :, :, :].rearrange("p a b c -> p (a b c)")
        vs = [zflat[:, b * 2048:(b + 1) * 2048] for b in range(2)]
        yt = zflat[:, 4096:6144].rearrange("p (a c) -> p a c", c=256)
        gt = zflat[:, 6144:6144 + TOK]
        uflat = ut[:, :, :].rearrange("p a c -> p (a c)")
        x0 = [uflat[:, HALF + b * GAPPED:HALF + (b + 1) * GAPPED] for b in range(2)]
        yf = taps[:, :, :].rearrange("p (b c) n -> p b c n", c=2)
        pb = m.psum()
        s_mat = m.sem("matrices_in")
        s_half = m.sem("half_in")
        s_win = m.sem("window_ready")
        s_kp = m.sem("taps_projected")
        s_tap = m.sem("tap_windowed")
        s_dve = m.sem("dve")
        s_zk = m.sem("filter_sums")
        s_kd = m.sem("filter_block")
        s_ke = m.sem("filter_kept")
        s_zu = m.sem("input_sums")
        s_ud = m.sem("input_block")
        s_pr = m.sem("product_ready")
        s_iv = m.sem("inverse_done")
        s_ve = m.sem("inverse_kept")
        s_x0 = [m.sem(f"x0_in{b}") for b in range(2)]
        s_g = m.sem("g_ready")
        s_gs = m.sem("g_stored")
        filt = keep["filt"]
        DVE_STEPS = 20 + 10 + BLOCKS * 5 + 4 + CT_HALF * 15

        def fcol(group, part, half=0):
            if group < 2:
                return group * 256 + part * 128
            return 512 + (group - 2) * 768 + part * 256 + half * 128

        with nc.Block() as block:

            @block.sync
            def _(sp):
                sp.dma_start(fwd[:, :, :], io["fwd"].rearrange("p (a b) -> p a b", a=2)).then_inc(s_mat, 16)
                sp.dma_start(inv04[:, :, :, :].rearrange("p a b c -> p (a b c)"), io["inv04"]).then_inc(s_mat, 16)
                sp.dma_start(inv[:, :, :, :].rearrange("p a b c -> p (a b c)"), io["inv"]).then_inc(s_mat, 16)
                sp.dma_start(negt[:, :], io["negt"]).then_inc(s_mat, 16)
                with sp.Fori(0, 2) as h:
                    sp.wait_ge(s_iv, h * CT_HALF)
                    at = bass.ds(h * HALF, HALF)
                    sp.dma_start(delta[:, :], io["deltas"][:, at].partition_broadcast(P)).then_inc(s_half, 16)
                    sp.dma_start(w3[:, 0, :], io["hy_f_w3"][0][:, at]).then_inc(s_half, 16)
                    sp.dma_start(w3[:, 1, :], io["hy_f_w3"][0][:, bass.ds(h * HALF + D, HALF)]).then_inc(s_half, 16)
                    sp.dma_start(fbias[:, :], io["hy_f_bias"][:, at]).then_inc(s_half, 16)
                    sp.dma_start(ut[:, :, :], io["u_dram"][:, :, at]).then_inc(s_half, 16)
                    sp.wait_ge(s_pr, h * BLOCKS + BLOCKS)
                    for ct in range(2):
                        sp.dma_start(x0[ct], io["x0_dram"][h * CT_HALF + ct]).then_inc(s_x0[ct], 16)
                    for ct in range(CT_HALF):
                        if ct >= 1 and ct + 1 < CT_HALF:
                            sp.wait_ge(s_g, h * CT_HALF + ct)
                            sp.dma_start(x0[(ct + 1) % 2], io["x0_dram"][h * CT_HALF + (ct + 1)]).then_inc(s_x0[(ct + 1) % 2], 16)
                        sp.wait_ge(s_g, h * CT_HALF + (ct + 1))
                        sp.dma_start(io["g_dram"][h * CT_HALF + ct], gt).then_inc(s_gs, 16)
                sp.wait_ge(s_gs, 16 * 2 * CT_HALF)

            @block.tensor
            def _(pe):
                pe.wait_ge(s_mat, 64)

                def transform(source, ctx_source, counter, emptied, h):
                    for blk in range(BLOCKS):
                        lo = 2 + 2 * (blk % 2)
                        if blk >= 2:
                            pe.wait_ge(emptied, h * BLOCKS + (blk - 1))
                        for part in (RE, IM):
                            if blk in (0, 1, CTX_BLOCK):
                                group = 0 if blk == CTX_BLOCK else blk
                                terms = [(fwd[:, c, fcol(group, part):fcol(group, part) + P],
                                          source(group, c) if blk != CTX_BLOCK else ctx_source(c)) for c in range(2)]
                                terms = [t for t in terms if t[1] is not None]
                            else:
                                group, half = 2 + (blk - 2) // 2, blk % 2
                                own, other = (0, 1) if part == RE else (1, 0)
                                terms = [(fwd[:, c, fcol(group, 0, half):fcol(group, 0, half) + P],
                                          source(2 * (group - 1) + own, c)) for c in range(2)]
                                terms += [(fwd[:, c, fcol(group, 1 + part, half):fcol(group, 1 + part, half) + P],
                                           source(2 * (group - 1) + other, c)) for c in range(2)]
                            for n, (a, b) in enumerate(terms):
                                ins = pe.matmul(pb[:, lo + part, :], a, b, start=(n == 0), stop=(n == len(terms) - 1))
                        ins.then_inc(counter, 1)

                with pe.Fori(0, 2) as h:
                    pe.wait_ge(s_half, h * 80 + 80)
                    pe.wait_ge(s_ve, h * CT_HALF)
                    for tt in range(TAP_TILES):
                        back = 1 if tt in range(8, 16) or tt == 17 else 0
                        if tt >= 2:
                            pe.wait_ge(s_tap, h * TAP_TILES + (tt - 1))
                        pe.matmul(pb[:, tt % 2, :], filt[0:HY_HID, tt * P:(tt + 1) * P], w3[:, back, :],
                                  start=True, stop=True).then_inc(s_kp, 1)
                    pe.wait_ge(s_zk, h + 1)
                    transform(lambda s, c: z[:, s, c, :], lambda c: taps[:, 16 + c, :], s_kd, s_ke, h)
                    pe.wait_ge(s_zu, h + 1)
                    pe.wait_ge(s_ke, h * BLOCKS + BLOCKS)
                    transform(lambda s, c: z[:, s, c, :], lambda c: ut[:, 0, :] if c == 0 else None, s_ud, s_pr, h)
                    pe.wait_ge(s_pr, h * BLOCKS + BLOCKS)
                    for ct in range(CT_HALF):
                        base = 3 * (ct % 2)
                        chan = slice(ct * P, (ct + 1) * P)
                        if ct >= 2:
                            pe.wait_ge(s_ve, h * CT_HALF + (ct - 1))
                        for g in range(3):
                            for c in range(4):
                                pe.matmul(pb[:, base + g, :], yf[:, 2 + 2 * g + c % 2, c // 2, chan], inv[:, g, c, :],
                                          start=(c == 0), stop=(c == 3))
                        if ct >= 1:
                            pe.wait_ge(s_ve, h * CT_HALF + ct)
                            pe.wait_ge(s_g, h * CT_HALF + ct)
                        for g in range(2):
                            for c in range(2):
                                pe.matmul(pb[:, 6, g * 256:(g + 1) * 256], yf[:, g, c, chan], inv04[:, g, c, :],
                                          start=(c == 0), stop=(c == 1))
                        for c in range(2):
                            ins = pe.matmul(pb[:, 7, 0:P], yf[:, CTX_BLOCK, c, chan], inv04[:, 0, c, 0:P],
                                            start=(c == 0), stop=(c == 1))
                        ins.then_inc(s_iv, 1)

            @block.scalar
            def _(act):
                act.wait_ge(s_mat, 64)
                with act.Fori(0, 2) as h:
                    act.wait_ge(s_half, h * 80 + 80)
                    for tt in range(TAP_TILES):
                        if tt >= 2:
                            act.wait_ge(s_tap, h * TAP_TILES + (tt - 1))
                        act.activation(win[:, tt % 2, :], delta[:, :], ACT.Exp, scale=negt[:, tt:tt + 1]).then_inc(s_win, 1)
                    for blk in range(BLOCKS):
                        act.wait_ge(s_kd, h * BLOCKS + (blk + 1))
                        act.activation(kf[:, blk, :, :], pb[:, 2 + 2 * (blk % 2):4 + 2 * (blk % 2), :], ACT.Copy
                                       ).then_inc(s_ke, 1)
                    for ct in range(CT_HALF):
                        act.wait_ge(s_iv, h * CT_HALF + (ct + 1))
                        if ct >= 2:
                            act.wait_ge(s_g, h * CT_HALF + (ct - 1))
                        v = vs[ct % 2]
                        act.activation(v[:, 0:3 * HALF].rearrange("p (a c) -> p a c", c=HALF),
                                       pb[:, 3 * (ct % 2):3 * (ct % 2) + 3, :], ACT.Copy)
                        act.activation(v[:, 3 * HALF:4 * HALF], pb[:, 6, :], ACT.Copy).then_inc(s_ve, 1)

            @block.vector
            def _(dve):
                tt_ = dve.tensor_tensor

                with dve.Fori(0, 2) as h:
                    ch = Chain(dve, s_dve, h * DVE_STEPS)
                    step, link = ch.step, ch.link

                    def done():
                        dve.wait_ge(s_dve, ch.base + ch.n)

                    dve.wait_ge(s_iv, h * CT_HALF)
                    for tt in range(TAP_TILES):
                        dve.wait_ge(s_win, h * TAP_TILES + (tt + 1))
                        dve.wait_ge(s_kp, h * TAP_TILES + (tt + 1))
                        tt_(taps[:, tt, :], pb[:, tt % 2, :], win[:, tt % 2, :], ALU.mult).then_inc(s_tap, 1)
                    dve.wait_ge(s_half, h * 80 + 80)
                    dve.wait_ge(s_tap, h * TAP_TILES + TAP_TILES)
                    for tt in (8, 17):
                        step(dve.memset(taps[0:1, tt, :], 0.0))
                    for tt in (0, 16):
                        step(tt_(taps[0:1, tt, :], taps[0:1, tt, :], fbias[:, :], ALU.add))
                    done()

                    def q(n):
                        return taps[:, 2 * n:2 * n + 2, :]

                    def zz(n):
                        return z[:, n, :, :]

                    dve.wait_ge(s_gs, h * 16 * CT_HALF)
                    for n in range(4):
                        step(tt_(zz(n), q(n), q(n + 4), ALU.subtract))
                    done()
                    for n in range(4):
                        step(tt_(q(n), q(n), q(n + 4), ALU.add))
                    done()
                    step(tt_(q(4), zz(1), zz(3), ALU.add))
                    step(tt_(q(5), zz(3), zz(1), ALU.subtract))
                    step(tt_(q(6), q(0), q(2), ALU.add))
                    step(tt_(q(7), q(1), q(3), ALU.add))
                    done()
                    dve.scalar_tensor_tensor(zz(4), q(5), -SQ, zz(0), ALU.mult, ALU.add)
                    dve.scalar_tensor_tensor(zz(5), q(4), -SQ, zz(2), ALU.mult, ALU.subtract)
                    dve.scalar_tensor_tensor(zz(6), q(5), SQ, zz(0), ALU.mult, ALU.add)
                    link(dve.scalar_tensor_tensor(zz(7), q(4), -SQ, zz(2), ALU.mult, ALU.add))
                    step(tt_(zz(0), q(6), q(7), ALU.add))
                    step(tt_(zz(1), q(6), q(7), ALU.subtract))
                    step(tt_(zz(2), q(0), q(2), ALU.subtract))
                    tt_(zz(3), q(3), q(1), ALU.subtract).then_inc(s_zk, 1)

                    dve.wait_ge(s_kd, h * BLOCKS + BLOCKS)
                    def x(n):
                        return ut[:, 1 + 2 * n:3 + 2 * n, :]
                    a, b = tmp[:, 0:2, :], tmp[:, 2:4, :]
                    step(tt_(a, x(0), x(2), ALU.add))
                    step(tt_(b, x(1), x(3), ALU.add))
                    step(tt_(zz(3), x(3), x(1), ALU.subtract))
                    step(tt_(zz(2), x(0), x(2), ALU.subtract))
                    done()
                    step(tt_(zz(0), a, b, ALU.add))
                    step(tt_(zz(1), a, b, ALU.subtract))
                    step(dve.scalar_tensor_tensor(zz(4), zz(3), -SQ, x(0), ALU.mult, ALU.add))
                    step(dve.scalar_tensor_tensor(zz(6), zz(3), SQ, x(0), ALU.mult, ALU.add))
                    step(dve.scalar_tensor_tensor(zz(5), b, -SQ, x(2), ALU.mult, ALU.subtract))
                    step(dve.scalar_tensor_tensor(zz(7), b, -SQ, x(2), ALU.mult, ALU.add))
                    done()
                    dve.memset(tmp[0:1, 0, 0:1], 0.0).then_inc(s_zu, 1)

                    for blk in range(BLOCKS):
                        lo = 2 + 2 * (blk % 2)
                        dve.wait_ge(s_ke, h * BLOCKS + (blk + 1))
                        dve.wait_ge(s_ud, h * BLOCKS + (blk + 1))
                        done()
                        dve.wait_ge(s_pr, h * BLOCKS + blk)
                        step(tt_(tmp[:, 0, :], pb[:, lo, :], kf[:, blk, RE, :], ALU.mult))
                        step(tt_(tmp[:, 2, :], pb[:, lo, :], kf[:, blk, IM, :], ALU.mult))
                        step(tt_(tmp[:, 3, :], pb[:, lo + 1, :], kf[:, blk, RE, :], ALU.mult))
                        step(tt_(tmp[:, 1, :], pb[:, lo + 1, :], kf[:, blk, IM, :], ALU.mult))
                        done()
                        step(tt_(yf[:, blk, RE, :], tmp[:, 0, :], tmp[:, 1, :], ALU.subtract))
                        if blk in (0, CTX_BLOCK):
                            step(tt_(yf[:, blk, IM, :], tmp[:, 2, :], tmp[:, 3, :], ALU.add))
                            done()
                            step(dve.tensor_copy(yf[0:1, blk, RE, :], tmp[0:1, 0, :]))
                            dve.tensor_copy(yf[0:1, blk, IM, :], tmp[0:1, 1, :]).then_inc(s_pr, 1)
                        else:
                            tt_(yf[:, blk, IM, :], tmp[:, 2, :], tmp[:, 3, :], ALU.add).then_inc(s_pr, 1)
                    done()
                    for ct in range(CT_HALF):
                        v = vs[ct % 2]
                        dve.wait_ge(s_ve, h * CT_HALF + (ct + 1))

                        def piece(n, k=1):
                            return v[:, n * 256:(n + k) * 256]

                        def t_(n, k=1):
                            return yt[:, n:n + k, :].rearrange("p a c -> p (a c)")
                        step(tt_(t_(0, 2), piece(2, 2), piece(4, 2), ALU.add))
                        step(tt_(t_(2, 2), piece(2, 2), piece(4, 2), ALU.subtract))
                        step(tt_(t_(4), piece(6), piece(7), ALU.add))
                        step(tt_(t_(5), piece(6), piece(7), ALU.subtract))
                        done()
                        step(tt_(t_(6), t_(4), piece(0), ALU.add))
                        step(tt_(t_(7), t_(4), piece(0), ALU.subtract))
                        done()
                        dve.wait_ge(s_gs, (h * CT_HALF + ct) * 16)
                        y = [gt[:, CTX_ROWS + n * 256:CTX_ROWS + (n + 1) * 256] for n in range(4)]
                        step(tt_(y[0], t_(6), t_(0), ALU.add))
                        step(tt_(y[2], t_(7), t_(3), ALU.subtract))
                        done()
                        step(tt_(t_(6), t_(2), t_(1), ALU.subtract))
                        step(tt_(t_(7), t_(2), t_(1), ALU.add))
                        step(tt_(t_(0), t_(5), piece(1), ALU.subtract))
                        step(tt_(t_(4), t_(5), piece(1), ALU.add))
                        done()
                        step(dve.scalar_tensor_tensor(y[1], t_(6), SQ, t_(0), ALU.mult, ALU.add))
                        step(dve.scalar_tensor_tensor(y[3], t_(7), -SQ, t_(4), ALU.mult, ALU.add))
                        done()
                        dve.wait_ge(s_x0[ct % 2], h * 32 + (ct // 2 + 1) * 16)
                        step(dve.scalar_tensor_tensor(gt[:, 0:CTX_ROWS], pb[:, 7, 0:P], float(NFFT // (2 * CTX_ROWS)),
                                                      x0[ct % 2][:, 0:CTX_ROWS], ALU.mult, ALU.mult))
                        tt_(gt[:, CTX_ROWS:TOK], gt[:, CTX_ROWS:TOK], x0[ct % 2][:, LAT_AT:LAT_AT + LAT], ALU.mult
                            ).then_inc(s_g, 1)
                    assert ch.n == DVE_STEPS, ch.n


def phase_hyena_out(nc, io, keep):
    x_rows = io["x_dram"].rearrange("(t p) d -> t p d", p=P)
    with ExitStack() as ctx:
        m = Mem(nc, ctx, "hyout_")
        g = m.sb("g", [P, KD, TOK])
        w = m.sb("w", [P, KD, D])
        gate = m.sb("gate", [P, 2, D])
        xr = m.sb("x", [P, 3, D])
        t1 = m.sb("t1", [P, 2, D])
        pb = m.psum()
        s_g = m.sem("g_in")
        s_w = m.sem("w_in")
        s_gate = m.sem("gate_in")
        s_x = [m.sem(f"x_in{b}") for b in range(3)]
        s_mm = m.sem("projected")
        s_t = m.sem("gated")
        s_sum = m.sem("summed")
        s_st = [m.sem(f"x_stored{b}") for b in range(3)]

        with nc.Block() as block:

            @block.sync
            def _(sp):
                sp.dma_start(g[:, :, :], io["g_dram"].rearrange("k p t -> p k t")).then_inc(s_g, 16)
                for c in range(2):
                    sp.dma_start(gate[:, c, :], io["vec_dram"][0, c, V_G1:V_G1 + 1, :].partition_broadcast(P)).then_inc(s_gate, 16)
                for t in range(TILES):
                    b = t % 3
                    if t >= 3:
                        sp.wait_ge(s_st[b], 16 * (t // 3))
                    sp.dma_start(xr[:, b, :], x_rows[t]).then_inc(s_x[b], 16)

            @block.scalar
            def _(act):
                act.dma_start(w[:, :, :], io["hy_out_w"][0].rearrange("(k p) n -> p k n", p=P)).then_inc(s_w, 16)
                for t in range(TILES):
                    act.wait_ge(s_sum, t + 1)
                    act.dma_start(x_rows[t], xr[:, t % 3, :]).then_inc(s_st[t % 3], 16)
                for b in range(3):
                    act.wait_ge(s_st[b], 48)

            @block.tensor
            def _(pe):
                pe.wait_ge(s_g, 16)
                pe.wait_ge(s_w, 16)
                for t in range(TILES):
                    if t >= 2:
                        pe.wait_ge(s_t, t - 1)
                    for half in range(2):
                        for k in range(KD):
                            ins = pe.matmul(pb[:, 2 * (t % 2) + half, :], g[:, k, t * P:(t + 1) * P],
                                            w[:, k, half * HALF:(half + 1) * HALF], start=(k == 0), stop=(k == KD - 1))
                    ins.then_inc(s_mm, 1)

            @block.vector
            def _(dve):
                dve.wait_ge(s_gate, 32)
                for t in range(TILES):
                    dve.wait_ge(s_mm, t + 1)
                    dve.tensor_tensor(t1[:, t % 2, :], pb[:, 2 * (t % 2):2 * (t % 2) + 2, :].rearrange("p a c -> p (a c)"),
                                      gate[:, CTX if t == 0 else LATENT, :], ALU.mult).then_inc(s_t, 1)
                    dve.wait_ge(s_x[t % 3], 16 * (t // 3 + 1))
                    dve.wait_ge(s_t, t + 1)
                    dve.tensor_tensor(xr[:, t % 3, :], xr[:, t % 3, :], t1[:, t % 2, :], ALU.add).then_inc(s_sum, 1)


PIECES = 6


def expert_piece(io, layer, j, expert):
    name, half = (("moe_w_gate", 0), ("moe_w_up", 0), ("moe_w_gate", 1), ("moe_w_up", 1),
                  ("moe_w_down", 0), ("moe_w_down", 1))[j]
    return io[name][layer].rearrange("e (k p) n -> p e k n", p=P)[:, expert, :, half * HALF:(half + 1) * HALF]


def phase_route(nc, io, keep, layer):
    x_rows = io["x_dram"].rearrange("(t p) d -> t p d", p=P)
    h_rows = io["h_dram"].rearrange("(t p) d -> t p d", p=P)
    with ExitStack() as ctx:
        m = Mem(nc, ctx, f"route{layer}_")
        xr = m.sb("x", [P, 2, D])
        hr = m.sb("h", [P, 2, D])
        junk = m.sb("junk", [P, D])
        ht = m.sb("ht", [P, 2, KD, P])
        vec = m.sb("vec", [P, 2, 2, D])
        wr = m.sb("router", [P, KD, EXPERTS])
        st = m.sb("stats", [P, 2, 8])
        ex = m.sb("ex", [P, 2, EXPERTS])
        aff = m.sb("aff", [P, 2, EXPERTS])
        cur = m.sb("cur", [EXPERTS, 2, TOK])
        vals = m.sb("vals", [EXPERTS, CAP_LAT + CAP_CTX])
        idx = m.sb("idx", [EXPERTS, CAP_LAT + CAP_CTX], U32)
        idxf = m.sb("idxf", [EXPERTS, CAP_LAT + CAP_CTX])
        pb = m.psum()
        s_vec = m.sem("vectors_in")
        s_x = [m.sem(f"x_in{b}") for b in range(2)]
        s_sq = m.sem("squared")
        s_rt = m.sem("root")
        s_dve = m.sem("dve")
        s_h = m.sem("h_ready")
        s_hs = [m.sem(f"h_stored{b}") for b in range(2)]
        s_tr = m.sem("h_transposed")
        s_ht = m.sem("ht_ready")
        s_lg = m.sem("logits")
        s_mx = m.sem("max_ready")
        s_ex = m.sem("exp_ready")
        s_af = m.sem("affinity")
        s_at = m.sem("affinity_transposed")
        s_ct = m.sem("affinity_kept")
        s_top = m.sem("slots_chosen")
        s_it = m.sem("slots_transposed")

        with nc.Block() as block:

            @block.sync
            def _(sp):
                sp.dma_start(wr[:, :, :], io["moe_router"][layer].rearrange("(k p) e -> p k e", p=P)).then_inc(s_vec, 16)
                for c in range(2):
                    for n, which in enumerate((V_A2, V_B2)):
                        sp.dma_start(vec[:, c, n, :], io["vec_dram"][layer, c, which:which + 1, :].partition_broadcast(P)
                                     ).then_inc(s_vec, 16)
                for t in range(TILES):
                    if t >= 2:
                        sp.wait_ge(s_h, t - 1)
                    sp.dma_start(xr[:, t % 2, :], x_rows[t]).then_inc(s_x[t % 2], 16)
                for j in range(PIECES):
                    sp.dma_start(keep["ring"][:, j, :, :], expert_piece(io, layer, j, 0)).then_inc(keep["s_ring"][j], 16)
                for b in range(2):
                    sp.wait_ge(s_hs[b], 16 * (5 - b))

            @block.gpsimd
            def _(pool):
                for t in range(TILES):
                    pool.wait_ge(s_h, t + 1)
                    pool.dma_start(h_rows[t], hr[:, t % 2, :]).then_inc(s_hs[t % 2], 16)

            @block.scalar
            def _(act):
                def stats(t):
                    b = t % 2
                    act.wait_ge(s_x[b], 16 * (t // 2 + 1))
                    if t:
                        act.wait_ge(s_sq, t)
                    if t >= 2:
                        act.wait_ge(s_h, t - 1)
                    act.activation(junk[:, :], xr[:, b, :], ACT.Square, accum_out=st[:, b, 0:1]).then_inc(s_sq, 1)
                    act.wait_ge(s_sq, t + 1)
                    act.activation(st[:, b, 1:2], st[:, b, 0:1], ACT.Sqrt, bias=keep["eps"][:, 0:1], scale=1.0 / D
                                   ).then_inc(s_rt, 1)

                def turned(t):
                    act.wait_ge(s_tr, t + 1)
                    if t >= 2:
                        act.wait_ge(s_lg, t - 1)
                    act.activation(ht[:, t % 2, :, :].rearrange("p (a k) c -> p a (k c)", a=2),
                                   pb[:, 2 * (t % 2):2 * (t % 2) + 2, :], ACT.Copy).then_inc(s_ht, 1)

                def exps(t):
                    b = t % 2
                    act.wait_ge(s_mx, t + 1)
                    act.activation(ex[:, b, :], pb[:, 4 + b, 0:EXPERTS], ACT.Exp, bias=st[:, b, 3:4],
                                   accum_out=st[:, b, 4:5]).then_inc(s_ex, 1)

                for t in range(TILES + 2):
                    if t < TILES:
                        stats(t)
                    if 1 <= t <= TILES:
                        turned(t - 1)
                    if t >= 2:
                        exps(t - 2)

            @block.tensor
            def _(pe):
                pe.wait_ge(s_vec, 80)

                def logits(t):
                    b = t % 2
                    pe.wait_ge(s_ht, t + 1)
                    if t >= 2:
                        pe.wait_ge(s_ex, t - 1)
                    for k in range(KD):
                        ins = pe.matmul(pb[:, 4 + b, 0:EXPERTS], ht[:, b, k, :], wr[:, k, :],
                                        start=(k == 0), stop=(k == KD - 1))
                    ins.then_inc(s_lg, 1)

                def affinities(t):
                    b = t % 2
                    pe.wait_ge(s_af, t + 1)
                    if t >= 2:
                        pe.wait_ge(s_ct, t - 1)
                    pe.transpose(pb[0:EXPERTS, 6 + b, 0:P], aff[:, b, :], keep["ident"][:, :]).then_inc(s_at, 1)

                for t in range(TILES + 2):
                    if t < TILES:
                        pe.wait_ge(s_h, t + 1)
                        if t >= 2:
                            pe.wait_ge(s_ht, t - 1)
                        for k in range(KD):
                            ins = pe.transpose(pb[:, 2 * (t % 2) + k // 4, (k % 4) * P:(k % 4 + 1) * P],
                                               hr[:, t % 2, k * P:(k + 1) * P], keep["ident"][:, :])
                        ins.then_inc(s_tr, 1)
                    if 1 <= t <= TILES:
                        logits(t - 1)
                    if t >= 2:
                        affinities(t - 2)
                pe.wait_ge(s_top, 1)
                pe.transpose(pb[:, 0, 0:EXPERTS], vals[:, 0:P], keep["ident"][0:EXPERTS, 0:EXPERTS])
                pe.transpose(pb[:, 0, 16:16 + EXPERTS], idxf[:, 0:P], keep["ident"][0:EXPERTS, 0:EXPERTS])
                pe.transpose(pb[0:CAP_CTX, 0, 32:32 + EXPERTS], vals[:, P:], keep["ident"][0:EXPERTS, 0:EXPERTS])
                pe.transpose(pb[0:CAP_CTX, 0, 48:48 + EXPERTS], idxf[:, P:], keep["ident"][0:EXPERTS, 0:EXPERTS]
                             ).then_inc(s_it, 1)

            @block.vector
            def _(dve):
                ch = Chain(dve, s_dve)
                dve.wait_ge(s_vec, 80)

                def rows(t):
                    b, c = t % 2, CTX if t == 0 else LATENT
                    dve.wait_ge(s_rt, t + 1)
                    ch.link(dve.reciprocal(st[:, b, 2:3], st[:, b, 1:2]))
                    if t >= 2:
                        dve.wait_ge(s_hs[b], 16 * (t // 2))
                        dve.wait_ge(s_tr, t - 1)
                    ch.link(dve.scalar_tensor_tensor(hr[:, b, :], xr[:, b, :], st[:, b, 2:3], vec[:, c, 0, :],
                                                     ALU.mult, ALU.mult))
                    dve.tensor_tensor(hr[:, b, :], hr[:, b, :], vec[:, c, 1, :], ALU.add).then_inc(s_h, 1)

                def top(t):
                    b = t % 2
                    dve.wait_ge(s_lg, t + 1)
                    dve.tensor_reduce(st[:, b, 3:4], pb[:, 4 + b, 0:EXPERTS], AX.X, ALU.max, negate=True).then_inc(s_mx, 1)

                def soft(t):
                    b = t % 2
                    dve.wait_ge(s_ex, t + 1)
                    ch.link(dve.reciprocal(st[:, b, 5:6], st[:, b, 4:5]))
                    if t >= 2:
                        dve.wait_ge(s_at, t - 1)
                    dve.tensor_scalar(aff[:, b, :], ex[:, b, :], st[:, b, 5:6], None, ALU.mult).then_inc(s_af, 1)

                def kept(t):
                    dve.wait_ge(s_at, t + 1)
                    dve.tensor_copy(cur[:, 0, t * P:(t + 1) * P], pb[0:EXPERTS, 6 + t % 2, 0:P]).then_inc(s_ct, 1)

                for t in range(TILES + 2):
                    if t < TILES:
                        rows(t)
                    if 1 <= t <= TILES:
                        top(t - 1)
                    if t >= 2:
                        soft(t - 2)
                        kept(t - 2)
                dve.wait_ge(s_ct, TILES)
                for at, width, first, cap in ((CTX_ROWS, LAT, 0, CAP_LAT), (0, CTX_ROWS, CAP_LAT, CAP_CTX)):
                    for r in range(cap // 8):
                        now, then = cur[:, r % 2, at:at + width], cur[:, 1 - r % 2, at:at + width]
                        eight = slice(first + 8 * r, first + 8 * r + 8)
                        ch.link(dve.max(vals[:, eight], now))
                        ch.step(dve.max_index(idx[:, eight], vals[:, eight], now))
                        ch.link(dve.match_replace(then, vals[:, eight], now, -1.0))
                dve.tensor_copy(idxf[:, :], idx[:, :]).then_inc(s_top, 1)
                dve.memset(keep["idx_lat"][:, EXPERTS:], 0)
                dve.memset(keep["idx_ctx"][:, EXPERTS:], 0)
                dve.wait_ge(s_it, 1)
                dve.tensor_copy(keep["gate_lat"][:, :], pb[:, 0, 0:EXPERTS])
                dve.tensor_scalar(keep["idx_lat"][:, 0:EXPERTS], pb[:, 0, 16:16 + EXPERTS], float(CTX_ROWS), None, ALU.add)
                dve.tensor_copy(keep["gate_ctx"][:, :], pb[0:CAP_CTX, 0, 32:32 + EXPERTS])
                dve.tensor_copy(keep["idx_ctx"][:, 0:EXPERTS], pb[0:CAP_CTX, 0, 48:48 + EXPERTS])


def phase_experts(nc, io, keep, layer):
    with ExitStack() as ctx:
        m = Mem(nc, ctx, f"moe{layer}_")
        xe = m.sb("xe", [P, D])
        xc = m.sb("xc", [CAP_CTX, D])
        xt = m.sb("xt", [P, KD, SLOTS])
        sg = m.sb("sg", [P, 2, SLOTS])
        hid = m.sb("hid", [P, KD, SLOTS])
        yt = m.sb("yt", [P, KD, SLOTS])
        yr = m.sb("yr", [P, D])
        yc = m.sb("yc", [CAP_CTX, D])
        g2 = m.sb("g2", [P, 2, D])
        pb = m.psum()
        ring = keep["ring"]
        s_ring = keep["s_ring"]
        s_g2 = m.sem("gates_in")
        s_xe = m.sem("rows_gathered")
        s_tx = m.sem("rows_transposed")
        s_xt = m.sem("xt_ready")
        s_gu = m.sem("gate_up_done")
        s_sg = m.sem("silu_ready")
        s_hid = m.sem("hidden_ready")
        s_dn = m.sem("down_done")
        s_yt = m.sem("yt_ready")
        s_ty = m.sem("y_transposed")
        s_yr = m.sem("y_rows_ready")
        s_sc = m.sem("scattered")
        ident = keep["ident"]

        with nc.Block() as block:

            @block.sync
            def _(sp):
                for c in range(2):
                    sp.dma_start(g2[:, c, :], io["vec_dram"][layer, c, V_G2:V_G2 + 1, :].partition_broadcast(P)
                                 ).then_inc(s_g2, 16)
                with sp.Fori(1, EXPERTS) as e:
                    for j in range(PIECES):
                        if j < 4:
                            sp.wait_ge(s_gu, e * 8 - (4 if j < 2 else 0))
                        else:
                            sp.wait_ge(s_dn, e * 8 - (4 if j == 4 else 0))
                        sp.dma_start(ring[:, j, :, :], expert_piece(io, layer, j, e)).then_inc(s_ring[j], 16)

            @block.gpsimd
            def _(pool):
                def at(table, e):
                    return bass.IndirectOffsetOnAxis(ap=keep[table][:, e:e + 1], axis=0)

                def gather(e):
                    pool.indirect_dma_start(xe[:, :], None, io["h_dram"], at("idx_lat", e)).then_inc(s_xe, 16)
                    pool.indirect_dma_start(xc[:, :], None, io["h_dram"], at("idx_ctx", e)).then_inc(s_xe, 16)

                gather(0)
                for e in range(EXPERTS):
                    pool.wait_ge(s_tx, e + 1)
                    gather(e + 1)
                    if e:
                        pool.wait_ge(s_sc, e * 32)
                    pool.wait_ge(s_yr, e * 2 + 2)
                    pool.indirect_dma_start(io["x_dram"], at("idx_lat", e), yr[:, :], None, compute_op=ALU.add
                                            ).then_inc(s_sc, 16)
                    pool.indirect_dma_start(io["x_dram"], at("idx_ctx", e), yc[:, :], None, compute_op=ALU.add
                                            ).then_inc(s_sc, 16)
                pool.wait_ge(s_sc, EXPERTS * 32)
                pool.wait_ge(s_xe, (EXPERTS + 1) * 32)

            @block.tensor
            def _(pe):
                def turn_rows():
                    for k in range(KD):
                        pe.transpose(pb[:, 4 + k // 4, (k % 4) * P:(k % 4 + 1) * P], xe[:, k * P:(k + 1) * P], ident[:, :])
                    for k in range(KD):
                        ins = pe.transpose(pb[:, 6, k * CAP_CTX:(k + 1) * CAP_CTX], xc[:, k * P:(k + 1) * P],
                                           ident[0:CAP_CTX, 0:CAP_CTX])
                    ins.then_inc(s_tx, 1)

                pe.wait_ge(s_xe, 32)
                turn_rows()
                with pe.Fori(0, EXPERTS) as e:
                    pe.wait_ge(s_xt, e * 3 + 3)
                    for f in range(KD):
                        half, col = f // 4, (f % 4) * P
                        if f % 4 == 0:
                            pe.wait_ge(s_ring[2 * half], e * 16 + 16)
                            pe.wait_ge(s_ring[2 * half + 1], e * 16 + 16)
                        if f == 0:
                            pe.wait_ge(s_yt, e * 8)
                        if f >= 2:
                            pe.wait_ge(s_hid, e * 8 + (f - 1))
                        for j in range(2):
                            for k in range(KD):
                                ins = pe.matmul(pb[:, 2 * (f % 2) + j, 0:SLOTS], ring[:, 2 * half + j, k, col:col + P],
                                                xt[:, k, :], start=(k == 0), stop=(k == KD - 1))
                        ins.then_inc(s_gu, 1)
                    pe.wait_ge(s_xe, e * 32 + 64)
                    pe.wait_ge(s_yr, e * 2)
                    turn_rows()
                    pe.wait_ge(s_hid, e * 8 + 8)
                    for d in range(KD):
                        half, col = d // 4, (d % 4) * P
                        if d % 4 == 0:
                            pe.wait_ge(s_ring[4 + half], e * 16 + 16)
                        if d >= 4:
                            pe.wait_ge(s_yt, e * 8 + (d - 3))
                        for k in range(KD):
                            ins = pe.matmul(pb[:, d % 4, 0:SLOTS], ring[:, 4 + half, k, col:col + P], hid[:, k, :],
                                            start=(k == 0), stop=(k == KD - 1))
                        ins.then_inc(s_dn, 1)
                    pe.wait_ge(s_xt, e * 3 + 6)
                    pe.wait_ge(s_yt, e * 8 + 8)
                    for d in range(KD):
                        ins = pe.transpose(pb[:, 4 + d // 4, (d % 4) * P:(d % 4 + 1) * P], yt[:, d, 0:CAP_LAT], ident[:, :])
                    ins.then_inc(s_ty, 1)
                    for d in range(KD):
                        ins = pe.transpose(pb[0:CAP_CTX, 6 + d // 4, (d % 4) * P:(d % 4 + 1) * P], yt[:, d, CAP_LAT:SLOTS],
                                           ident[:, :])
                    ins.then_inc(s_ty, 1)

            @block.scalar
            def _(act):
                def keep_rows(e1):
                    act.wait_ge(s_tx, e1)
                    act.activation(xt[:, 0:4, 0:CAP_LAT], pb[:, 4, :].rearrange("p (a c) -> p a c", c=P), ACT.Copy
                                   ).then_inc(s_xt, 1)
                    act.activation(xt[:, 4:8, 0:CAP_LAT], pb[:, 5, :].rearrange("p (a c) -> p a c", c=P), ACT.Copy
                                   ).then_inc(s_xt, 1)
                    act.activation(xt[:, :, CAP_LAT:SLOTS], pb[:, 6, 0:P].rearrange("p (a c) -> p a c", c=CAP_CTX), ACT.Copy
                                   ).then_inc(s_xt, 1)

                keep_rows(1)
                with act.Fori(0, EXPERTS) as e:
                    for f in range(KD):
                        act.wait_ge(s_gu, e * 8 + (f + 1))
                        if f < 2:
                            act.wait_ge(s_hid, e * 8)
                        else:
                            act.wait_ge(s_hid, e * 8 + (f - 1))
                        act.activation(sg[:, f % 2, :], pb[:, 2 * (f % 2), 0:SLOTS], ACT.Silu).then_inc(s_sg, 1)
                    keep_rows(e + 2)
                    act.wait_ge(s_ty, e * 2)
                    for d in range(KD):
                        act.wait_ge(s_dn, e * 8 + (d + 1))
                        act.activation(yt[:, d, :], pb[:, d % 4, 0:SLOTS], ACT.Copy).then_inc(s_yt, 1)

            @block.vector
            def _(dve):
                dve.wait_ge(s_g2, 32)
                with dve.Fori(0, EXPERTS) as e:
                    dve.wait_ge(s_dn, e * 8)
                    for f in range(KD):
                        dve.wait_ge(s_sg, e * 8 + (f + 1))
                        dve.tensor_tensor(hid[:, f, :], pb[:, 2 * (f % 2) + 1, 0:SLOTS], sg[:, f % 2, :], ALU.mult
                                          ).then_inc(s_hid, 1)
                    dve.wait_ge(s_ty, e * 2 + 1)
                    dve.wait_ge(s_sc, e * 32)
                    dve.scalar_tensor_tensor(yr[:, :], pb[:, 4:6, :].rearrange("p a c -> p (a c)"),
                                             keep["gate_lat"][:, bass.ds(e, 1)], g2[:, LATENT, :], ALU.mult, ALU.mult
                                             ).then_inc(s_yr, 1)
                    dve.wait_ge(s_ty, e * 2 + 2)
                    dve.scalar_tensor_tensor(yc[:, :], pb[0:CAP_CTX, 6:8, :].rearrange("p a c -> p (a c)"),
                                             keep["gate_ctx"][:, bass.ds(e, 1)], g2[0:CAP_CTX, CTX, :], ALU.mult, ALU.mult
                                             ).then_inc(s_yr, 1)


def mixture(nc, io, keep, layer):
    with ExitStack() as ctx:
        m = Mem(nc, ctx, f"mix{layer}_")
        keep["ring"] = m.sb("ring", [P, PIECES, KD, HALF])
        keep["s_ring"] = [m.sem(f"weights_in{j}") for j in range(PIECES)]
        keep["idx_lat"] = m.sb("idx_lat", [P, EXPERTS + 1], U32)
        keep["idx_ctx"] = m.sb("idx_ctx", [CAP_CTX, EXPERTS + 1], U32)
        keep["gate_lat"] = m.sb("gate_lat", [P, EXPERTS])
        keep["gate_ctx"] = m.sb("gate_ctx", [CAP_CTX, EXPERTS])
        phase_route(nc, io, keep, layer)
        phase_experts(nc, io, keep, layer)


R_DT, R_DA, R_IN, R_W, R_TOT = range(5)
TRI_LE, TRI_GT, TRI_GE, TRI_LT = 1, 2, 3, 4
BANKS3 = ((0, CTX_ROWS), (CTX_ROWS, HALF), (CTX_ROWS + HALF, HALF))
LAST_TILE = TILES - 1


def phase_ssd_in(nc, io, keep):
    win = io["ssd_in_w"][0].rearrange("(k p) n -> p k n", p=P)
    PER = 4
    DT_AT = INNER + XBC_TILES * P
    with ExitStack() as ctx:
        m = Mem(nc, ctx, "ssdin_")
        w = m.sb("w", [P, 2, KD, PER * P])
        wdt = m.sb("wdt", [P, KD, 2 * HEADS])
        hcol = m.sb("head_columns", [2 * HEADS, 3])
        sp_ = m.sb("softplus", [2 * HEADS, 6, TOK])
        pad = m.sb("pad", [P, 2, GAPPED + 4])
        mid = m.sb("mid", [P, 2, GAPPED])
        out = m.sb("out", [P, 2, GAPPED])
        eend = m.sb("decay_end", [P, TILES, 2 * HEADS])
        ones = m.sb("ones", [P, P])
        pb = m.psum()
        s_w = [m.sem(f"w_in{b}") for b in range(2)]
        s_wdt = m.sem("dt_weights_in")
        s_mm = m.sem("projected")
        s_dt = m.sem("dt_projected")
        s_dv = m.sem("dt_kept")
        s_act = m.sem("act")
        s_dve = m.sem("dve")
        s_zero = m.sem("pads_zero")
        s_ev = m.sem("padded")
        s_mid = m.sem("mid_tap")
        s_cv = m.sem("convolved")
        s_cnt = m.sem("taps_added")
        s_si = m.sem("silu_ready")
        s_st = [m.sem(f"stored{b}") for b in range(2)]
        s_rows = m.sem("rates_rows")
        s_kept = m.sem("rates_kept")
        s_cum = m.sem("cumulated")
        s_ex = m.sem("decays_ready")
        prm, hT, rates, tri = keep["prm"], keep["hT"], keep["rates"], keep["tri"]

        def bank(q):
            return 3 * (q % 2)

        with nc.Block() as block:

            @block.sync
            def _(sp):
                sp.dma_start(wdt[:, :, :], win[:, :, DT_AT:]).then_inc(s_wdt, 16)
                sp.dma_start(hcol[:, 0:1], io["ssd_dt_bias"][0].rearrange("a (h b) -> (a h) b", b=1)).then_inc(s_wdt, 16)
                sp.dma_start(hcol[:, 1:2], io["ssd_A_log"][0].rearrange("a (h b) -> (a h) b", b=1)).then_inc(s_wdt, 16)
                for b in range(2):
                    sp.dma_start(w[:, b, :, :], win[:, :, b * HALF:(b + 1) * HALF]).then_inc(s_w[b], 16)
                with sp.Fori(1, 5) as i:
                    for b in range(2):
                        sp.wait_ge(s_mm, i * 2 * PER - (PER if b == 0 else 0))
                        sp.dma_start(w[:, b, :, :], win[:, :, bass.ds((i * 2 + b) * HALF, HALF)]).then_inc(s_w[b], 16)

            @block.tensor
            def _(pe):
                def project(b, n, i, q0):
                    q = PER * b + n
                    if n == 0:
                        pe.wait_ge(s_w[b], i * 16 + 16)
                    pe.wait_ge(s_ev, i * 2 * PER + (q - 1 if q >= 1 else 0))
                    for piece, (at, width) in enumerate(BANKS3):
                        for k in range(KD):
                            ins = pe.matmul(pb[:, bank(q) + piece, 0:width], w[:, b, k, n * P:(n + 1) * P],
                                            hT[:, k, at:at + width], start=(k == 0), stop=(k == KD - 1))
                    ins.then_inc(s_mm, 1)

                pe.wait_ge(s_wdt, 48)
                for piece, (at, width) in enumerate(BANKS3):
                    for k in range(KD):
                        ins = pe.matmul(pb[0:2 * HEADS, 3 + piece, 0:width], wdt[:, k, :], hT[:, k, at:at + width],
                                        start=(k == 0), stop=(k == KD - 1))
                ins.then_inc(s_dt, 1)
                pe.wait_ge(s_dv, 1)
                with pe.Fori(0, 2) as i:
                    for b in range(2):
                        for n in range(PER):
                            project(b, n, i, 0)
                pe.wait_ge(s_rows, 1)
                for which in range(2):
                    for t in range(TILES - 1):
                        ins = pe.transpose(pb[:, 6 + which, t * 64:(t + 1) * 64], sp_[:, which, t * P:(t + 1) * P],
                                           keep["ident"][0:64, 0:64])
                ins.then_inc(s_cum, 1)
                pe.wait_ge(s_kept, 2)
                for which in range(2):
                    ins = pe.transpose(pb[:, 6, which * 64:(which + 1) * 64], sp_[:, which, LAST_TILE * P:TOK],
                                       keep["ident"][0:64, 0:64])
                ins.then_inc(s_cum, 1)
                pe.wait_ge(s_kept, 4)
                for n, (left, back) in enumerate(((TRI_LE, 0), (TRI_GE, 1), (TRI_GT, 0), (TRI_LT, 1), (None, 0), (None, 1))):
                    if n >= 2:
                        pe.wait_ge(s_ex, n - 1)
                    pe.matmul(pb[:, 6 + n % 2, 0:TILES * HEADS], ones[:, :] if left is None else tri[:, left, :],
                              rates[:, :, R_DA, back * HEADS:(back + 1) * HEADS], start=True, stop=True).then_inc(s_cum, 1)
                with pe.Fori(2, 5) as i:
                    for b in range(2):
                        for n in range(PER):
                            project(b, n, i, 0)

            @block.scalar
            def _(act):
                ch = Chain(act, s_act)
                S = lambda n: sp_[:, n, :]
                act.wait_ge(s_wdt, 48)
                ch.step(act.activation(hcol[:, 2:3], hcol[:, 1:2], ACT.Exp))
                act.wait_ge(s_dt, 1)
                act.activation(sp_[:, 0, 0:CTX_ROWS], pb[0:64, 3, 0:CTX_ROWS], ACT.Identity, bias=hcol[:, 0:1])
                act.activation(sp_[:, 0, CTX_ROWS:TOK].rearrange("p (a c) -> p a c", c=HALF), pb[0:64, 4:6, :],
                               ACT.Identity, bias=hcol[:, 0:1]).then_inc(s_dv, 1)
                act.wait_ge(s_dv, 1)
                ch.link(act.activation(S(1), S(0), ACT.Abs))
                ch.link(act.activation(S(2), S(1), ACT.Exp, scale=-1.0))
                act.wait_ge(s_dve, 1)
                ch.step(act.activation(S(3), S(4), ACT.Ln))

                def store_free(b, n, i, before):
                    return None

                act.wait_ge(s_zero, 6)

                def z_tile(b, n, i):
                    q = PER * b + n
                    act.wait_ge(s_mm, i * 8 + (q + 1))
                    act.wait_ge(s_st[q % 2], i * 64 + 16 * (q // 2))
                    act.activation(out[:, q % 2, 0:CTX_ROWS], pb[:, bank(q), 0:CTX_ROWS], ACT.Silu)
                    act.activation(out[:, q % 2, CTX_ROWS:TOK].rearrange("p (a c) -> p a c", c=HALF),
                                   pb[:, bank(q) + 1:bank(q) + 3, :], ACT.Silu).then_inc(s_ev, 1)

                def xbc_tile(b, n, i):
                    q = PER * b + n
                    act.wait_ge(s_mm, i * 8 + (q + 1))
                    if q < 2:
                        act.wait_ge(s_cv, i * 8 - 16)
                    else:
                        act.wait_ge(s_cv, i * 8 - 16 + (q - 1))
                    act.activation(pad[:, q % 2, 2:2 + CTX_ROWS], pb[:, bank(q), 0:CTX_ROWS], ACT.Copy)
                    act.activation(pad[:, q % 2, LAT_AT + 2:LAT_AT + 2 + LAT].rearrange("p (a c) -> p a c", c=HALF),
                                   pb[:, bank(q) + 1:bank(q) + 3, :], ACT.Copy).then_inc(s_ev, 1)
                    act.wait_ge(s_ev, i * 8 + (q + 1))
                    if q < 2:
                        act.wait_ge(s_si, i * 8 - 16)
                    else:
                        act.wait_ge(s_si, i * 8 - 16 + (q - 1))
                    act.activation(mid[:, q % 2, :], pad[:, q % 2, 2:2 + GAPPED], ACT.Identity,
                                   bias=prm[:, 1, bass.ds(i * 8 + (q - 16), 1)],
                                   scale=prm[:, 0, bass.ds(i * 8 + (2 * XBC_TILES - 16 + q), 1)]).then_inc(s_mid, 1)

                def silu(b, n, i, first):
                    q = PER * b + n
                    act.wait_ge(s_cv, i * 8 + (q - 15))
                    act.wait_ge(s_st[q % 2], i * 128 + (32 * (q // 2) - 256 + 128))
                    act.activation(out[:, q % 2, :], mid[:, q % 2, :], ACT.Silu).then_inc(s_si, 1)

                with act.Fori(0, 2) as i:
                    for b in range(2):
                        for n in range(PER):
                            z_tile(b, n, i)
                for n, (slot, back) in enumerate(((R_IN, 0), (R_IN, 1), (None, 0), (None, 1), (R_TOT, 0), (R_TOT, 1))):
                    act.wait_ge(s_cum, n + 3)
                    cols = slice(back * HEADS, (back + 1) * HEADS)
                    dst = eend[:, :, cols] if slot is None else rates[:, :, slot, cols]
                    act.activation(dst, pb[:, 6 + n % 2, 0:TILES * HEADS].rearrange("p (a c) -> p a c", c=HEADS), ACT.Exp
                                   ).then_inc(s_ex, 1)
                with act.Fori(2, 5) as i:
                    for b in range(2):
                        for n in range(PER):
                            xbc_tile(b, n, i)
                            silu(b, n, i, 0)

            @block.vector
            def _(dve):
                ch = Chain(dve, s_dve)
                S = lambda n: sp_[:, n, :]
                dve.wait_ge(s_act, 3)
                ch.link(dve.tensor_scalar(S(4), S(2), 1.0, None, ALU.add))
                ch.link(dve.tensor_scalar(S(1), S(4), -1.0, 1e-30, ALU.add, ALU.max))
                ch.link(dve.reciprocal(S(5), S(1)))
                dve.wait_ge(s_act, 4)
                ch.link(dve.tensor_tensor(S(5), S(5), S(3), ALU.mult))
                ch.link(dve.tensor_tensor(S(5), S(5), S(2), ALU.mult))
                ch.link(dve.scalar_tensor_tensor(S(4), S(4), 1.0, S(2), ALU.is_equal, ALU.mult))
                ch.link(dve.tensor_tensor(S(5), S(5), S(4), ALU.add))
                ch.link(dve.scalar_tensor_tensor(S(0), S(0), 0.0, S(5), ALU.max, ALU.add))
                ch.link(dve.tensor_scalar(S(1), S(0), hcol[:, 2:3], -1.0, ALU.mult, ALU.mult))
                dve.memset(ones[:, :], 1.0).then_inc(s_rows, 1)
                for b in range(2):
                    for at, width in ((0, 2), (CTX_ROWS + 2, 2), (GAPPED + 2, 2)):
                        dve.memset(pad[:, b, at:at + width], 0.0).then_inc(s_zero, 1)
                dve.wait_ge(s_cum, 1)
                for which in range(2):
                    dve.tensor_copy(rates[:, 0:LAST_TILE, which, :],
                                    pb[:, 6 + which, :].rearrange("p (a c) -> p a c", c=64)).then_inc(s_kept, 1)
                dve.wait_ge(s_cum, 2)
                for which in range(2):
                    dve.tensor_copy(rates[:, LAST_TILE, which, :], pb[:, 6, which * 64:(which + 1) * 64]).then_inc(s_kept, 1)
                dve.wait_ge(s_ex, 4)
                dve.wait_ge(s_kept, 4)
                dve.tensor_tensor(rates[:, :, R_W, :], rates[:, :, R_DT, :], eend[:, :, :], ALU.mult)
                with dve.Fori(0, 3) as i:
                    for q in range(2 * PER):
                        dve.wait_ge(s_mid, i * 8 + (q + 1))
                        for n, tap in enumerate((0, 1, 3, 4)):
                            ins = dve.scalar_tensor_tensor(mid[:, q % 2, :], pad[:, q % 2, tap:tap + GAPPED],
                                                           prm[:, 0, bass.ds(i * 8 + (tap * XBC_TILES + q), 1)],
                                                           mid[:, q % 2, :], ALU.mult, ALU.add)
                            if n < 3:
                                ins.then_inc(s_cnt, 1)
                                dve.wait_ge(s_cnt, i * 24 + (3 * q + n + 1))
                            else:
                                ins.then_inc(s_cv, 1)

            @block.gpsimd
            def _(pool):
                with pool.Fori(0, 2) as i:
                    for q in range(8):
                        pool.wait_ge(s_ev, i * 8 + (q + 1))
                        pool.dma_start(io["z_dram"][:, :, i * 8 + q, :].rearrange("t p c -> p t c"),
                                       out[:, q % 2, 0:TOK].rearrange("p (t c) -> p t c", c=P)).then_inc(s_st[q % 2], 16)
                with pool.Fori(0, 3) as i:
                    for q in range(8):
                        pool.wait_ge(s_si, i * 8 + (q + 1))
                        pool.dma_start(io["xbc_dram"][0, :, i * 8 + q, :], out[:, q % 2, 0:P]).then_inc(s_st[q % 2], 16)
                        pool.dma_start(io["xbc_dram"][1:, :, i * 8 + q, :].rearrange("t p c -> p t c"),
                                       out[:, q % 2, LAT_AT:].rearrange("p (t c) -> p t c", c=P)).then_inc(s_st[q % 2], 16)
                for b in range(2):
                    pool.wait_ge(s_st[b], 8 * 16 + 12 * 32)


GW = INNER // GROUPS
GH = HEADS // GROUPS


def per_head(ap):
    return ap.unsqueeze(2).broadcast_to([P, ap.shape[-1], HEAD])


def by_head(ap):
    return ap.rearrange("p (h c) -> p h c", c=HEAD)


def phase_states(nc, io, keep):
    XB = 20 * P
    with ExitStack() as ctx:
        m = Mem(nc, ctx, "st_")
        xb = m.sb("xb", [P, 2, XB])
        init = m.sb("init", [P, 2, 16, P])
        rc = m.sb("rates", [P, 2, 5, 64])
        xrow = m.sb("xrow", [P, 2, INNER])
        brow = m.sb("brow", [P, 2, GROUPS * P])
        xw = m.sb("xw", [P, 2, INNER])
        decayed = m.sb("decayed", [P, INNER])
        sb_ = m.sb("state_back", [P, 2, INNER])
        out = m.sb("ctx_state", [P, 2, 16, P])
        pb = m.psum()
        s_xb = [m.sem(f"chunk_in{b}") for b in range(2)]
        s_init = m.sem("init_in")
        s_rc = m.sem("rates_ready")
        s_tr = m.sem("transposed")
        s_row = m.sem("rows_ready")
        s_xw = m.sem("weighted")
        s_con = m.sem("contributions")
        s_cx = m.sem("ctx_kept")
        s_it = m.sem("init_transposed")
        s_ik = m.sem("init_kept")
        s_dec = m.sem("decayed")
        s_new = m.sem("state_ready")
        s_st = [m.sem(f"state_stored{b}") for b in range(2)]
        s_out = m.sem("ctx_stored")
        state, rates, ident = keep["state"], keep["rates"], keep["ident"]

        with nc.Block() as block:

            @block.sync
            def _(sp):
                sp.dma_start(xb[:, 0, :], io["xbc_dram"][0, :, 0:20, :].rearrange("p a c -> p (a c)")).then_inc(s_xb[0], 16)
                for d in range(2):
                    for h in range(2):
                        sp.dma_start(init[h * HEAD:(h + 1) * HEAD, d, :, :],
                                     io["state_ssd"][0, 0, d].rearrange("(a b) p n -> b p a n", b=2)[h]).then_inc(s_init, 16)
                sp.dma_start(xb[:, 1, :], io["xbc_dram"][8, :, 0:20, :].rearrange("p a c -> p (a c)")).then_inc(s_xb[1], 16)
                with sp.Fori(0, 4) as i:
                    for b in range(2):
                        sp.wait_ge(s_tr, i * 2 + (b + 1))
                        sp.dma_start(xb[:, b, :], io["xbc_dram"][(7 - b) + i * -2, :, 0:20, :].rearrange("p a c -> p (a c)")
                                     ).then_inc(s_xb[b], 16)
                sp.wait_ge(s_xb[1], 80)

            @block.tensor
            def _(pe):
                def turn(b, done):
                    for a in range(20):
                        ins = pe.transpose(pb[:, a // 4, (a % 4) * P:(a % 4 + 1) * P], xb[:, b, a * P:(a + 1) * P], ident)
                    ins.then_inc(s_tr, 1)

                pe.wait_ge(s_xb[0], 16)
                turn(0, 0)
                pe.wait_ge(s_xw, 8)
                pe.wait_ge(s_row, 5)
                for d in range(2):
                    for a in range(16):
                        n = d * 16 + a
                        if n % 4 == 0 and n >= 12:
                            pe.wait_ge(s_cx, n // 4 - 2)
                        ins = pe.matmul(pb[:, 5 + (n // 4) % 3, (a % 4) * P:(a % 4 + 1) * P], xw[:, d, a * P:(a + 1) * P],
                                        brow[:, 0, (a // 4) * P:(a // 4 + 1) * P], start=True, stop=True)
                        if a % 4 == 3:
                            ins.then_inc(s_con, 1)
                pe.wait_ge(s_init, 64)
                for d in range(2):
                    for a in range(16):
                        n = d * 16 + a
                        if n % 4 == 0:
                            if n == 0:
                                pe.wait_ge(s_cx, 8)
                            if n >= 12:
                                pe.wait_ge(s_ik, n // 4 - 2)
                        ins = pe.transpose(pb[:, 5 + (n // 4) % 3, (a % 4) * P:(a % 4 + 1) * P], init[:, d, a, :], ident)
                        if a % 4 == 3:
                            ins.then_inc(s_it, 1)
                pe.wait_ge(s_ik, 8)
                with pe.Fori(0, 4) as i:
                    for b in range(2):
                        pe.wait_ge(s_row, i * 10 + (5 * b + 5))
                        if b == 0:
                            pe.wait_ge(s_xb[1], i * 16 + 16)
                        else:
                            pe.wait_ge(s_xb[0], i * 16 + 32)
                        turn(1 - b, 0)
                        pe.wait_ge(s_row, i * 10 + (5 * b + 10))
                        for g in range(GROUPS):
                            n = 4 * b + g
                            pe.wait_ge(s_xw, i * 8 + (n + 9))
                            pe.wait_ge(s_new, i * 8 + (4 * b + (1 if g == 3 else 0)))
                            pe.matmul(pb[:, 5 + g % 3, :], brow[:, b, g * P:(g + 1) * P], xw[:, b, g * GW:(g + 1) * GW],
                                      start=True, stop=True).then_inc(s_con, 1)

            @block.scalar
            def _(act):
                def rows(b, br):
                    for a in range(4):
                        act.activation(xrow[:, b, a * GW:(a + 1) * GW], pb[:, a, :], ACT.Copy).then_inc(s_row, 1)
                    act.activation(brow[:, br, :], pb[:, 4, :], ACT.Copy).then_inc(s_row, 1)

                act.wait_ge(s_tr, 1)
                rows(0, 0)
                for n in range(8):
                    act.wait_ge(s_con, n + 1)
                    act.activation(out[:, n // 4, 4 * (n % 4):4 * (n % 4) + 4, :].rearrange("p a c -> p (a c)"),
                                   pb[:, 5 + n % 3, :], ACT.Copy).then_inc(s_cx, 1)
                act.wait_ge(s_cx, 8)
                for d in range(2):
                    for h in range(2):
                        act.dma_start(io["new_state"][0, 0, d].rearrange("(a b) p n -> b p a n", b=2)[h],
                                      out[h * HEAD:(h + 1) * HEAD, d, :, :]).then_inc(s_out, 16)
                for n in range(8):
                    act.wait_ge(s_it, n + 1)
                    dst = state if n < 4 else sb_[:, 0, :]
                    act.activation(dst[:, (n % 4) * GW:(n % 4 + 1) * GW], pb[:, 5 + n % 3, :], ACT.Copy).then_inc(s_ik, 1)
                with act.Fori(0, 4) as i:
                    for b in range(2):
                        act.wait_ge(s_tr, i * 2 + (b + 2))
                        act.wait_ge(s_xw, i * 8 + (4 * b + 8))
                        act.wait_ge(s_con, i * 8 + (4 * b + 8) )
                        rows(b, b)
                act.wait_ge(s_out, 64)

            @block.vector
            def _(dve):
                dve.tensor_copy(rc[:, 0, :, :], rates[:, 0, :, :]).then_inc(s_rc, 1)
                dve.wait_ge(s_rc, 1)
                for d in range(2):
                    for g in range(GROUPS):
                        dve.wait_ge(s_row, g + 1)
                        h0 = d * HEADS + g * GH
                        dve.tensor_tensor(by_head(xw[:, d, g * GW:(g + 1) * GW]), by_head(xrow[:, 0, g * GW:(g + 1) * GW]),
                                          per_head(rc[:, 0, R_W, h0:h0 + GH]), ALU.mult).then_inc(s_xw, 1)
                dve.wait_ge(s_ik, 8)
                with dve.Fori(0, 4) as i:
                    for b in range(2):
                        dve.wait_ge(s_new, i * 8 + 4 * b)
                        dve.wait_ge(s_xw, i * 8 + (4 * b + 8))
                        dve.tensor_copy(rc[:, b, :, :], rates[:, bass.ds((8 - b) + i * -2, 1), :, :].rearrange("p a b c -> p (a b) c")
                                        ).then_inc(s_rc, 1)
                        dve.wait_ge(s_rc, i * 2 + (b + 2))
                        for g in range(GROUPS):
                            h0 = HEADS + g * GH
                            cols = slice(g * GW, (g + 1) * GW)
                            dve.wait_ge(s_row, i * 10 + (5 * b + g + 6))
                            if g == 0:
                                dve.wait_ge(s_con, i * 8 + (4 * b + 8))
                            dve.tensor_tensor(by_head(xw[:, b, cols]), by_head(xrow[:, b, cols]),
                                              per_head(rc[:, b, R_W, h0:h0 + GH]), ALU.mult).then_inc(s_xw, 1)
                            dve.tensor_tensor(by_head(decayed[:, cols]), by_head(sb_[:, b, cols]),
                                              per_head(rc[:, b, R_TOT, h0:h0 + GH]), ALU.mult).then_inc(s_dec, 1)
                        dve.wait_ge(s_st[1 - b], i * 16 + 16 * b)
                        for g in range(GROUPS):
                            n = 4 * b + g
                            cols = slice(g * GW, (g + 1) * GW)
                            dve.wait_ge(s_con, i * 8 + (n + 9))
                            dve.wait_ge(s_dec, i * 8 + (n + 1))
                            dve.tensor_tensor(sb_[:, 1 - b, cols], decayed[:, cols], pb[:, 5 + g % 3, :], ALU.add
                                              ).then_inc(s_new, 1)

            @block.gpsimd
            def _(pool):
                pool.wait_ge(s_ik, 8)
                with pool.Fori(0, 4) as i:
                    for b in range(2):
                        pool.wait_ge(s_new, i * 8 + 4 * b)
                        pool.dma_start(io["sb_dram"][(8 - b) + i * -2], sb_[:, b, :]).then_inc(s_st[b], 16)
                for b in range(2):
                    pool.wait_ge(s_st[b], 4 * 16)


def phase_scan(nc, io, keep):
    x_rows = io["x_dram"].rearrange("(t p) d -> t p d", p=P)
    with ExitStack() as ctx:
        m = Mem(nc, ctx, "scan_")
        w = m.sb("w", [P, Z_TILES, D])
        xbc = m.sb("xbc", [P, 2, XBC_TILES, P])
        zt = m.sb("z", [P, Z_TILES, P])
        sbt = m.sb("state_back", [P, INNER])
        xr = m.sb("x", [P, D])
        gate = m.sb("gate", [P, 2, D])
        rc = m.sb("rates", [P, 2, 5, 64])
        tri_by = m.sb("tri_by_rate", [P, 2, GH, P])
        ex = m.sb("exp", [P, 2, GH, P])
        mix = m.sb("mix", [P, GH, P])
        cb = m.sb("cb", [P, 2, GROUPS, P])
        xrow = m.sb("xrow", [P, INNER])
        brow = m.sb("brow", [P, GROUPS * P])
        xw = m.sb("xw", [P, GW])
        tmp = m.sb("tmp", [P, 2, GW])
        y = m.sb("y", [P, INNER])
        yc = m.sb("yc", [P, Z_TILES, P])
        red = m.sb("red", [P, P])
        ones = m.sb("ones", [P, 2])
        st = m.sb("stats", [P, 2])
        sq = y[:, :].rearrange("p (a c) -> p a c", c=P)
        pb = m.psum()
        s_w = m.sem("w_in")
        s_gw = m.sem("w_scaled")
        s_gate = m.sem("gate_in")
        s_c = [m.sem(f"chunk_in{b}") for b in range(2)]
        s_z = m.sem("z_in")
        s_sb = m.sem("state_back_in")
        s_x = m.sem("x_in")
        s_one = m.sem("ones_ready")
        s_rc = m.sem("rates_ready")
        s_tx = m.sem("chunk_transposed")
        s_row = m.sem("rows_ready")
        s_cb = m.sem("cb_done")
        s_cbm = m.sem("cb_masked")
        s_tr = m.sem("tri_by_rate_ready")
        s_seg = m.sem("segments")
        s_ex = m.sem("exp_ready")
        s_dve = m.sem("dve")
        s_mix = m.sem("mix_ready")
        s_y = m.sem("diagonal_done")
        s_off = m.sem("off_done")
        s_xw = m.sem("weighted")
        s_con = m.sem("contribution")
        s_yr = m.sem("y_rows_ready")
        s_new = m.sem("state_ready")
        s_yt = m.sem("y_transposed")
        s_yk = m.sem("y_kept")
        s_zg = m.sem("gated")
        s_sq = m.sem("squared")
        s_red = m.sem("squares_summed")
        s_ss = m.sem("norm_summed")
        s_pj = m.sem("projected")
        s_rt = m.sem("root")
        s_pe = m.sem("projection_kept")
        s_sum = m.sem("x_summed")
        s_st = m.sem("x_stored")
        s_gc = m.sem("gate_changed")
        s_cm = m.sem("combined")
        s_rcp = m.sem("inverse_root")
        state, rates, ident, tri, prm = keep["state"], keep["rates"], keep["ident"], keep["tri"], keep["prm"]
        B_T, C_T = 16, 20

        with nc.Block() as block:

            @block.sync
            def _(sp):
                for c in range(2):
                    sp.dma_start(xbc[:, c, :, :], io["xbc_dram"][c]).then_inc(s_c[c], 16)
                    if c == 0:
                        sp.dma_start(w[:, :, :], io["ssd_out_w"][0].rearrange("(k p) n -> p k n", p=P)).then_inc(s_w, 16)
                        sp.dma_start(sbt[:, :], io["sb_dram"][1]).then_inc(s_sb, 16)
                        for n in range(2):
                            sp.dma_start(gate[:, n, :], io["vec_dram"][1, n, V_G1:V_G1 + 1, :].partition_broadcast(P)
                                         ).then_inc(s_gate, 16)
                        sp.dma_start(zt[:, :, :], io["z_dram"][0]).then_inc(s_z, 16)
                        sp.dma_start(xr[:, :], x_rows[0]).then_inc(s_x, 16)

                for t in range(TILES):
                    sp.wait_ge(s_yk, t * 16 + 16)
                    if t + 2 < TILES:
                        sp.dma_start(xbc[:, t % 2, :, :], io["xbc_dram"][t + 2]).then_inc(s_c[t % 2], 16)
                    if t < LAST_TILE:
                        sp.wait_ge(s_zg, t + 1)
                        sp.dma_start(zt[:, :, :], io["z_dram"][t + 1]).then_inc(s_z, 16)
                    sp.wait_ge(s_sum, t + 1)
                    sp.dma_start(x_rows[t], xr[:, :]).then_inc(s_st, 16)
                    sp.wait_ge(s_st, t * 16 + 16)
                    if t < LAST_TILE:
                        sp.dma_start(xr[:, :], x_rows[t + 1]).then_inc(s_x, 16)
                    if t + 2 < TILES:
                        sp.wait_ge(s_yr, t * 4 + 8)
                        sp.dma_start(sbt[:, :], io["sb_dram"][t + 2]).then_inc(s_sb, 16)

            @block.tensor
            def _(pe):
                def turn_in(b, c, use, ctx_chunk):
                    pe.wait_ge(s_c[b], use * 16 + 16)
                    if not ctx_chunk:
                        pe.wait_ge(s_ex, c * 8)
                        pe.wait_ge(s_yr, c * 4)
                    for a in range(16):
                        ins = pe.transpose(pb[:, a // 4, (a % 4) * P:(a % 4 + 1) * P], xbc[:, b, a, :], ident)
                        if a % 4 == 3:
                            ins.then_inc(s_tx, 1)
                    for a in range(GROUPS):
                        ins = pe.transpose(pb[:, 4, a * P:(a + 1) * P], xbc[:, b, B_T + a, :], ident)
                    ins.then_inc(s_tx, 1)
                    for g in range(GROUPS):
                        ins = pe.matmul(pb[:, 5, g * P:(g + 1) * P], xbc[:, b, B_T + g, :], xbc[:, b, C_T + g, :],
                                        start=True, stop=True)
                    ins.then_inc(s_cb, 1)

                def turn_y(t):
                    pe.wait_ge(s_yr, t * 4 + 4)
                    pe.wait_ge(s_new, t * 4 + 4)
                    for q in range(4):
                        if q >= 2:
                            pe.wait_ge(s_yk, t * 16 + 4 * (q - 1))
                        for a in range(4):
                            ins = pe.transpose(pb[:, 6 + q % 2, a * P:(a + 1) * P], y[:, (4 * q + a) * P:(4 * q + a + 1) * P], ident)
                        ins.then_inc(s_yt, 1)

                def project(t):
                    pe.wait_ge(s_zg, t + 1)
                    for half in range(2):
                        for k in range(Z_TILES):
                            ins = pe.matmul(pb[:, 6 + half, :], yc[:, k, :], w[:, k, half * HALF:(half + 1) * HALF],
                                            start=(k == 0), stop=(k == Z_TILES - 1))
                    ins.then_inc(s_pj, 1)
                    pe.wait_ge(s_red, t + 1)
                    pe.matmul(pb[:, 5, 0:2], red[:, :], ones[:, :], start=True, stop=True).then_inc(s_ss, 1)

                def segments(g, c):
                    n = g
                    pe.wait_ge(s_tr, c * 8 + (2 * n + 2))
                    if g == 0:
                        pe.wait_ge(s_row, c * 5 + 4)
                    else:
                        pe.wait_ge(s_ex, c * 8 + 2 * n)
                    for d, left in enumerate((TRI_GT, TRI_LT)):
                        for half in range(2):
                            ins = pe.matmul(pb[:, 2 * d + half, :], tri[:, left, :],
                                            tri_by[:, d, 4 * half:4 * half + 4, :].rearrange("p a c -> p (a c)"),
                                            start=True, stop=True)
                        ins.then_inc(s_seg, 1)

                def group(g, b, c, ctx_chunk):
                    if g < 3:
                        segments(g + 1, c)
                    if not ctx_chunk:
                        if g:
                            pe.wait_ge(s_yr, c * 4 + g)
                            pe.wait_ge(s_new, c * 4 + g)
                        else:
                            pe.wait_ge(s_sb, c * 16)
                            pe.wait_ge(s_row, c * 5 + 5)
                            pe.wait_ge(s_new, c * 4)
                            pe.wait_ge(s_pe, c)
                            pe.wait_ge(s_rt, c)
                        cols = slice(g * GW, (g + 1) * GW)
                        pe.matmul(pb[:, 5, :], xbc[:, b, C_T + g, :], state[:, cols], start=True, stop=True)
                        pe.matmul(pb[:, 6, :], xbc[:, b, C_T + g, :], sbt[:, cols], start=True, stop=True).then_inc(s_off, 1)
                        pe.wait_ge(s_xw, c * 4 + (g - 3))
                        pe.matmul(pb[:, 7, :], brow[:, g * P:(g + 1) * P], xw[:, :], start=True, stop=True).then_inc(s_con, 1)
                    else:
                        if g:
                            pe.wait_ge(s_yr, g)
                        else:
                            pe.wait_ge(s_row, 5)
                    pe.wait_ge(s_mix, c * 4 + (g + 1))
                    for h in range(GH):
                        ins = pe.matmul(pb[:, 4, h * HEAD:(h + 1) * HEAD], mix[:, h, :],
                                        xrow[:, (g * GH + h) * HEAD:(g * GH + h + 1) * HEAD], start=True, stop=True)
                    ins.then_inc(s_y, 1)

                pe.wait_ge(s_one, 1)
                turn_in(0, 0, 0, True)
                segments(0, 0)
                for g in range(GROUPS):
                    group(g, 0, 0, True)

                def chunk(b, c, use):
                    turn_in(b, c, use, False)
                    pe.wait_ge(s_cbm, c * 2 + 2)
                    turn_y(c - 1)
                    segments(0, c)
                    project(c - 1)
                    for g in range(GROUPS):
                        group(g, b, c, False)

                pe.wait_ge(s_gw, Z_TILES)
                with pe.Fori(0, 4) as i:
                    chunk(1, i * 2 + 1, i)
                    chunk(0, i * 2 + 2, i + 1)
                turn_y(8)
                pe.wait_ge(s_gate, 32)
                project(8)

            @block.scalar
            def _(act):
                def rows(c, ctx_chunk):
                    for a in range(4):
                        act.wait_ge(s_tx, c * 5 + (a + 1))
                        if a == 0 and not ctx_chunk:
                            act.wait_ge(s_y, c * 4)
                        act.activation(xrow[:, a * GW:(a + 1) * GW], pb[:, a, :], ACT.Copy).then_inc(s_row, 1)
                    act.wait_ge(s_tx, c * 5 + 5)
                    if not ctx_chunk:
                        act.wait_ge(s_new, c * 4)
                    act.activation(brow[:, :], pb[:, 4, :], ACT.Copy).then_inc(s_row, 1)

                def exps(g, c):
                    for d in range(2):
                        act.wait_ge(s_seg, c * 8 + (2 * g + d + 1))
                        if d == 0:
                            act.wait_ge(s_mix, c * 4 + g)
                        act.activation(ex[:, d, :, :].rearrange("p (a h) c -> p a (h c)", a=2), pb[:, 2 * d:2 * d + 2, :], ACT.Exp
                                       ).then_inc(s_ex, 1)

                def square(t):
                    act.wait_ge(s_zg, t + 1)
                    act.wait_ge(s_yt, t * 4 + 4)
                    act.activation(sq, yc[:, :, :], ACT.Square).then_inc(s_sq, 1)

                def root(t):
                    act.wait_ge(s_ss, t + 1)
                    act.activation(st[:, 0:1], pb[:, 5, 0:1], ACT.Sqrt, bias=keep["eps"][:, 0:1], scale=1.0 / INNER
                                   ).then_inc(s_rt, 1)

                rows(0, True)
                for g in range(GROUPS):
                    exps(g, 0)

                def chunk(c):
                    rows(c, False)
                    exps(0, c)
                    square(c - 1)
                    root(c - 1)
                    for g in range(1, GROUPS):
                        exps(g, c)

                with act.Fori(0, 4) as i:
                    chunk(i * 2 + 1)
                    chunk(i * 2 + 2)
                square(8)
                root(8)

            @block.gpsimd
            def _(pool):
                def chunk(b, c):
                    pool.wait_ge(s_rc, c + 1)
                    for g in range(GROUPS):
                        for d, left in enumerate((TRI_LE, TRI_GE)):
                            pool.wait_ge(s_seg, c * 8 + (2 * g + d - 1) if (g or d) else c * 8)
                            h0 = d * HEADS + g * GH
                            pool.tensor_tensor(tri_by[:, d, :, :], tri[:, left:left + 1, :].broadcast_to([P, GH, P]),
                                               rc[:, b, R_DA, h0:h0 + GH].unsqueeze(2).broadcast_to([P, GH, P]), ALU.mult
                                               ).then_inc(s_tr, 1)

                chunk(0, 0)
                with pool.Fori(0, 4) as i:
                    chunk(1, i * 2 + 1)
                    chunk(0, i * 2 + 2)

            @block.vector
            def _(dve):
                dve.memset(ones[:, :], 1.0).then_inc(s_one, 1)

                def get_rates(b, c, ctx_chunk):
                    if not ctx_chunk:
                        dve.wait_ge(s_tr, c * 8 - 8)
                        dve.wait_ge(s_yr, c * 4 - 4)
                        dve.wait_ge(s_new, c * 4 - 4)
                    src = rates[:, 0, :, :] if ctx_chunk else rates[:, bass.ds(c, 1), :, :].rearrange("p a b c -> p (a b) c")
                    dve.tensor_copy(rc[:, b, :, :], src).then_inc(s_rc, 1)

                def masks(c):
                    dve.wait_ge(s_cb, c + 1)
                    dve.wait_ge(s_mix, c * 4)
                    for d, left in enumerate((TRI_LE, TRI_GE)):
                        dve.tensor_tensor(cb[:, d, :, :], pb[:, 5, :].rearrange("p (a c) -> p a c", c=P),
                                          tri[:, left:left + 1, :].broadcast_to([P, GROUPS, P]), ALU.mult).then_inc(s_cbm, 1)

                def mixing(g, b, c):
                    for d in range(2):
                        dve.wait_ge(s_ex, c * 8 + (2 * g + d + 1))
                        if d == 0:
                            dve.wait_ge(s_cbm, c * 2 + 2)
                        for h in range(GH):
                            col = d * HEADS + g * GH + h
                            ins = dve.scalar_tensor_tensor(ex[:, d, h, :], ex[:, d, h, :], rc[:, b, R_DT, col:col + 1],
                                                           cb[:, d, g, :], ALU.mult, ALU.mult)
                        ins.then_inc(s_dve, 1)
                    dve.wait_ge(s_dve, c * 8 + (2 * g + 2))
                    dve.wait_ge(s_y, c * 4 + g)
                    dve.tensor_tensor(mix[:, :, :], ex[:, 0, :, :], ex[:, 1, :, :], ALU.add).then_inc(s_mix, 1)

                def weigh(g, b, c):
                    cols = slice(g * GW, (g + 1) * GW)
                    dve.wait_ge(s_row, c * 5 + (g + 1))
                    if g:
                        dve.wait_ge(s_con, c * 4 + (g - 4))
                    else:
                        dve.wait_ge(s_con, c * 4 - 4)
                    dve.tensor_tensor(by_head(xw[:, :]), by_head(xrow[:, cols]),
                                      per_head(rc[:, b, R_W, g * GH:(g + 1) * GH]), ALU.mult).then_inc(s_xw, 1)

                def combine(g, b, c, ctx_chunk):
                    cols = slice(g * GW, (g + 1) * GW)
                    if ctx_chunk:
                        dve.wait_ge(s_y, g + 1)
                        dve.tensor_copy(y[:, cols], pb[:, 4, :]).then_inc(s_yr, 1)
                        return
                    dve.wait_ge(s_off, c * 4 + (g - 3))
                    dve.wait_ge(s_yr, c * 4 + g)
                    dve.wait_ge(s_sum, c)
                    dve.wait_ge(s_new, c * 4 + g)
                    for d in range(2):
                        h0 = d * HEADS + g * GH
                        dve.tensor_tensor(by_head(tmp[:, d, :]), by_head(pb[:, 5 + d, :]),
                                          per_head(rc[:, b, R_IN, h0:h0 + GH]), ALU.mult).then_inc(s_cm, 1)
                    dve.tensor_tensor(by_head(state[:, cols]), by_head(state[:, cols]),
                                      per_head(rc[:, b, R_TOT, g * GH:(g + 1) * GH]), ALU.mult).then_inc(s_cm, 1)
                    dve.wait_ge(s_cm, c * 16 + (4 * g - 13))
                    dve.tensor_tensor(tmp[:, 0, :], tmp[:, 0, :], tmp[:, 1, :], ALU.add).then_inc(s_cm, 1)
                    dve.wait_ge(s_con, c * 4 + (g - 3))
                    dve.tensor_tensor(state[:, cols], state[:, cols], pb[:, 7, :], ALU.add).then_inc(s_new, 1)
                    dve.wait_ge(s_y, c * 4 + (g + 1))
                    if g == 0:
                        dve.wait_ge(s_red, c)
                    dve.wait_ge(s_cm, c * 16 + (4 * g - 12))
                    dve.tensor_tensor(y[:, cols], tmp[:, 0, :], pb[:, 4, :], ALU.add).then_inc(s_yr, 1)

                def gating(bt, t):
                    for q in range(4):
                        dve.wait_ge(s_yt, t * 4 + (q + 1))
                        if q == 0:
                            dve.wait_ge(s_pj, t)
                            dve.wait_ge(s_sq, t)
                        for a in range(4):
                            k = 4 * q + a
                            dve.scalar_tensor_tensor(yc[:, k, :], xbc[:, bt, k, :], keep["d_skip"][:, k:k + 1],
                                                     pb[:, 6 + q % 2, a * P:(a + 1) * P], ALU.mult, ALU.add).then_inc(s_yk, 1)
                    dve.wait_ge(s_yk, t * 16 + 16)
                    dve.wait_ge(s_z, t * 16 + 16)
                    dve.tensor_tensor(yc[:, :, :], yc[:, :, :], zt[:, :, :], ALU.mult).then_inc(s_zg, 1)

                def reduce(t):
                    dve.wait_ge(s_sq, t + 1)
                    dve.wait_ge(s_ss, t)
                    dve.tensor_reduce(red[:, :], sq.rearrange("p a c -> p c a"), AX.X, ALU.add).then_inc(s_red, 1)

                def residual(t, cond):
                    dve.wait_ge(s_yr, t * 4 + 4)
                    dve.wait_ge(s_new, t * 4 + 4)
                    dve.wait_ge(s_rt, t + 1)
                    dve.reciprocal(st[:, 1:2], st[:, 0:1]).then_inc(s_rcp, 1)
                    dve.wait_ge(s_rcp, t + 1)
                    dve.wait_ge(s_pj, t + 1)
                    dve.wait_ge(s_x, t * 16 + 16)
                    dve.scalar_tensor_tensor(tmp[:, :, :].rearrange("p a c -> p (a c)"), pb[:, 6:8, :].rearrange("p a c -> p (a c)"),
                                             st[:, 1:2], gate[:, cond, :], ALU.mult, ALU.mult).then_inc(s_pe, 1)
                    dve.wait_ge(s_pe, t + 1)
                    dve.tensor_tensor(xr[:, :], xr[:, :], tmp[:, :, :].rearrange("p a c -> p (a c)"), ALU.add).then_inc(s_sum, 1)

                get_rates(0, 0, True)
                dve.wait_ge(s_rc, 1)
                masks(0)
                mixing(0, 0, 0)
                for g in range(GROUPS):
                    if g < 3:
                        mixing(g + 1, 0, 0)
                    combine(g, 0, 0, True)
                for g in range(GROUPS):
                    dve.memset(tmp[0:1, 0, g:g + 1], 0.0).then_inc(s_new, 1)
                dve.wait_ge(s_w, 16)
                for k in range(Z_TILES):
                    dve.tensor_scalar(w[:, k, :], w[:, k, :], prm[:, 1, XBC_TILES + k:XBC_TILES + k + 1], None, ALU.mult
                                      ).then_inc(s_gw, 1)
                dve.wait_ge(s_gate, 32)

                def chunk(b, c, first):
                    get_rates(b, c, False)
                    masks(c)
                    gating(1 - b, c - 1)
                    dve.wait_ge(s_rc, c + 1)
                    mixing(0, b, c)
                    reduce(c - 1)
                    weigh(0, b, c)
                    residual(c - 1, CTX if first else LATENT)
                    if first:
                        dve.wait_ge(s_pe, c)
                        dve.tensor_copy(gate[:, CTX, :], gate[:, LATENT, :]).then_inc(s_gc, 1)
                    for g in range(GROUPS):
                        if g < 3:
                            mixing(g + 1, b, c)
                        combine(g, b, c, False)
                        if g < 3:
                            weigh(g + 1, b, c)

                with dve.Fori(0, 4) as i:
                    dve.wait_ge(s_gc, i)
                    chunk(1, i * 2 + 1, True)
                    chunk(0, i * 2 + 2, False)
                gating(0, 8)
                reduce(8)
                residual(8, LATENT)


def phase_final(nc, io, keep):
    x_rows = io["x_dram"].rearrange("(t p) d -> t p d", p=P)
    with ExitStack() as ctx:
        m = Mem(nc, ctx, "final_")
        x = m.sb("x", [P, TILES, D])
        squares = m.sb("squares", [P, TILES, D])
        g = m.sb("gain", [P, D])
        st = m.sb("stats", [P, TILES, 3])
        s_x = [m.sem(f"x_in{t}") for t in range(TILES)]
        s_g = m.sem("gain_in")
        s_sq = m.sem("squared")
        s_root = m.sem("root_ready")
        s_rcp = m.sem("reciprocal_ready")
        s_y = m.sem("y_ready")
        s_out = m.sem("y_stored")

        with nc.Block() as block:

            @block.sync
            def _(sp):
                sp.dma_start(x[:, 0, :], x_rows[0]).then_inc(s_x[0], 16)
                sp.dma_start(g[:, :], io["final_norm_g"].rearrange("(a d) -> a d", a=1).partition_broadcast(P)).then_inc(s_g, 16)
                for t in range(1, TILES):
                    sp.dma_start(x[:, t, :], x_rows[t]).then_inc(s_x[t], 16)
                for t in range(TILES):
                    sp.wait_ge(s_y, t + 1)
                    dst = io["y_prompt"][0] if t == 0 else io["y_sample"][0, (t - 1) * P:t * P, :]
                    sp.dma_start(dst, x[:, t, :]).then_inc(s_out, 16)
                sp.wait_ge(s_out, 16 * TILES)

            @block.scalar
            def _(act):
                for t in range(TILES):
                    act.wait_ge(s_x[t], 16)
                    act.activation(squares[:, t, :], x[:, t, :], ACT.Square, accum_out=st[:, t, 0:1]).then_inc(s_sq, 1)
                    act.wait_ge(s_sq, t + 1)
                    act.activation(st[:, t, 1:2], st[:, t, 0:1], ACT.Sqrt, bias=keep["eps"][:, 0:1], scale=1.0 / D
                                   ).then_inc(s_root, 1)

            @block.vector
            def _(dve):
                dve.wait_ge(s_g, 16)
                for t in range(TILES):
                    dve.wait_ge(s_root, t + 1)
                    dve.reciprocal(st[:, t, 2:3], st[:, t, 1:2]).then_inc(s_rcp, 1)
                    dve.wait_ge(s_rcp, t + 1)
                    dve.scalar_tensor_tensor(x[:, t, :], x[:, t, :], st[:, t, 2:3], g[:, :], ALU.mult, ALU.mult
                                             ).then_inc(s_y, 1)


def build(nc, io):
    with ExitStack() as ctx:
        m = Mem(nc, ctx)
        tri = m.sb("tri", [P, 5, P])
        keep = {
            "tri": tri, "ident": tri[:, 0, :],
            "eps": m.sb("eps", [P, 1]),
            "prm": m.sb("prm", [P, 4, 120]),
            "mod": m.sb("mod", [P, 2, 96]),
            "gain1": m.sb("gain1", [P, 2, 2, KD]),
            "d_skip": m.sb("d_skip", [P, Z_TILES]),
            "s_const": m.sem("const_in"),
        }
        rows = lambda a: a.rearrange("w (t p) -> (w t) p", p=P)
        keep["param_rows"] = [
            (rows(io["ssd_conv_w"][0]), (0, 0), 120),
            (rows(io["ssd_conv_b"]), (1, 0), 24), (rows(io["ssd_norm_g"]), (1, 24), 16),
            (rows(io["hy_short_w"][0]), (2, 0), 72), (rows(io["hy_in_b"]), (2, 72), 24),
            (rows(io["hy_short_b"]), (2, 96), 24),
            (rows(io["norm_g"][0, 0:1, :]), (3, 0), 8), (rows(io["norm_g"][1, 0:1, :]), (3, 8), 8),
        ]
        keep["param_counts"] = (120, 40, 120, 16)
        with nc.Block() as block:
            @block.sync
            def _(sp):
                sp.dma_start(tri[:, :, :], io["tri"].rearrange("p (a b) -> p a b", b=P)).then_inc(keep["s_const"], 16)
        phase_modulation(nc, io, keep)
        with ExitStack() as inner:
            keep["hT"] = inner.enter_context(nc.sbuf_tensor("hT0", [P, KD, TOK], F32))
            phase_norm(nc, io, keep, 0)
            phase_hyena_in(nc, io, keep)
        with ExitStack() as inner:
            keep["filt"] = inner.enter_context(nc.sbuf_tensor("filt", [HY_HID, TAPS], F32))
            phase_filter(nc, io, keep)
            phase_long_conv(nc, io, keep)
        phase_hyena_out(nc, io, keep)
        mixture(nc, io, keep, 0)
        with ExitStack() as ssd:
            keep["rates"] = ssd.enter_context(nc.sbuf_tensor("rates", [P, TILES, 5, 2 * HEADS], F32))
            with ExitStack() as inner:
                keep["hT"] = inner.enter_context(nc.sbuf_tensor("hT1", [P, KD, TOK], F32))
                phase_norm(nc, io, keep, 1)
                phase_ssd_in(nc, io, keep)
            keep["state"] = ssd.enter_context(nc.sbuf_tensor("state", [P, INNER], F32))
            phase_states(nc, io, keep)
            phase_scan(nc, io, keep)
        mixture(nc, io, keep, 1)
        phase_final(nc, io, keep)


def shape_constants():
    r = np.arange(P)
    tri = np.stack([r[:, None] == r, r[:, None] <= r, r[:, None] > r, r[:, None] >= r, r[:, None] < r], 1)
    q = D // 4
    omega = (1.0 / (10000.0 ** (np.arange(q, dtype=np.float32) / np.float32(q)))).astype(np.float32)
    t = np.arange(LAT)
    er = (t // 64).astype(np.float32)[:, None] * omega
    ec = (t % 64).astype(np.float32)[:, None] * omega
    pos = np.concatenate([np.sin(er), np.cos(er), np.sin(ec), np.cos(ec)], -1)

    def clock(n):
        at = np.concatenate([np.arange(n), n - np.arange(n)])
        at[n] = 0
        tt = np.linspace(0.0, 1.0, n, dtype=np.float32)[:, None]
        w = (2.0 * np.pi * np.arange(n, dtype=np.float32)[:, None] / n).astype(np.float32)
        f = np.linspace(1e-4, 15, 16, dtype=np.float32)[None]
        z = np.concatenate([tt, np.cos(f * w), -np.sin(f * w)], -1)
        return z[at].T, tt[at, 0]

    z1, t1 = clock(LAT)
    z2, t2 = clock(CTX_ROWS)
    zfeat = np.concatenate([z1, z2], 1)
    negt = -np.concatenate([t1, t2]).reshape(18, P).T
    deltas = np.abs(np.linspace(np.log(1e-2) / 1.5, np.log(1e-2) / 0.3, D, dtype=np.float32))[None]

    b = np.arange(256)
    ang = lambda k, r_: 2 * np.pi * ((b[:, None] * (8 * k[None] + r_)) % NFFT) / NFFT
    k1, k2 = np.arange(128), np.arange(256)
    f0 = np.concatenate([np.cos(ang(k1, 0)), -np.sin(ang(k1, 0))], 1)
    f0[:, 128] = (-1.0) ** b
    f4 = np.concatenate([np.cos(ang(k1, 4)), -np.sin(ang(k1, 4))], 1)
    fwd = [f0, f4] + [x for r_ in (2, 1, 3) for x in (np.cos(ang(k2, r_)), np.sin(ang(k2, r_)), -np.sin(ang(k2, r_)))]
    fwd = np.concatenate(fwd, 1).reshape(2, P, -1).transpose(1, 0, 2)
    g0 = np.concatenate([np.cos(ang(k1, 0)), -np.sin(ang(k1, 0))], 1).T * 2
    g0[0] = 1.0
    g0[128] = (-1.0) ** b
    g4 = np.concatenate([np.cos(ang(k1, 4)), -np.sin(ang(k1, 4))], 1).T * 2
    inv04 = np.stack([g0, g4]).reshape(2, 2, P, 256).transpose(2, 0, 1, 3) / NFFT
    inv = []
    for r_ in (2, 1, 3):
        c, s = np.cos(ang(k2, r_)).T, np.sin(ang(k2, r_)).T
        inv.append(np.concatenate([np.concatenate([c, s], 1), np.concatenate([-s, c], 1)], 0).reshape(4, P, 512))
    inv = np.stack(inv).transpose(2, 0, 1, 3) * 2 / NFFT
    f32 = lambda a: np.ascontiguousarray(a, dtype=np.float32)
    return {"tri": f32(tri.reshape(P, -1)), "pos": f32(pos), "zfeat": f32(zfeat), "negt": f32(negt), "deltas": f32(deltas),
            "fwd": f32(fwd.reshape(P, -1)), "inv04": f32(inv04.reshape(P, -1)), "inv": f32(inv.reshape(P, -1))}


INPUTS = ["x_prompt", "x_sample", "state_ssd", "c", "c_ctx", "norm_g", "ada_w", "ada_b",
          "hy_in_w", "hy_in_b", "hy_short_w", "hy_short_b", "hy_f_w1", "hy_f_b1", "hy_f_w2", "hy_f_b2",
          "hy_f_w3", "hy_f_freq", "hy_f_bias", "hy_out_w",
          "ssd_in_w", "ssd_conv_w", "ssd_conv_b", "ssd_dt_bias", "ssd_A_log", "ssd_D", "ssd_norm_g", "ssd_out_w",
          "moe_router", "moe_w_gate", "moe_w_up", "moe_w_down", "final_norm_g"]
OUTPUTS = {"y_prompt": (1, CTX_ROWS, D), "y_sample": (1, LAT, D), "new_state": (1, 1, 2, HEADS, HEAD, 128)}
SCRATCH = {"mod_dram": (2, 12 * D), "vec_dram": (2, 2, 4, D), "x_dram": (TOK, D), "h_dram": (TOK, D),
           "x0_dram": (KD, P, GAPPED), "u_dram": (P, TILES, D), "g_dram": (KD, P, TOK),
           "xbc_dram": (TILES, P, XBC_TILES, P), "z_dram": (TILES, P, Z_TILES, P), "sb_dram": (TILES, P, INNER)}


def lay_out(nc, inputs):
    arrays = {f"in_{n}": np.ascontiguousarray(inputs[n]) for n in INPUTS}
    arrays.update({f"in_{n}": a for n, a in shape_constants().items()})
    io = {n[3:]: nc.dram_tensor(n, a.shape, F32, kind="ExternalInput").ap() for n, a in arrays.items()}
    io.update({n: nc.dram_tensor(f"out_{n}", s, F32, kind="ExternalOutput").ap() for n, s in OUTPUTS.items()})
    io.update({n: nc.dram_tensor(n, s, F32, kind="Internal").ap() for n, s in SCRATCH.items()})
    return arrays, io


def kernel(**inputs):
    import concourse.bacc as bacc
    from concourse.bass_utils import run_bass_kernel_spmd

    nc = bacc.Bacc("TRN2", target_bir_lowering=False, num_devices=1)
    arrays, io = lay_out(nc, inputs)
    build(nc, io)
    r = run_bass_kernel_spmd(nc, [arrays], core_ids=[0])
    return tuple(r.results[0][f"out_{n}"] for n in OUTPUTS)
```

```python
from contextlib import ExitStack

import numpy as np

import concourse.bass as bass
from concourse import mybir

F32 = mybir.dt.float32
F32R = mybir.dt.float32r
U32 = mybir.dt.uint32
ALU = mybir.AluOpType
ACT = mybir.ActivationFunctionType
AX = mybir.AxisListType

P = 128
D = 1024
KD = D // P
TILES = 9
CTX_ROWS = 128
LAT = 1024
TOK = CTX_ROWS + LAT
CTX, LATENT = 0, 1
EPS = 1e-6
HALF = 512
HY_HID = 64
HY_EMB = 33
NFFT = 2 * LAT
HEADS = 32
HEAD = 64
INNER = 2 * D
GROUPS = 4
XBC_TILES = 24
Z_TILES = 16
EXPERTS = 16
CAP_LAT = 2 * LAT // EXPERTS
CAP_CTX = 2 * CTX_ROWS // EXPERTS
SLOTS = CAP_LAT + CAP_CTX
GAPPED = TOK + 2
LAT_AT = CTX_ROWS + 2
THIRD = TOK // 3
V_G1, V_A2, V_B2, V_G2 = range(4)


def product3(pe, out, w, w_at, h, h_k):
    for k in range(KD):
        for a, b in ((0, 0), (0, 1), (1, 0)):
            for piece in range(3):
                ins = pe.matmul(out(piece), w_at(w[a], k), h_k(h[b], k, piece),
                                start=(k == 0 and a == 0 and b == 0), stop=(k == KD - 1 and a == 1))
    return ins


def third(h, k, piece):
    return h[:, k, piece * THIRD:(piece + 1) * THIRD]


class Chain:

    def __init__(self, eng, sem, base=0):
        self.eng, self.sem, self.base, self.n = eng, sem, base, 0

    def step(self, ins):
        ins.then_inc(self.sem, 1)
        self.n += 1
        return self.base + self.n

    def link(self, ins):
        self.eng.wait_ge(self.sem, self.step(ins))


class Mem:

    def __init__(self, nc, ctx, prefix=""):
        self.nc, self.ctx, self.prefix, self.sems = nc, ctx, prefix, []
        ctx.callback(self.clear)

    def clear(self):
        self.nc.clear_and_free_semaphores(self.sems)
        self.nc.all_engine_barrier()

    def sb(self, name, shape, dt=F32):
        return self.ctx.enter_context(self.nc.sbuf_tensor(self.prefix + name, shape, dt))

    def psum(self, name="banks"):
        return self.ctx.enter_context(self.nc.psum_tensor(self.prefix + name, [P, 8, HALF], F32))

    def sem(self, name):
        self.sems.append(self.nc.alloc_semaphore(name=self.prefix + name))
        return self.sems[-1]


def phase_modulation(nc, io, keep):
    ada = io["ada_w"].rearrange("l (k p) n -> p l k n", p=P)
    RING = 3
    COLUMNS = 6 * D // HALF
    with ExitStack() as ctx:
        m = Mem(nc, ctx, "mod_")
        cond_rows = m.sb("cond_rows", [16, P])
        cond_t = m.sb("cond_t", [P, KD, 2])
        w = m.sb("w", [P, RING, KD, HALF])
        bias = m.sb("bias", [2, 2 * 6 * D])
        rows = m.sb("rows", [2, 2 * 6 * D])
        a_rows = m.sb("a_rows", [2, 2, D])
        gains = m.sb("gains", [2, 2, D])
        mrows = m.sb("mrows", [96, 2, P])
        stage = m.sb("stage", [P, 4, P])
        filt = Filter(m, io, keep["filt"])
        pb = m.psum()
        s_c = m.sem("cond_in")
        s_stage = m.sem("stage_in")
        s_bias = m.sem("bias_in")
        s_w = [m.sem(f"w_in{i}") for i in range(RING)]
        s_ct = m.sem("cond_transposed")
        s_silu = m.sem("cond_ready")
        s_acc = m.sem("piece_summed")
        s_row = m.sem("piece_in_rows")
        s_dve = m.sem("dve")
        s_arow = m.sem("a_rows_ready")
        s_out = m.sem("rows_in_dram")
        s_back = m.sem("rows_back")
        s_tr = m.sem("param_transposed")
        s_done = m.sem("params_kept")
        mod_dram = io["mod_dram"]
        vec_dram = io["vec_dram"]

        with nc.Block() as block:

            @block.sync
            def _(sp):
                sp.dma_start(cond_rows[0:8, :], io["c_ctx"].rearrange("(k p) -> k p", p=P)).then_inc(s_c, 16)
                sp.dma_start(cond_rows[8:16, :], io["c"][0].rearrange("(k p) -> k p", p=P)).then_inc(s_c, 16)
                filt.load(sp)
                for r in range(RING):
                    sp.dma_start(w[:, r, :, :], ada[:, 0, :, r * HALF:(r + 1) * HALF]).then_inc(s_w[r], 16)
                for layer in range(2):
                    with sp.Fori(0 if layer else 1, COLUMNS // RING) as i:
                        for r in range(RING):
                            sp.wait_ge(s_acc, i * RING + (layer * COLUMNS + r - RING + 1))
                            sp.dma_start(w[:, r, :, :], ada[:, layer, :, bass.ds((i * RING + r) * HALF, HALF)]
                                         ).then_inc(s_w[r], 16)
                sp.wait_ge(s_row, 2 * COLUMNS)
                sp.dma_start(mod_dram, rows[:, :]).then_inc(s_out, 16)
                sp.wait_ge(s_arow, 2)
                for layer in range(2):
                    for which, src in ((V_G1, 2), (V_B2, 3), (V_G2, 5)):
                        sp.dma_start(vec_dram[layer, :, which, :],
                                     rows[:, (layer * 6 + src) * D:(layer * 6 + src + 1) * D]).then_inc(s_out, 16)
                    sp.dma_start(vec_dram[layer, :, V_A2, :], a_rows[:, layer, :]).then_inc(s_out, 16)
                sp.wait_ge(s_out, 16 * 9)
                for c in range(2):
                    sp.dma_start(mrows[:, c, :], mod_dram[c].rearrange("(r p) -> r p", p=P)).then_inc(s_back, 16)

            @block.scalar
            def _(act):
                for c in range(2):
                    act.dma_start(bias[c:c + 1, :], io["ada_b"].rearrange("(a l) n -> a (l n)", a=1)).then_inc(s_bias, 16)
                    act.dma_start(gains[c:c + 1, :, :], io["norm_g"][:, 1, :].rearrange("(a l) d -> a l d", a=1)
                                  ).then_inc(s_bias, 16)
                for n, (src, at, cnt) in enumerate(keep["param_rows"]):
                    act.dma_start(stage[at[1]:at[1] + cnt, at[0], :], src).then_inc(s_stage, 16)
                for h in range(2):
                    act.dma_start(keep["d_skip"][h * HEAD:(h + 1) * HEAD, :],
                                  bass.AP(io["ssd_D"].tensor, h, [[0, HEAD], [2, Z_TILES]]),
                                  allow_slow_non_contiguous=True).then_inc(s_stage, 16)
                act.wait_ge(s_ct, 1)
                for c in range(2):
                    act.activation(cond_t[:, :, c], pb[:, 0, 8 * c:8 * c + 8], ACT.Silu).then_inc(s_silu, 1)
                filt.sine(act, 0)
                filt.sine(act, 1)

            @block.tensor
            def _(pe):
                pe.wait_ge(keep["s_const"], 16)
                pe.wait_ge(s_c, 32)
                pe.transpose(pb[:, 0, 0:16], cond_rows[:, :], keep["ident"][0:16, 0:16]).then_inc(s_ct, 1)
                pe.wait_ge(s_silu, 2)
                for layer in range(2):
                    filt.products(pe, pb, layer)
                    with pe.Fori(0, COLUMNS // RING) as i:
                        for r in range(RING):
                            pe.wait_ge(s_w[r], (i + (layer * COLUMNS // RING + 1)) * 16)
                            pe.wait_ge(s_row, i * RING + (COLUMNS + r - RING + 1 if layer else 0))
                            for k in range(KD):
                                ins = pe.matmul(pb[0:2, 1 + r, :], cond_t[:, k, :], w[:, r, k, :],
                                                start=(k == 0), stop=(k == KD - 1))
                            ins.then_inc(s_acc, 1)
                pe.wait_ge(filt.s_arg, 2)
                pe.wait_ge(s_stage, 16 * (len(keep["param_rows"]) + 2))
                for n, cnt in enumerate(keep["param_counts"]):
                    pe.transpose(pb[:, 4 + n // 4, (n % 4) * P:(n % 4) * P + cnt], stage[0:cnt, n, :],
                                 keep["ident"][0:cnt, 0:cnt]).then_inc(s_tr, 1)
                pe.wait_ge(s_back, 32)
                for c in range(2):
                    pe.transpose(pb[:, 6, c * P:c * P + 96], mrows[:, c, :], keep["ident"][0:96, 0:96]).then_inc(s_tr, 1)

            @block.vector
            def _(dve):
                ch = Chain(dve, s_dve)
                ch.link(dve.memset(keep["eps"][:, :], EPS))
                dve.wait_ge(s_bias, 64)
                for layer in range(2):
                    filt.angles(dve, pb, layer)
                    with dve.Fori(0, COLUMNS // RING) as i:
                        for r in range(RING):
                            dve.wait_ge(s_acc, i * RING + (layer * COLUMNS + r + 1))
                            at = bass.ds((i * RING + (layer * COLUMNS + r)) * HALF, HALF)
                            dve.tensor_tensor(rows[:, at], pb[0:2, 1 + r, :], bias[:, at], ALU.add).then_inc(s_row, 1)
                dve.wait_ge(s_row, 2 * COLUMNS)
                for layer in range(2):
                    dve.scalar_tensor_tensor(a_rows[:, layer, :], rows[:, (layer * 6 + 4) * D:(layer * 6 + 5) * D],
                                             1.0, gains[:, layer, :], ALU.add, ALU.mult).then_inc(s_arow, 1)
                dve.wait_ge(s_tr, 6)
                for n, cnt in enumerate(keep["param_counts"]):
                    dve.tensor_copy(keep["prm"][:, n, 0:cnt], pb[:, 4 + n // 4, (n % 4) * P:(n % 4) * P + cnt]
                                    ).then_inc(s_done, 1)
                for c in range(2):
                    dve.tensor_copy(keep["mod"][:, c, :], pb[:, 6, c * P:c * P + 96]).then_inc(s_done, 1)
                dve.wait_ge(s_done, 6)
                for layer in range(2):
                    for c in range(2):
                        ch.link(dve.scalar_tensor_tensor(
                            keep["gain1"][:, layer, c, :], keep["mod"][:, c, layer * 48 + 8:layer * 48 + 16], 1.0,
                            keep["prm"][:, 3, layer * 8:layer * 8 + 8], ALU.add, ALU.mult))


def phase_norm(nc, io, keep, layer):
    x_rows = io["x_dram"].rearrange("(t p) d -> t p d", p=P)
    with ExitStack() as ctx:
        m = Mem(nc, ctx, f"norm{layer}_")
        xr = m.sb("x", [P, 2, D])
        pos = m.sb("pos", [P, 2, D])
        xn = m.sb("xn", [P, 2, D])
        junk = m.sb("junk", [P, D])
        hf = m.sb("h", [P, 2, KD, P])
        st = m.sb("stats", [P, 2, 3])
        pb = m.psum()
        s_x = [m.sem(f"x_in{b}") for b in range(2)]
        s_pos = [m.sem(f"pos_in{b}") for b in range(2)]
        s_add = m.sem("x_added")
        s_st = [m.sem(f"x_stored{b}") for b in range(2)]
        s_sq = m.sem("squared")
        s_rt = m.sem("root")
        s_rc = m.sem("reciprocal")
        s_xn = m.sem("scaled")
        s_tr = m.sem("transposed")
        s_ea = m.sem("evicted_act")
        s_ed = m.sem("evicted_dve")
        s_hi = m.sem("leading_ready")
        s_lo = m.sem("trailing_ready")
        h_hi, h_lo = keep["hT"]

        def src(t):
            if layer:
                return x_rows[t]
            return io["x_prompt"][0] if t == 0 else io["x_sample"][0, (t - 1) * P:t * P, :]

        def args(t, k):
            c = CTX if t == 0 else LATENT
            return keep["gain1"][:, layer, c, k:k + 1], keep["mod"][:, c, layer * 48 + k:layer * 48 + k + 1]

        with nc.Block() as block:

            @block.sync
            def _(sp):
                for t in range(TILES):
                    b, u = t % 2, t // 2
                    if t >= 2:
                        sp.wait_ge(s_xn, t - 1)
                        if not layer:
                            sp.wait_ge(s_st[b], 16 * u)
                    sp.dma_start(xr[:, b, :], src(t)).then_inc(s_x[b], 16)
                    if not layer and t:
                        sp.dma_start(pos[:, b, :], io["pos"][(t - 1) * P:t * P, :]).then_inc(s_pos[b], 16)
                if not layer:
                    for b in range(2):
                        sp.wait_ge(s_st[b], 16 * (5 - b))

            @block.gpsimd
            def _(pool):
                if not layer:
                    for t in range(TILES):
                        pool.wait_ge(s_x[0], 16) if t == 0 else pool.wait_ge(s_add, t)
                        pool.dma_start(x_rows[t], xr[:, t % 2, :]).then_inc(s_st[t % 2], 16)

            @block.scalar
            def _(act):
                def tile_stats(t):
                    b = t % 2
                    if layer or t == 0:
                        act.wait_ge(s_x[b], 16 * (t // 2 + 1))
                    else:
                        act.wait_ge(s_add, t)
                    if t:
                        act.wait_ge(s_sq, t)
                    if t >= 2:
                        act.wait_ge(s_rc, t - 1)
                    act.activation(junk[:, :], xr[:, b, :], ACT.Square, accum_out=st[:, b, 0:1]).then_inc(s_sq, 1)
                    act.wait_ge(s_sq, t + 1)
                    act.activation(st[:, b, 1:2], st[:, b, 0:1], ACT.Sqrt, bias=keep["eps"][:, 0:1], scale=1.0 / D
                                   ).then_inc(s_rt, 1)

                def tile_evict(t):
                    act.wait_ge(s_tr, t + 1)
                    if t >= 2:
                        act.wait_ge(s_lo, t - 1)
                    for k in range(0, 4):
                        gain, shift = args(t, k)
                        act.activation(hf[:, t % 2, k, :], pb[:, 2 * (t % 2) + k // 4, (k % 4) * P:(k % 4 + 1) * P],
                                       ACT.Identity, bias=shift, scale=gain).then_inc(s_ea, 1)

                def tile_lead(t):
                    act.wait_ge(s_ea, 4 * t + 4)
                    act.wait_ge(s_ed, 4 * t + 4)
                    act.activation(h_hi[:, :, t * P:(t + 1) * P], hf[:, t % 2, :, :], ACT.Copy).then_inc(s_hi, 1)

                for t in range(TILES + 2):
                    if t < TILES:
                        tile_stats(t)
                    if 1 <= t <= TILES:
                        tile_evict(t - 1)
                    if t >= 2:
                        tile_lead(t - 2)

            @block.tensor
            def _(pe):
                for t in range(TILES):
                    pe.wait_ge(s_xn, t + 1)
                    if t >= 2:
                        pe.wait_ge(s_ea, 4 * (t - 1))
                        pe.wait_ge(s_ed, 4 * (t - 1))
                    for k in range(KD):
                        ins = pe.transpose(pb[:, 2 * (t % 2) + k // 4, (k % 4) * P:(k % 4 + 1) * P],
                                           xn[:, t % 2, k * P:(k + 1) * P], keep["ident"][:, :])
                    ins.then_inc(s_tr, 1)

            @block.vector
            def _(dve):
                def tile_scale(t):
                    b = t % 2
                    if not layer and t:
                        dve.wait_ge(s_x[b], 16 * (t // 2 + 1))
                        dve.wait_ge(s_pos[b], 16 * ((t + 1) // 2))
                        dve.tensor_tensor(xr[:, b, :], xr[:, b, :], pos[:, b, :], ALU.add).then_inc(s_add, 1)
                    dve.wait_ge(s_rt, t + 1)
                    dve.reciprocal(st[:, b, 2:3], st[:, b, 1:2]).then_inc(s_rc, 1)
                    dve.wait_ge(s_rc, t + 1)
                    if t >= 2:
                        dve.wait_ge(s_tr, t - 1)
                    dve.tensor_scalar(xn[:, b, :], xr[:, b, :], st[:, b, 2:3], None, ALU.mult).then_inc(s_xn, 1)

                def tile_evict(t):
                    dve.wait_ge(s_tr, t + 1)
                    if t >= 2:
                        dve.wait_ge(s_lo, t - 1)
                    for k in range(4, KD):
                        gain, shift = args(t, k)
                        dve.tensor_scalar(hf[:, t % 2, k, :], pb[:, 2 * (t % 2) + k // 4, (k % 4) * P:(k % 4 + 1) * P],
                                          gain, shift, ALU.mult, ALU.add).then_inc(s_ed, 1)

                def tile_rest(t):
                    dve.wait_ge(s_hi, t + 1)
                    dve.tensor_tensor(h_lo[:, :, t * P:(t + 1) * P], hf[:, t % 2, :, :],
                                      h_hi[:, :, t * P:(t + 1) * P].bitcast(F32), ALU.subtract).then_inc(s_lo, 1)

                for t in range(TILES + 3):
                    if t < TILES:
                        tile_scale(t)
                    if t >= 3:
                        tile_rest(t - 3)
                    if 1 <= t <= TILES:
                        tile_evict(t - 1)


def phase_hyena_in(nc, io, keep):
    win = io["hy_in_w"][0].rearrange("(k p) (s j c) -> p k s j c", p=P, s=3, c=P)
    PARTS = (1, 2, 0)
    with ExitStack() as ctx:
        m = Mem(nc, ctx, "hyin_")
        w = m.sb("w", [P, 2, KD, 3, P])
        split = m.sb("w_split", [P, 2, 2, KD, P], F32R)
        pad = m.sb("pad", [P, 2, GAPPED + 2])
        mid = m.sb("mid", [P, 2, GAPPED])
        out = m.sb("out", [P, 3, GAPPED])
        u = m.sb("u", [P, 2, GAPPED])
        u_rows = m.sb("u_rows", [P, 2, TILES, P])
        pb = m.psum()
        s_w = [m.sem(f"w_in{b}") for b in range(2)]
        s_hi = m.sem("w_leading")
        s_lo = m.sem("w_trailing")
        s_mm = m.sem("projected")
        s_zero = m.sem("pads_zero")
        s_ev = m.sem("padded")
        s_mid = m.sem("mid_tap")
        s_cv = m.sem("convolved")
        s_dve = m.sem("dve")
        s_u = m.sem("u_ready")
        s_tr = m.sem("u_transposed")
        s_ur = m.sem("u_rows_ready")
        s_x0 = [m.sem(f"x0_stored{b}") for b in range(2)]
        s_us = [m.sem(f"u_stored{b}") for b in range(2)]
        prm = keep["prm"]
        x0_dram, u_dram = io["x0_dram"], io["u_dram"]

        def bank(b, n):
            return 3 * ((b + n) % 2)

        with nc.Block() as block:

            @block.sync
            def _(sp):
                for b in range(2):
                    for part in PARTS:
                        sp.dma_start(w[:, b, :, part, :], win[:, :, part, b, :]).then_inc(s_w[b], 16)
                with sp.Fori(1, 4) as i:
                    for b in range(2):
                        sp.wait_ge(s_lo, i * 6 - 3 * (1 - b))
                        for part in PARTS:
                            sp.dma_start(w[:, b, :, part, :], win[:, :, part, i * 2 + b, :]).then_inc(s_w[b], 16)

            @block.tensor
            def _(pe):
                def project(b, i):
                    for n in range(3):
                        q = 3 * b + n
                        pe.wait_ge(s_lo, i * 6 + (q + 1))
                        pe.wait_ge(s_ev, i * 6 + max(q - 1, 0))
                        product3(pe, lambda piece: pb[:, bank(b, n) + piece, 0:THIRD],
                                 (split[:, q % 2, 0, :, :], split[:, q % 2, 1, :, :]), lambda w_, k: w_[:, k, :],
                                 keep["hT"], third).then_inc(s_mm, 1)

                def turn(b, i):
                    pe.wait_ge(s_u, i * 2 + (b + 1))
                    for go, tiles in enumerate(((0, 4), (4, 8), (8, 9))):
                        pe.wait_ge(s_ur, i * 6 + (3 * b + (0 if go < 2 else 1)))
                        for t in range(*tiles):
                            at = t * P + (2 if t else 0)
                            ins = pe.transpose(pb[:, 6 + go % 2, (t % 4) * P:(t % 4 + 1) * P], u[:, b, at:at + P],
                                               keep["ident"][:, :])
                        ins.then_inc(s_tr, 1)

                with pe.Fori(0, 4) as i:
                    project(0, i)
                    project(1, i)
                    turn(0, i)
                    turn(1, i)

            @block.scalar
            def _(act):
                def evict(b, n, i):
                    q = 3 * b + n
                    act.wait_ge(s_mm, i * 6 + (q + 1))
                    act.wait_ge(s_cv, i * 6 if q < 2 else i * 6 + (q - 1))
                    pd = q % 2
                    part = PARTS[n]
                    col = 72 + part * 8
                    bias = prm[:, 2, bass.ds(i * 2 + (col + b), 1)]
                    act.activation(pad[:, pd, 1:1 + CTX_ROWS], pb[:, bank(b, n), 0:CTX_ROWS], ACT.Identity, bias=bias)
                    act.activation(pad[:, pd, LAT_AT + 1:THIRD + 3], pb[:, bank(b, n), CTX_ROWS:THIRD], ACT.Identity, bias=bias)
                    act.activation(pad[:, pd, THIRD + 3:GAPPED + 1].rearrange("p (a c) -> p a c", c=THIRD),
                                   pb[:, bank(b, n) + 1:bank(b, n) + 3, 0:THIRD], ACT.Identity, bias=bias).then_inc(s_ev, 1)
                    act.wait_ge(s_ev, i * 6 + (q + 1))
                    act.activation(mid[:, pd, :], pad[:, pd, 1:1 + GAPPED], ACT.Identity,
                                   bias=prm[:, 2, bass.ds(i * 2 + (96 + part * 8 + b), 1)],
                                   scale=prm[:, 2, bass.ds(i * 2 + (24 + part * 8 + b), 1)]).then_inc(s_mid, 1)

                def lead(b, n, i, first=False):
                    q = 3 * b + n
                    if n == 0:
                        act.wait_ge(s_w[b], i * 48 + 48)
                    if not first:
                        act.wait_ge(s_lo, i * 6 + (q - 1))
                        act.wait_ge(s_mm, i * 6 + (q - 1))
                    act.activation(split[:, q % 2, 0, :, :], w[:, b, :, PARTS[n], :], ACT.Copy).then_inc(s_hi, 1)

                def evict_u(b, i):
                    for go, tiles in enumerate(((0, 4), (4, 8), (8, 9))):
                        act.wait_ge(s_tr, i * 6 + (3 * b + go + 1))
                        if go == 0:
                            act.wait_ge(s_us[b], i * 16)
                        act.activation(u_rows[:, b, tiles[0]:tiles[1], :],
                                       pb[:, 6 + go % 2, 0:(tiles[1] - tiles[0]) * P].rearrange("p (a c) -> p a c", c=P),
                                       ACT.Copy).then_inc(s_ur, 1)

                def tiles(i, last):
                    for q in range(6):
                        evict(q // 3, q % 3, i)
                        if q < 4:
                            lead((q + 2) // 3, (q + 2) % 3, i)
                        elif not last:
                            lead(0, q - 4, i + 1)
                    evict_u(0, i)
                    evict_u(1, i)

                lead(0, 0, 0, True)
                lead(0, 1, 0, True)
                act.wait_ge(s_zero, 6)
                with act.Fori(0, 3) as i:
                    tiles(i, False)
                tiles(3, True)

            @block.vector
            def _(dve):
                for b in range(2):
                    for at in (0, CTX_ROWS + 1, GAPPED + 1):
                        w_ = 2 if at == CTX_ROWS + 1 else 1
                        dve.memset(pad[:, b, at:at + w_], 0.0).then_inc(s_zero, 1)
                def rest(b, n, i):
                    q = 3 * b + n
                    dve.wait_ge(s_hi, i * 6 + (q + 1))
                    dve.tensor_tensor(split[:, q % 2, 1, :, :], w[:, b, :, PARTS[n], :],
                                      split[:, q % 2, 0, :, :].bitcast(F32), ALU.subtract).then_inc(s_lo, 1)

                rest(0, 0, 0)
                rest(0, 1, 0)

                def tiles(i, is_last):
                    ch = Chain(dve, s_dve, i * 6)
                    for b in range(2):
                        for n, part in enumerate(PARTS):
                            q = 3 * b + n
                            pd = q % 2
                            dve.wait_ge(s_mid, i * 6 + (q + 1))
                            first = prm[:, 2, bass.ds(i * 2 + (part * 8 + b), 1)]
                            last = prm[:, 2, bass.ds(i * 2 + (48 + part * 8 + b), 1)]
                            ch.link(dve.scalar_tensor_tensor(mid[:, pd, :], pad[:, pd, 0:GAPPED], first, mid[:, pd, :],
                                                             ALU.mult, ALU.add))
                            if n == 2:
                                if b == 0:
                                    dve.wait_ge(s_x0[1], i * 16)
                                else:
                                    dve.wait_ge(s_x0[0], i * 16 + 16)
                            dve.scalar_tensor_tensor(out[:, n, :], pad[:, pd, 2:2 + GAPPED], last, mid[:, pd, :],
                                                     ALU.mult, ALU.add).then_inc(s_cv, 1)
                            if n == 1:
                                dve.wait_ge(s_cv, i * 6 + (q + 1))
                                dve.wait_ge(s_tr, i * 6)
                                dve.tensor_tensor(u[:, b, :], out[:, 0, :], out[:, 1, :], ALU.mult).then_inc(s_u, 1)
                            if q < 4:
                                rest((q + 2) // 3, (q + 2) % 3, i)
                            elif not is_last:
                                rest(0, q - 4, i + 1)

                with dve.Fori(0, 3) as i:
                    tiles(i, False)
                tiles(3, True)

            @block.gpsimd
            def _(pool):
                with pool.Fori(0, 4) as i:
                    for b in range(2):
                        pool.wait_ge(s_cv, i * 6 + (3 * b + 3))
                        pool.dma_start(x0_dram[i * 2 + b], out[:, 2, :]).then_inc(s_x0[b], 16)
                    for b in range(2):
                        pool.wait_ge(s_ur, i * 6 + 3 * (b + 1))
                        pool.dma_start(u_dram[:, :, bass.ds((i * 2 + b) * P, P)], u_rows[:, b, :, :]).then_inc(s_us[b], 16)
                for b in range(2):
                    pool.wait_ge(s_x0[b], 64)
                    pool.wait_ge(s_us[b], 64)


TAPS = 2 * LAT + 2 * CTX_ROWS
TAP_TILES = TAPS // P
ROUND = 1.5 * 2.0 ** 23
TWO_PI_HI = 6.28125
TWO_PI_LO = float(2 * np.pi - 6.28125)
PI_IN = 3.1415925


class Filter:
    BANKS = (4, 5, 6, 7, 0)
    pieces = [(a, min(HALF, TAPS - a)) for a in range(0, TAPS, HALF)]

    def __init__(self, m, io, filt):
        self.io, self.filt = io, filt
        self.z = m.sb("tap_clock", [HY_EMB, TAPS])
        self.w1 = m.sb("f_w1", [HY_EMB, HY_HID])
        self.w2 = m.sb("f_w2", [HY_HID, HY_HID])
        self.col = m.sb("f_columns", [HY_HID, 5])
        self.arg = m.sb("angle", [HY_HID, TAPS])
        self.turns = m.sb("turns", [HY_HID, TAPS])
        self.h1 = self.turns
        self.s_in = m.sem("filter_in")
        self.s_mm = m.sem("filter_layer")
        self.s_dve = m.sem("filter_dve")
        self.s_arg = m.sem("angle_ready")
        self.s_sin = m.sem("sine_ready")

    def load(self, eng):
        io, s_in = self.io, self.s_in
        eng.dma_start(self.z[:, :], io["zfeat"]).then_inc(s_in, 16)
        eng.dma_start(self.w1[:, :], io["hy_f_w1"][0]).then_inc(s_in, 16)
        eng.dma_start(self.w2[:, :], io["hy_f_w2"][0]).then_inc(s_in, 16)
        for n, name in enumerate(("hy_f_b1", "hy_f_b2", "hy_f_freq")):
            eng.dma_start(self.col[:, n:n + 1], io[name].rearrange("a h -> h a")).then_inc(s_in, 16)

    def products(self, pe, pb, layer):
        w, src = ((self.w1, self.z), (self.w2, self.h1))[layer]
        pe.wait_ge(self.s_in, 96)
        if layer:
            pe.wait_ge(self.s_sin, 1)
        for n, (at, width) in enumerate(self.pieces):
            pe.matmul(pb[0:HY_HID, self.BANKS[n], 0:width], w[:, :], src[:, at:at + width], start=True, stop=True
                      ).then_inc(self.s_mm, 1)

    def sine(self, act, layer):
        act.wait_ge(self.s_arg, layer + 1)
        act.activation((self.h1, self.filt)[layer][0:HY_HID, :], self.arg[:, :], ACT.Sin).then_inc(self.s_sin, 1)

    def angles(self, dve, pb, layer):
        ch = Chain(dve, self.s_dve, layer * (2 + len(self.pieces) + 4))
        arg, turns, col = self.arg, self.turns, self.col
        if layer == 0:
            dve.wait_ge(self.s_in, 96)
            for n in range(2):
                ch.link(dve.tensor_tensor(col[:, 3 + n:4 + n], col[:, n:n + 1], col[:, 2:3], ALU.mult))
        else:
            dve.wait_ge(self.s_sin, 1)
        for n, (at, width) in enumerate(self.pieces):
            dve.wait_ge(self.s_mm, layer * len(self.pieces) + n + 1)
            last = ch.step(dve.tensor_scalar(arg[:, at:at + width], pb[0:HY_HID, self.BANKS[n], 0:width], col[:, 2:3],
                                             col[:, 3 + layer:4 + layer], ALU.mult, ALU.add))
        dve.wait_ge(self.s_dve, last)
        ch.link(dve.tensor_scalar(turns[:, :], arg[:, :], 1 / (2 * np.pi), ROUND, ALU.mult, ALU.add))
        ch.link(dve.tensor_scalar(turns[:, :], turns[:, :], ROUND, None, ALU.subtract))
        ch.link(dve.scalar_tensor_tensor(arg[:, :], turns[:, :], -TWO_PI_HI, arg[:, :], ALU.mult, ALU.add))
        ch.link(dve.scalar_tensor_tensor(arg[:, :], turns[:, :], -TWO_PI_LO, arg[:, :], ALU.mult, ALU.add))
        dve.tensor_scalar(arg[:, :], arg[:, :], PI_IN, -PI_IN, ALU.min, ALU.max).then_inc(self.s_arg, 1)


SQ = float(np.sqrt(0.5))
RE, IM = 0, 1
BLOCKS = 9
CTX_BLOCK = 8
ORDER = (CTX_BLOCK, 0, 1, 2, 3, 4, 5, 6, 7)
EVEN_R = 5
CT_HALF = HALF // P


def phase_long_conv(nc, io, keep):
    FW = 2 * 256 + 9 * 256
    with ExitStack() as ctx:
        m = Mem(nc, ctx, "conv_")
        fwd = m.sb("fwd", [P, 2, FW])
        inv04 = m.sb("inv04", [P, 2, 2, 256])
        inv = m.sb("inv", [P, 3, 4, HALF])
        negt = m.sb("negt", [P, TAP_TILES])
        delta = m.sb("delta", [P, HALF])
        w3 = m.sb("w3", [HY_HID, 2, HALF])
        fbias = m.sb("fbias", [1, HALF])
        win = m.sb("window", [P, 2, HALF])
        ut = m.sb("u", [P, TILES, HALF])
        taps = m.sb("taps", [P, 2 * BLOCKS, HALF])
        z = m.sb("z", [P, 8, 2, HALF])
        tmp = m.sb("tmp", [P, 4, HALF])
        kf = m.sb("kf", [P, BLOCKS, 2, HALF])
        zflat = z[:, :, :, :].rearrange("p a b c -> p (a b c)")
        vs = [zflat[:, b * 2048:(b + 1) * 2048] for b in range(2)]
        yt = zflat[:, 4096:6144].rearrange("p (a c) -> p a c", c=256)
        gt = zflat[:, 6144:6144 + TOK]
        uflat = ut[:, :, :].rearrange("p a c -> p (a c)")
        x0 = [uflat[:, HALF + b * GAPPED:HALF + (b + 1) * GAPPED] for b in range(2)]
        yf = taps[:, :, :].rearrange("p (b c) n -> p b c n", c=2)
        pb = m.psum()
        s_negt = m.sem("times_in")
        s_fwd = m.sem("forward_in")
        s_inv = m.sem("inverse_in")
        s_half = m.sem("filter_half_in")
        s_u = m.sem("u_in")
        s_win = m.sem("window_ready")
        s_kp = m.sem("taps_projected")
        s_tap = m.sem("tap_windowed")
        s_dve = m.sem("dve")
        s_edge = m.sem("edge_taps_ready")
        s_zk = m.sem("filter_sums")
        s_kd = m.sem("filter_block")
        s_ke = m.sem("filter_kept")
        s_zu = m.sem("input_sums")
        s_ud = m.sem("input_block")
        s_pr = m.sem("product_ready")
        s_iv = m.sem("inverse_done")
        s_ve = m.sem("inverse_kept")
        s_x0 = [m.sem(f"x0_in{b}") for b in range(2)]
        s_g = m.sem("g_ready")
        s_gs = m.sem("g_stored")
        filt = keep["filt"]
        DVE_STEPS = 19 + 9 + BLOCKS * 5 + 4 + CT_HALF * 15

        def fcol(group, part, half=0):
            if group < 2:
                return group * 256 + part * 128
            return 512 + (group - 2) * 768 + part * 256 + half * 128

        with nc.Block() as block:

            @block.sync
            def _(sp):
                def filter_half(h):
                    at = slice(h * HALF, (h + 1) * HALF)
                    sp.dma_start(delta[:, :], io["deltas"][:, at].partition_broadcast(P)).then_inc(s_half, 16)
                    for back in range(2):
                        sp.dma_start(w3[:, back, :], io["hy_f_w3"][0][:, back * D + h * HALF:back * D + (h + 1) * HALF]
                                     ).then_inc(s_half, 16)
                    sp.dma_start(fbias[:, :], io["hy_f_bias"][:, at]).then_inc(s_half, 16)

                sp.dma_start(negt[:, :], io["negt"]).then_inc(s_negt, 16)
                filter_half(0)
                sp.dma_start(fwd[:, :, :], io["fwd"].rearrange("p (a b) -> p a b", a=2)).then_inc(s_fwd, 16)
                for h in range(2):
                    if h:
                        sp.wait_ge(s_g, h * CT_HALF)
                    sp.dma_start(ut[:, :, :], io["u_dram"][:, :, h * HALF:(h + 1) * HALF]).then_inc(s_u, 16)
                    if h == 0:
                        sp.dma_start(inv04[:, :, :, :].rearrange("p a b c -> p (a b c)"), io["inv04"]).then_inc(s_inv, 16)
                        sp.dma_start(inv[:, :, :, :].rearrange("p a b c -> p (a b c)"), io["inv"]).then_inc(s_inv, 16)
                        sp.wait_ge(s_edge, 1)
                        filter_half(1)
                    sp.wait_ge(s_pr, h * BLOCKS + BLOCKS)
                    for ct in range(2):
                        sp.dma_start(x0[ct], io["x0_dram"][h * CT_HALF + ct]).then_inc(s_x0[ct], 16)
                    for ct in range(CT_HALF):
                        if ct >= 1 and ct + 1 < CT_HALF:
                            sp.wait_ge(s_g, h * CT_HALF + ct)
                            sp.dma_start(x0[(ct + 1) % 2], io["x0_dram"][h * CT_HALF + (ct + 1)]).then_inc(s_x0[(ct + 1) % 2], 16)
                        sp.wait_ge(s_g, h * CT_HALF + (ct + 1))
                        sp.dma_start(io["g_dram"][h * CT_HALF + ct], gt).then_inc(s_gs, 16)
                sp.wait_ge(s_gs, 16 * 2 * CT_HALF)

            @block.tensor
            def _(pe):
                def transform(source, ctx_source, counter, emptied, sums, h):
                    for at, blk in enumerate(ORDER):
                        lo = 2 + 2 * (at % 2)
                        if at >= 2:
                            pe.wait_ge(emptied, h * BLOCKS + (at - 1))
                        if at in (1, 3, 5):
                            pe.wait_ge(sums, h * 3 + (at + 1) // 2)
                        for part in (RE, IM):
                            if blk in (0, 1, CTX_BLOCK):
                                group = 0 if blk == CTX_BLOCK else blk
                                terms = [(fwd[:, c, fcol(group, part):fcol(group, part) + P],
                                          source(group, c) if blk != CTX_BLOCK else ctx_source(c)) for c in range(2)]
                                terms = [t for t in terms if t[1] is not None]
                            else:
                                group, half = 2 + (blk - 2) // 2, blk % 2
                                own, other = (0, 1) if part == RE else (1, 0)
                                terms = [(fwd[:, c, fcol(group, 0, half):fcol(group, 0, half) + P],
                                          source(2 * (group - 1) + own, c)) for c in range(2)]
                                terms += [(fwd[:, c, fcol(group, 1 + part, half):fcol(group, 1 + part, half) + P],
                                           source(2 * (group - 1) + other, c)) for c in range(2)]
                            for n, (a, b) in enumerate(terms):
                                ins = pe.matmul(pb[:, lo + part, :], a, b, start=(n == 0), stop=(n == len(terms) - 1))
                        ins.then_inc(counter, 1)

                with pe.Fori(0, 2) as h:
                    pe.wait_ge(s_half, h * 64 + 64)
                    pe.wait_ge(s_ve, h * CT_HALF)
                    for tt in range(TAP_TILES):
                        back = 1 if tt in range(8, 16) or tt == 17 else 0
                        if tt >= 2:
                            pe.wait_ge(s_tap, h * TAP_TILES + (tt - 1))
                        pe.matmul(pb[:, tt % 2, :], filt[0:HY_HID, tt * P:(tt + 1) * P], w3[:, back, :],
                                  start=True, stop=True).then_inc(s_kp, 1)
                    pe.wait_ge(s_edge, h + 1)
                    pe.wait_ge(s_fwd, 16)
                    transform(lambda s, c: z[:, s, c, :], lambda c: taps[:, 16 + c, :], s_kd, s_ke, s_zk, h)
                    pe.wait_ge(s_ke, h * BLOCKS + BLOCKS)
                    pe.wait_ge(s_u, h * 16 + 16)
                    transform(lambda s, c: z[:, s, c, :], lambda c: ut[:, 0, :] if c == 0 else None, s_ud, s_pr, s_zu, h)
                    pe.wait_ge(s_pr, h * BLOCKS + BLOCKS)
                    pe.wait_ge(s_inv, 32)
                    for ct in range(CT_HALF):
                        base = 3 * (ct % 2)
                        chan = slice(ct * P, (ct + 1) * P)
                        if ct >= 2:
                            pe.wait_ge(s_ve, h * CT_HALF + (ct - 1))
                        for g in range(3):
                            for c in range(4):
                                pe.matmul(pb[:, base + g, :], yf[:, 2 + 2 * g + c % 2, c // 2, chan], inv[:, g, c, :],
                                          start=(c == 0), stop=(c == 3))
                        if ct >= 1:
                            pe.wait_ge(s_ve, h * CT_HALF + ct)
                            pe.wait_ge(s_g, h * CT_HALF + ct)
                        for g in range(2):
                            for c in range(2):
                                pe.matmul(pb[:, 6, g * 256:(g + 1) * 256], yf[:, g, c, chan], inv04[:, g, c, :],
                                          start=(c == 0), stop=(c == 1))
                        for c in range(2):
                            ins = pe.matmul(pb[:, 7, 0:P], yf[:, CTX_BLOCK, c, chan], inv04[:, 0, c, 0:P],
                                            start=(c == 0), stop=(c == 1))
                        ins.then_inc(s_iv, 1)

            @block.scalar
            def _(act):
                act.wait_ge(s_negt, 16)
                with act.Fori(0, 2) as h:
                    act.wait_ge(s_half, h * 64 + 64)
                    for tt in range(TAP_TILES):
                        if tt >= 2:
                            act.wait_ge(s_tap, h * TAP_TILES + (tt - 1))
                        act.activation(win[:, tt % 2, :], delta[:, :], ACT.Exp, scale=negt[:, tt:tt + 1]).then_inc(s_win, 1)
                    for at, blk in enumerate(ORDER):
                        act.wait_ge(s_kd, h * BLOCKS + (at + 1))
                        act.activation(kf[:, blk, :, :], pb[:, 2 + 2 * (at % 2):4 + 2 * (at % 2), :], ACT.Copy
                                       ).then_inc(s_ke, 1)
                    for ct in range(CT_HALF):
                        act.wait_ge(s_iv, h * CT_HALF + (ct + 1))
                        if ct >= 2:
                            act.wait_ge(s_g, h * CT_HALF + (ct - 1))
                        v = vs[ct % 2]
                        act.activation(v[:, 0:3 * HALF].rearrange("p (a c) -> p a c", c=HALF),
                                       pb[:, 3 * (ct % 2):3 * (ct % 2) + 3, :], ACT.Copy)
                        act.activation(v[:, 3 * HALF:4 * HALF], pb[:, 6, :], ACT.Copy).then_inc(s_ve, 1)

            @block.vector
            def _(dve):
                tt_ = dve.tensor_tensor

                with dve.Fori(0, 2) as h:
                    ch = Chain(dve, s_dve, h * DVE_STEPS)
                    step, link = ch.step, ch.link

                    def done():
                        dve.wait_ge(s_dve, ch.base + ch.n)

                    dve.wait_ge(s_iv, h * CT_HALF)
                    for tt in range(TAP_TILES):
                        dve.wait_ge(s_win, h * TAP_TILES + (tt + 1))
                        dve.wait_ge(s_kp, h * TAP_TILES + (tt + 1))
                        tt_(taps[:, tt, :], pb[:, tt % 2, :], win[:, tt % 2, :], ALU.mult).then_inc(s_tap, 1)
                    dve.wait_ge(s_half, h * 64 + 64)
                    dve.wait_ge(s_tap, h * TAP_TILES + TAP_TILES)
                    for tt in (8, 17):
                        step(dve.memset(taps[0:1, tt, :], 0.0))
                    for tt in (0, 16):
                        step(tt_(taps[0:1, tt, :], taps[0:1, tt, :], fbias[:, :], ALU.add))
                    done()
                    dve.memset(tmp[0:1, 0, 0:1], 0.0).then_inc(s_edge, 1)

                    def q(n):
                        return taps[:, 2 * n:2 * n + 2, :]

                    def zz(n):
                        return z[:, n, :, :]
                    a, b = tmp[:, 0:2, :], tmp[:, 2:4, :]
                    stt = dve.scalar_tensor_tensor

                    dve.wait_ge(s_edge, h + 1)
                    dve.wait_ge(s_gs, h * 16 * CT_HALF)
                    for n in range(4):
                        step(tt_(zz(4 + n), q(n), q(n + 4), ALU.add))
                    done()
                    step(tt_(a, zz(4), zz(6), ALU.add))
                    step(tt_(b, zz(5), zz(7), ALU.add))
                    done()
                    step(tt_(zz(0), a, b, ALU.add))
                    tt_(zz(1), a, b, ALU.subtract).then_inc(s_zk, 1)
                    step(tt_(zz(2), zz(4), zz(6), ALU.subtract))
                    tt_(zz(3), zz(7), zz(5), ALU.subtract).then_inc(s_zk, 1)
                    for n in range(4):
                        step(tt_(q(n), q(n), q(n + 4), ALU.subtract))
                    done()
                    step(tt_(q(4), q(1), q(3), ALU.add))
                    step(tt_(q(5), q(3), q(1), ALU.subtract))
                    done()
                    step(stt(zz(4), q(5), -SQ, q(0), ALU.mult, ALU.add))
                    step(stt(zz(5), q(4), -SQ, q(2), ALU.mult, ALU.subtract))
                    step(stt(zz(6), q(5), SQ, q(0), ALU.mult, ALU.add))
                    stt(zz(7), q(4), -SQ, q(2), ALU.mult, ALU.add).then_inc(s_zk, 1)

                    def x(n):
                        return ut[:, 1 + 2 * n:3 + 2 * n, :]
                    dve.wait_ge(s_zk, h * 3 + 2)
                    dve.wait_ge(s_u, h * 16 + 16)
                    step(tt_(a, x(0), x(2), ALU.add))
                    step(tt_(b, x(1), x(3), ALU.add))
                    done()
                    dve.wait_ge(s_kd, h * BLOCKS + EVEN_R)
                    step(tt_(zz(0), a, b, ALU.add))
                    tt_(zz(1), a, b, ALU.subtract).then_inc(s_zu, 1)
                    step(tt_(zz(2), x(0), x(2), ALU.subtract))
                    tt_(zz(3), x(3), x(1), ALU.subtract).then_inc(s_zu, 1)
                    dve.wait_ge(s_zu, h * 3 + 2)
                    dve.wait_ge(s_kd, h * BLOCKS + BLOCKS)
                    step(stt(zz(4), zz(3), -SQ, x(0), ALU.mult, ALU.add))
                    step(stt(zz(6), zz(3), SQ, x(0), ALU.mult, ALU.add))
                    step(stt(zz(5), b, -SQ, x(2), ALU.mult, ALU.subtract))
                    stt(zz(7), b, -SQ, x(2), ALU.mult, ALU.add).then_inc(s_zu, 1)
                    dve.wait_ge(s_zu, h * 3 + 3)
                    done()

                    for at, blk in enumerate(ORDER):
                        lo = 2 + 2 * (at % 2)
                        dve.wait_ge(s_ke, h * BLOCKS + (at + 1))
                        dve.wait_ge(s_ud, h * BLOCKS + (at + 1))
                        done()
                        dve.wait_ge(s_pr, h * BLOCKS + at)
                        step(tt_(tmp[:, 0, :], pb[:, lo, :], kf[:, blk, RE, :], ALU.mult))
                        step(tt_(tmp[:, 2, :], pb[:, lo, :], kf[:, blk, IM, :], ALU.mult))
                        step(tt_(tmp[:, 3, :], pb[:, lo + 1, :], kf[:, blk, RE, :], ALU.mult))
                        step(tt_(tmp[:, 1, :], pb[:, lo + 1, :], kf[:, blk, IM, :], ALU.mult))
                        done()
                        step(tt_(yf[:, blk, RE, :], tmp[:, 0, :], tmp[:, 1, :], ALU.subtract))
                        if blk in (0, CTX_BLOCK):
                            step(tt_(yf[:, blk, IM, :], tmp[:, 2, :], tmp[:, 3, :], ALU.add))
                            done()
                            step(dve.tensor_copy(yf[0:1, blk, RE, :], tmp[0:1, 0, :]))
                            dve.tensor_copy(yf[0:1, blk, IM, :], tmp[0:1, 1, :]).then_inc(s_pr, 1)
                        else:
                            tt_(yf[:, blk, IM, :], tmp[:, 2, :], tmp[:, 3, :], ALU.add).then_inc(s_pr, 1)
                    done()
                    for ct in range(CT_HALF):
                        v = vs[ct % 2]
                        dve.wait_ge(s_ve, h * CT_HALF + (ct + 1))

                        def piece(n, k=1):
                            return v[:, n * 256:(n + k) * 256]

                        def t_(n, k=1):
                            return yt[:, n:n + k, :].rearrange("p a c -> p (a c)")
                        step(tt_(t_(0, 2), piece(2, 2), piece(4, 2), ALU.add))
                        step(tt_(t_(2, 2), piece(2, 2), piece(4, 2), ALU.subtract))
                        step(tt_(t_(4), piece(6), piece(7), ALU.add))
                        step(tt_(t_(5), piece(6), piece(7), ALU.subtract))
                        done()
                        step(tt_(t_(6), t_(4), piece(0), ALU.add))
                        step(tt_(t_(7), t_(4), piece(0), ALU.subtract))
                        done()
                        dve.wait_ge(s_gs, (h * CT_HALF + ct) * 16)
                        y = [gt[:, CTX_ROWS + n * 256:CTX_ROWS + (n + 1) * 256] for n in range(4)]
                        step(tt_(y[0], t_(6), t_(0), ALU.add))
                        step(tt_(y[2], t_(7), t_(3), ALU.subtract))
                        done()
                        step(tt_(t_(6), t_(2), t_(1), ALU.subtract))
                        step(tt_(t_(7), t_(2), t_(1), ALU.add))
                        step(tt_(t_(0), t_(5), piece(1), ALU.subtract))
                        step(tt_(t_(4), t_(5), piece(1), ALU.add))
                        done()
                        step(dve.scalar_tensor_tensor(y[1], t_(6), SQ, t_(0), ALU.mult, ALU.add))
                        step(dve.scalar_tensor_tensor(y[3], t_(7), -SQ, t_(4), ALU.mult, ALU.add))
                        done()
                        dve.wait_ge(s_x0[ct % 2], h * 32 + (ct // 2 + 1) * 16)
                        step(dve.scalar_tensor_tensor(gt[:, 0:CTX_ROWS], pb[:, 7, 0:P], float(NFFT // (2 * CTX_ROWS)),
                                                      x0[ct % 2][:, 0:CTX_ROWS], ALU.mult, ALU.mult))
                        tt_(gt[:, CTX_ROWS:TOK], gt[:, CTX_ROWS:TOK], x0[ct % 2][:, LAT_AT:LAT_AT + LAT], ALU.mult
                            ).then_inc(s_g, 1)
                    assert ch.n == DVE_STEPS, ch.n


def phase_hyena_out(nc, io, keep):
    x_rows = io["x_dram"].rearrange("(t p) d -> t p d", p=P)
    with ExitStack() as ctx:
        m = Mem(nc, ctx, "hyout_")
        g = m.sb("g", [P, KD, TOK])
        w = m.sb("w", [P, KD, D])
        gate = m.sb("gate", [P, 2, D])
        xr = m.sb("x", [P, 3, D])
        t1 = m.sb("t1", [P, 2, D])
        pb = m.psum()
        s_g = m.sem("g_in")
        s_w = m.sem("w_in")
        s_gate = m.sem("gate_in")
        s_x = [m.sem(f"x_in{b}") for b in range(3)]
        s_mm = m.sem("projected")
        s_t = m.sem("gated")
        s_sum = m.sem("summed")
        s_st = [m.sem(f"x_stored{b}") for b in range(3)]

        with nc.Block() as block:

            @block.sync
            def _(sp):
                sp.dma_start(g[:, :, :], io["g_dram"].rearrange("k p t -> p k t")).then_inc(s_g, 16)
                for c in range(2):
                    sp.dma_start(gate[:, c, :], io["vec_dram"][0, c, V_G1:V_G1 + 1, :].partition_broadcast(P)).then_inc(s_gate, 16)
                for t in range(TILES):
                    b = t % 3
                    if t >= 3:
                        sp.wait_ge(s_st[b], 16 * (t // 3))
                    sp.dma_start(xr[:, b, :], x_rows[t]).then_inc(s_x[b], 16)

            @block.scalar
            def _(act):
                act.dma_start(w[:, :, :], io["hy_out_w"][0].rearrange("(k p) n -> p k n", p=P)).then_inc(s_w, 16)
                for t in range(TILES):
                    act.wait_ge(s_sum, t + 1)
                    act.dma_start(x_rows[t], xr[:, t % 3, :]).then_inc(s_st[t % 3], 16)
                for b in range(3):
                    act.wait_ge(s_st[b], 48)

            @block.tensor
            def _(pe):
                pe.wait_ge(s_g, 16)
                pe.wait_ge(s_w, 16)
                for t in range(TILES):
                    if t >= 2:
                        pe.wait_ge(s_t, t - 1)
                    for half in range(2):
                        for k in range(KD):
                            ins = pe.matmul(pb[:, 2 * (t % 2) + half, :], g[:, k, t * P:(t + 1) * P],
                                            w[:, k, half * HALF:(half + 1) * HALF], start=(k == 0), stop=(k == KD - 1))
                    ins.then_inc(s_mm, 1)

            @block.vector
            def _(dve):
                dve.wait_ge(s_gate, 32)
                for t in range(TILES):
                    dve.wait_ge(s_mm, t + 1)
                    dve.tensor_tensor(t1[:, t % 2, :], pb[:, 2 * (t % 2):2 * (t % 2) + 2, :].rearrange("p a c -> p (a c)"),
                                      gate[:, CTX if t == 0 else LATENT, :], ALU.mult).then_inc(s_t, 1)
                    dve.wait_ge(s_x[t % 3], 16 * (t // 3 + 1))
                    dve.wait_ge(s_t, t + 1)
                    dve.tensor_tensor(xr[:, t % 3, :], xr[:, t % 3, :], t1[:, t % 2, :], ALU.add).then_inc(s_sum, 1)


PIECES = 6


def expert_piece(io, layer, j, expert):
    name, half = (("moe_w_gate", 0), ("moe_w_up", 0), ("moe_w_gate", 1), ("moe_w_up", 1),
                  ("moe_w_down", 0), ("moe_w_down", 1))[j]
    return io[name][layer].rearrange("e (k p) n -> p e k n", p=P)[:, expert, :, half * HALF:(half + 1) * HALF]


def phase_route(nc, io, keep, layer):
    x_rows = io["x_dram"].rearrange("(t p) d -> t p d", p=P)
    h_rows = io["h_dram"].rearrange("(t p) d -> t p d", p=P)
    with ExitStack() as ctx:
        m = Mem(nc, ctx, f"route{layer}_")
        xr = m.sb("x", [P, 2, D])
        hr = m.sb("h", [P, 2, D])
        junk = m.sb("junk", [P, D])
        ht = m.sb("ht", [P, 2, KD, P])
        vec = m.sb("vec", [P, 2, 2, D])
        wr = m.sb("router", [P, KD, EXPERTS])
        st = m.sb("stats", [P, 2, 8])
        ex = m.sb("ex", [P, 2, EXPERTS])
        aff = m.sb("aff", [P, 2, EXPERTS])
        cur = m.sb("cur", [EXPERTS, 2, TOK])
        vals = m.sb("vals", [EXPERTS, CAP_LAT + CAP_CTX])
        idx = m.sb("idx", [EXPERTS, CAP_LAT + CAP_CTX], U32)
        idxf = m.sb("idxf", [EXPERTS, CAP_LAT + CAP_CTX])
        pb = m.psum()
        s_vec = m.sem("vectors_in")
        s_x = [m.sem(f"x_in{b}") for b in range(2)]
        s_sq = m.sem("squared")
        s_rt = m.sem("root")
        s_dve = m.sem("dve")
        s_h = m.sem("h_ready")
        s_hs = [m.sem(f"h_stored{b}") for b in range(2)]
        s_tr = m.sem("h_transposed")
        s_ht = m.sem("ht_ready")
        s_lg = m.sem("logits")
        s_mx = m.sem("max_ready")
        s_ex = m.sem("exp_ready")
        s_af = m.sem("affinity")
        s_at = m.sem("affinity_transposed")
        s_ct = m.sem("affinity_kept")
        s_top = m.sem("slots_chosen")
        s_it = m.sem("slots_transposed")

        with nc.Block() as block:

            @block.sync
            def _(sp):
                sp.dma_start(wr[:, :, :], io["moe_router"][layer].rearrange("(k p) e -> p k e", p=P)).then_inc(s_vec, 16)
                for c in range(2):
                    for n, which in enumerate((V_A2, V_B2)):
                        sp.dma_start(vec[:, c, n, :], io["vec_dram"][layer, c, which:which + 1, :].partition_broadcast(P)
                                     ).then_inc(s_vec, 16)
                for t in range(TILES):
                    if t >= 2:
                        sp.wait_ge(s_h, t - 1)
                    sp.dma_start(xr[:, t % 2, :], x_rows[t]).then_inc(s_x[t % 2], 16)
                for j in range(PIECES):
                    sp.dma_start(keep["ring"][:, j, :, :], expert_piece(io, layer, j, 0)).then_inc(keep["s_ring"][j], 16)
                for b in range(2):
                    sp.wait_ge(s_hs[b], 16 * (5 - b))

            @block.gpsimd
            def _(pool):
                for t in range(TILES):
                    pool.wait_ge(s_h, t + 1)
                    pool.dma_start(h_rows[t], hr[:, t % 2, :]).then_inc(s_hs[t % 2], 16)

            @block.scalar
            def _(act):
                def stats(t):
                    b = t % 2
                    act.wait_ge(s_x[b], 16 * (t // 2 + 1))
                    if t:
                        act.wait_ge(s_sq, t)
                    if t >= 2:
                        act.wait_ge(s_h, t - 1)
                    act.activation(junk[:, :], xr[:, b, :], ACT.Square, accum_out=st[:, b, 0:1]).then_inc(s_sq, 1)
                    act.wait_ge(s_sq, t + 1)
                    act.activation(st[:, b, 1:2], st[:, b, 0:1], ACT.Sqrt, bias=keep["eps"][:, 0:1], scale=1.0 / D
                                   ).then_inc(s_rt, 1)

                def turned(t):
                    act.wait_ge(s_tr, t + 1)
                    if t >= 2:
                        act.wait_ge(s_lg, t - 1)
                    act.activation(ht[:, t % 2, :, :].rearrange("p (a k) c -> p a (k c)", a=2),
                                   pb[:, 2 * (t % 2):2 * (t % 2) + 2, :], ACT.Copy).then_inc(s_ht, 1)

                def exps(t):
                    b = t % 2
                    act.wait_ge(s_mx, t + 1)
                    act.activation(ex[:, b, :], pb[:, 4 + b, 0:EXPERTS], ACT.Exp, bias=st[:, b, 3:4],
                                   accum_out=st[:, b, 4:5]).then_inc(s_ex, 1)

                stats(0)
                for t in range(TILES + 2):
                    if t + 1 < TILES:
                        stats(t + 1)
                    if 1 <= t <= TILES:
                        turned(t - 1)
                    if t >= 2:
                        exps(t - 2)

            @block.tensor
            def _(pe):
                pe.wait_ge(s_vec, 80)

                def logits(t):
                    b = t % 2
                    pe.wait_ge(s_ht, t + 1)
                    if t >= 2:
                        pe.wait_ge(s_ex, t - 1)
                    for k in range(KD):
                        ins = pe.matmul(pb[:, 4 + b, 0:EXPERTS], ht[:, b, k, :], wr[:, k, :],
                                        start=(k == 0), stop=(k == KD - 1))
                    ins.then_inc(s_lg, 1)

                def affinities(t):
                    b = t % 2
                    pe.wait_ge(s_af, t + 1)
                    if t >= 2:
                        pe.wait_ge(s_ct, t - 1)
                    pe.transpose(pb[0:EXPERTS, 6 + b, 0:P], aff[:, b, :], keep["ident"][:, :]).then_inc(s_at, 1)

                for t in range(TILES + 2):
                    if t < TILES:
                        pe.wait_ge(s_h, t + 1)
                        if t >= 2:
                            pe.wait_ge(s_ht, t - 1)
                        for k in range(KD):
                            ins = pe.transpose(pb[:, 2 * (t % 2) + k // 4, (k % 4) * P:(k % 4 + 1) * P],
                                               hr[:, t % 2, k * P:(k + 1) * P], keep["ident"][:, :])
                        ins.then_inc(s_tr, 1)
                    if 1 <= t <= TILES:
                        logits(t - 1)
                    if t >= 2:
                        affinities(t - 2)
                pe.wait_ge(s_top, 1)
                pe.transpose(pb[:, 0, 0:EXPERTS], vals[:, 0:P], keep["ident"][0:EXPERTS, 0:EXPERTS])
                pe.transpose(pb[:, 0, 16:16 + EXPERTS], idxf[:, 0:P], keep["ident"][0:EXPERTS, 0:EXPERTS])
                pe.transpose(pb[0:CAP_CTX, 0, 32:32 + EXPERTS], vals[:, P:], keep["ident"][0:EXPERTS, 0:EXPERTS])
                pe.transpose(pb[0:CAP_CTX, 0, 48:48 + EXPERTS], idxf[:, P:], keep["ident"][0:EXPERTS, 0:EXPERTS]
                             ).then_inc(s_it, 1)

            @block.vector
            def _(dve):
                ch = Chain(dve, s_dve)
                dve.wait_ge(s_vec, 80)

                def rows(t):
                    b, c = t % 2, CTX if t == 0 else LATENT
                    dve.wait_ge(s_rt, t + 1)
                    ch.link(dve.reciprocal(st[:, b, 2:3], st[:, b, 1:2]))
                    if t >= 2:
                        dve.wait_ge(s_hs[b], 16 * (t // 2))
                        dve.wait_ge(s_tr, t - 1)
                    ch.link(dve.scalar_tensor_tensor(hr[:, b, :], xr[:, b, :], st[:, b, 2:3], vec[:, c, 0, :],
                                                     ALU.mult, ALU.mult))
                    dve.tensor_tensor(hr[:, b, :], hr[:, b, :], vec[:, c, 1, :], ALU.add).then_inc(s_h, 1)

                def top(t):
                    b = t % 2
                    dve.wait_ge(s_lg, t + 1)
                    dve.tensor_reduce(st[:, b, 3:4], pb[:, 4 + b, 0:EXPERTS], AX.X, ALU.max, negate=True).then_inc(s_mx, 1)

                def soft(t):
                    b = t % 2
                    dve.wait_ge(s_ex, t + 1)
                    ch.link(dve.reciprocal(st[:, b, 5:6], st[:, b, 4:5]))
                    if t >= 2:
                        dve.wait_ge(s_at, t - 1)
                    dve.tensor_scalar(aff[:, b, :], ex[:, b, :], st[:, b, 5:6], None, ALU.mult).then_inc(s_af, 1)

                def kept(t):
                    dve.wait_ge(s_at, t + 1)
                    dve.tensor_copy(cur[:, 0, t * P:(t + 1) * P], pb[0:EXPERTS, 6 + t % 2, 0:P]).then_inc(s_ct, 1)

                rows(0)
                for t in range(TILES + 2):
                    if t + 1 < TILES:
                        rows(t + 1)
                    if 1 <= t <= TILES:
                        top(t - 1)
                    if t >= 2:
                        soft(t - 2)
                        kept(t - 2)
                dve.wait_ge(s_ct, TILES)
                for at, width, first, cap in ((CTX_ROWS, LAT, 0, CAP_LAT), (0, CTX_ROWS, CAP_LAT, CAP_CTX)):
                    for r in range(cap // 8):
                        now, then = cur[:, r % 2, at:at + width], cur[:, 1 - r % 2, at:at + width]
                        eight = slice(first + 8 * r, first + 8 * r + 8)
                        ch.link(dve.max(vals[:, eight], now))
                        ch.step(dve.max_index(idx[:, eight], vals[:, eight], now))
                        ch.link(dve.match_replace(then, vals[:, eight], now, -1.0))
                dve.tensor_copy(idxf[:, :], idx[:, :]).then_inc(s_top, 1)
                dve.memset(keep["idx_lat"][:, EXPERTS:], 0)
                dve.memset(keep["idx_ctx"][:, EXPERTS:], 0)
                dve.wait_ge(s_it, 1)
                dve.tensor_copy(keep["gate_lat"][:, :], pb[:, 0, 0:EXPERTS])
                dve.tensor_scalar(keep["idx_lat"][:, 0:EXPERTS], pb[:, 0, 16:16 + EXPERTS], float(CTX_ROWS), None, ALU.add)
                dve.tensor_copy(keep["gate_ctx"][:, :], pb[0:CAP_CTX, 0, 32:32 + EXPERTS])
                dve.tensor_copy(keep["idx_ctx"][:, 0:EXPERTS], pb[0:CAP_CTX, 0, 48:48 + EXPERTS])


def phase_experts(nc, io, keep, layer):
    with ExitStack() as ctx:
        m = Mem(nc, ctx, f"moe{layer}_")
        xe = m.sb("xe", [P, D])
        xc = m.sb("xc", [CAP_CTX, D])
        xt = m.sb("xt", [P, KD, SLOTS])
        sg = m.sb("sg", [P, 2, SLOTS])
        hid = m.sb("hid", [P, KD, SLOTS])
        yt = m.sb("yt", [P, KD, SLOTS])
        yr = m.sb("yr", [P, D])
        yc = m.sb("yc", [CAP_CTX, D])
        g2 = m.sb("g2", [P, 2, D])
        pb = m.psum()
        ring = keep["ring"]
        s_ring = keep["s_ring"]
        s_g2 = m.sem("gates_in")
        s_xe = m.sem("rows_gathered")
        s_tx = m.sem("rows_transposed")
        s_xt = m.sem("xt_ready")
        s_gu = m.sem("gate_up_done")
        s_sg = m.sem("silu_ready")
        s_hid = m.sem("hidden_ready")
        s_dn = m.sem("down_done")
        s_yt = m.sem("yt_ready")
        s_ty = m.sem("y_transposed")
        s_yr = m.sem("y_rows_ready")
        s_sc = m.sem("scattered")
        ident = keep["ident"]

        with nc.Block() as block:

            @block.sync
            def _(sp):
                for c in range(2):
                    sp.dma_start(g2[:, c, :], io["vec_dram"][layer, c, V_G2:V_G2 + 1, :].partition_broadcast(P)
                                 ).then_inc(s_g2, 16)
                with sp.Fori(1, EXPERTS) as e:
                    for j in range(PIECES):
                        if j < 4:
                            sp.wait_ge(s_gu, e * 8 - (4 if j < 2 else 0))
                        else:
                            sp.wait_ge(s_dn, e * 8 - (4 if j == 4 else 0))
                        sp.dma_start(ring[:, j, :, :], expert_piece(io, layer, j, e)).then_inc(s_ring[j], 16)

            @block.gpsimd
            def _(pool):
                def at(table, e):
                    return bass.IndirectOffsetOnAxis(ap=keep[table][:, e:e + 1], axis=0)

                def gather(e):
                    pool.indirect_dma_start(xe[:, :], None, io["h_dram"], at("idx_lat", e)).then_inc(s_xe, 16)
                    pool.indirect_dma_start(xc[:, :], None, io["h_dram"], at("idx_ctx", e)).then_inc(s_xe, 16)

                gather(0)
                for e in range(EXPERTS):
                    pool.wait_ge(s_tx, e + 1)
                    gather(e + 1)
                    if e:
                        pool.wait_ge(s_sc, e * 32)
                    pool.wait_ge(s_yr, e * 2 + 2)
                    pool.indirect_dma_start(io["x_dram"], at("idx_lat", e), yr[:, :], None, compute_op=ALU.add
                                            ).then_inc(s_sc, 16)
                    pool.indirect_dma_start(io["x_dram"], at("idx_ctx", e), yc[:, :], None, compute_op=ALU.add
                                            ).then_inc(s_sc, 16)
                pool.wait_ge(s_sc, EXPERTS * 32)
                pool.wait_ge(s_xe, (EXPERTS + 1) * 32)

            @block.tensor
            def _(pe):
                def turn_rows():
                    for k in range(KD):
                        pe.transpose(pb[:, 4 + k // 4, (k % 4) * P:(k % 4 + 1) * P], xe[:, k * P:(k + 1) * P], ident[:, :])
                    for k in range(KD):
                        ins = pe.transpose(pb[:, 6, k * CAP_CTX:(k + 1) * CAP_CTX], xc[:, k * P:(k + 1) * P],
                                           ident[0:CAP_CTX, 0:CAP_CTX])
                    ins.then_inc(s_tx, 1)

                pe.wait_ge(s_xe, 32)
                turn_rows()
                with pe.Fori(0, EXPERTS) as e:
                    pe.wait_ge(s_xt, e * 3 + 3)
                    for f in range(KD):
                        half, col = f // 4, (f % 4) * P
                        if f % 4 == 0:
                            pe.wait_ge(s_ring[2 * half], e * 16 + 16)
                            pe.wait_ge(s_ring[2 * half + 1], e * 16 + 16)
                        if f == 0:
                            pe.wait_ge(s_yt, e * 8)
                        if f >= 2:
                            pe.wait_ge(s_hid, e * 8 + (f - 1))
                        for j in range(2):
                            for k in range(KD):
                                ins = pe.matmul(pb[:, 2 * (f % 2) + j, 0:SLOTS], ring[:, 2 * half + j, k, col:col + P],
                                                xt[:, k, :], start=(k == 0), stop=(k == KD - 1))
                        ins.then_inc(s_gu, 1)
                    pe.wait_ge(s_xe, e * 32 + 64)
                    pe.wait_ge(s_yr, e * 2)
                    turn_rows()
                    pe.wait_ge(s_hid, e * 8 + 8)
                    for d in range(KD):
                        half, col = d // 4, (d % 4) * P
                        if d % 4 == 0:
                            pe.wait_ge(s_ring[4 + half], e * 16 + 16)
                        if d >= 4:
                            pe.wait_ge(s_yt, e * 8 + (d - 3))
                        for k in range(KD):
                            ins = pe.matmul(pb[:, d % 4, 0:SLOTS], ring[:, 4 + half, k, col:col + P], hid[:, k, :],
                                            start=(k == 0), stop=(k == KD - 1))
                        ins.then_inc(s_dn, 1)
                    pe.wait_ge(s_xt, e * 3 + 6)
                    pe.wait_ge(s_yt, e * 8 + 8)
                    for d in range(KD):
                        ins = pe.transpose(pb[:, 4 + d // 4, (d % 4) * P:(d % 4 + 1) * P], yt[:, d, 0:CAP_LAT], ident[:, :])
                    ins.then_inc(s_ty, 1)
                    for d in range(KD):
                        ins = pe.transpose(pb[0:CAP_CTX, 6 + d // 4, (d % 4) * P:(d % 4 + 1) * P], yt[:, d, CAP_LAT:SLOTS],
                                           ident[:, :])
                    ins.then_inc(s_ty, 1)

            @block.scalar
            def _(act):
                def keep_rows(e1):
                    act.wait_ge(s_tx, e1)
                    act.activation(xt[:, 0:4, 0:CAP_LAT], pb[:, 4, :].rearrange("p (a c) -> p a c", c=P), ACT.Copy
                                   ).then_inc(s_xt, 1)
                    act.activation(xt[:, 4:8, 0:CAP_LAT], pb[:, 5, :].rearrange("p (a c) -> p a c", c=P), ACT.Copy
                                   ).then_inc(s_xt, 1)
                    act.activation(xt[:, :, CAP_LAT:SLOTS], pb[:, 6, 0:P].rearrange("p (a c) -> p a c", c=CAP_CTX), ACT.Copy
                                   ).then_inc(s_xt, 1)

                keep_rows(1)
                with act.Fori(0, EXPERTS) as e:
                    for f in range(KD):
                        act.wait_ge(s_gu, e * 8 + (f + 1))
                        if f < 2:
                            act.wait_ge(s_hid, e * 8)
                        else:
                            act.wait_ge(s_hid, e * 8 + (f - 1))
                        act.activation(sg[:, f % 2, :], pb[:, 2 * (f % 2), 0:SLOTS], ACT.Silu).then_inc(s_sg, 1)
                    keep_rows(e + 2)
                    act.wait_ge(s_ty, e * 2)
                    for d in range(KD):
                        act.wait_ge(s_dn, e * 8 + (d + 1))
                        act.activation(yt[:, d, :], pb[:, d % 4, 0:SLOTS], ACT.Copy).then_inc(s_yt, 1)

            @block.vector
            def _(dve):
                dve.wait_ge(s_g2, 32)
                with dve.Fori(0, EXPERTS) as e:
                    dve.wait_ge(s_dn, e * 8)
                    for f in range(KD):
                        dve.wait_ge(s_sg, e * 8 + (f + 1))
                        dve.tensor_tensor(hid[:, f, :], pb[:, 2 * (f % 2) + 1, 0:SLOTS], sg[:, f % 2, :], ALU.mult
                                          ).then_inc(s_hid, 1)
                    dve.wait_ge(s_ty, e * 2 + 1)
                    dve.wait_ge(s_sc, e * 32)
                    dve.scalar_tensor_tensor(yr[:, :], pb[:, 4:6, :].rearrange("p a c -> p (a c)"),
                                             keep["gate_lat"][:, bass.ds(e, 1)], g2[:, LATENT, :], ALU.mult, ALU.mult
                                             ).then_inc(s_yr, 1)
                    dve.wait_ge(s_ty, e * 2 + 2)
                    dve.scalar_tensor_tensor(yc[:, :], pb[0:CAP_CTX, 6:8, :].rearrange("p a c -> p (a c)"),
                                             keep["gate_ctx"][:, bass.ds(e, 1)], g2[0:CAP_CTX, CTX, :], ALU.mult, ALU.mult
                                             ).then_inc(s_yr, 1)


def mixture(nc, io, keep, layer):
    with ExitStack() as ctx:
        m = Mem(nc, ctx, f"mix{layer}_")
        keep["ring"] = m.sb("ring", [P, PIECES, KD, HALF])
        keep["s_ring"] = [m.sem(f"weights_in{j}") for j in range(PIECES)]
        keep["idx_lat"] = m.sb("idx_lat", [P, EXPERTS + 1], U32)
        keep["idx_ctx"] = m.sb("idx_ctx", [CAP_CTX, EXPERTS + 1], U32)
        keep["gate_lat"] = m.sb("gate_lat", [P, EXPERTS])
        keep["gate_ctx"] = m.sb("gate_ctx", [CAP_CTX, EXPERTS])
        phase_route(nc, io, keep, layer)
        phase_experts(nc, io, keep, layer)


R_DT, R_DA, R_IN, R_W, R_TOT = range(5)
TRI_LE, TRI_GT, TRI_GE, TRI_LT = 1, 2, 3, 4
LAST_TILE = TILES - 1


def phase_ssd_in(nc, io, keep):
    win = io["ssd_in_w"][0].rearrange("(k p) n -> p k n", p=P)
    PER = 4
    DT_AT = INNER + XBC_TILES * P
    with ExitStack() as ctx:
        m = Mem(nc, ctx, "ssdin_")
        w = m.sb("w", [P, 2, KD, PER * P])
        split = m.sb("w_split", [P, 2, 2, KD, P], F32R)
        wdt = m.sb("wdt", [P, KD, 2 * HEADS])
        dt_split = m.sb("wdt_split", [P, 2, KD, 2 * HEADS], F32R)
        hcol = m.sb("head_columns", [2 * HEADS, 3])
        sp_ = m.sb("softplus", [2 * HEADS, 6, TOK])
        pad = m.sb("pad", [P, 2, GAPPED + 4])
        mid = m.sb("mid", [P, 2, GAPPED])
        out = m.sb("out", [P, 2, GAPPED])
        eend = m.sb("decay_end", [P, TILES, 2 * HEADS])
        ones = m.sb("ones", [P, P])
        pb = m.psum()
        s_w = [m.sem(f"w_in{b}") for b in range(2)]
        s_wdt = m.sem("dt_weights_in")
        s_hi = m.sem("w_leading")
        s_lo = m.sem("w_trailing")
        s_dts = m.sem("dt_weights_split")
        s_mm = m.sem("projected")
        s_dt = m.sem("dt_projected")
        s_dv = m.sem("dt_kept")
        s_act = m.sem("act")
        s_dve = m.sem("dve")
        s_zero = m.sem("pads_zero")
        s_ev = m.sem("padded")
        s_mid = m.sem("mid_tap")
        s_cv = m.sem("convolved")
        s_cnt = m.sem("taps_added")
        s_si = m.sem("silu_ready")
        s_st = [m.sem(f"stored{b}") for b in range(2)]
        s_rows = m.sem("rates_rows")
        s_kept = m.sem("rates_kept")
        s_cum = m.sem("cumulated")
        s_ex = m.sem("decays_ready")
        prm, rates, tri = keep["prm"], keep["rates"], keep["tri"]

        def bank(q):
            return 3 * (q % 2)

        with nc.Block() as block:

            @block.sync
            def _(sp):
                sp.dma_start(wdt[:, :, :], win[:, :, DT_AT:]).then_inc(s_wdt, 16)
                sp.dma_start(hcol[:, 0:1], io["ssd_dt_bias"][0].rearrange("a (h b) -> (a h) b", b=1)).then_inc(s_wdt, 16)
                sp.dma_start(hcol[:, 1:2], io["ssd_A_log"][0].rearrange("a (h b) -> (a h) b", b=1)).then_inc(s_wdt, 16)
                for b in range(2):
                    sp.dma_start(w[:, b, :, :], win[:, :, b * HALF:(b + 1) * HALF]).then_inc(s_w[b], 16)
                with sp.Fori(1, 5) as i:
                    for b in range(2):
                        sp.wait_ge(s_lo, i * 2 * PER - (PER if b == 0 else 0))
                        sp.dma_start(w[:, b, :, :], win[:, :, bass.ds((i * 2 + b) * HALF, HALF)]).then_inc(s_w[b], 16)

            @block.tensor
            def _(pe):
                def project(b, n, i):
                    q = PER * b + n
                    pe.wait_ge(s_lo, i * 2 * PER + (q + 1))
                    pe.wait_ge(s_ev, i * 2 * PER + max(q - 1, 0))
                    product3(pe, lambda piece: pb[:, bank(q) + piece, 0:THIRD],
                             (split[:, q % 2, 0, :, :], split[:, q % 2, 1, :, :]), lambda w_, k: w_[:, k, :],
                             keep["hT"], third).then_inc(s_mm, 1)

                pe.wait_ge(s_dts, 2)
                product3(pe, lambda piece: pb[0:2 * HEADS, 3 + piece, 0:THIRD], (dt_split[:, 0, :, :], dt_split[:, 1, :, :]),
                         lambda w_, k: w_[:, k, :], keep["hT"], third).then_inc(s_dt, 1)
                pe.wait_ge(s_dv, 1)
                with pe.Fori(0, 2) as i:
                    for b in range(2):
                        for n in range(PER):
                            project(b, n, i)
                pe.wait_ge(s_rows, 1)
                for which in range(2):
                    for t in range(TILES - 1):
                        ins = pe.transpose(pb[:, 6 + which, t * 64:(t + 1) * 64], sp_[:, which, t * P:(t + 1) * P],
                                           keep["ident"][0:64, 0:64])
                ins.then_inc(s_cum, 1)
                pe.wait_ge(s_kept, 2)
                for which in range(2):
                    ins = pe.transpose(pb[:, 6, which * 64:(which + 1) * 64], sp_[:, which, LAST_TILE * P:TOK],
                                       keep["ident"][0:64, 0:64])
                ins.then_inc(s_cum, 1)
                pe.wait_ge(s_kept, 4)
                for n, (left, back) in enumerate(((TRI_LE, 0), (TRI_GE, 1), (TRI_GT, 0), (TRI_LT, 1), (None, 0), (None, 1))):
                    if n >= 2:
                        pe.wait_ge(s_ex, n - 1)
                    pe.matmul(pb[:, 6 + n % 2, 0:TILES * HEADS], ones[:, :] if left is None else tri[:, left, :],
                              rates[:, :, R_DA, back * HEADS:(back + 1) * HEADS], start=True, stop=True).then_inc(s_cum, 1)
                with pe.Fori(2, 5) as i:
                    for b in range(2):
                        for n in range(PER):
                            project(b, n, i)

            @block.scalar
            def _(act):
                ch = Chain(act, s_act)
                S = lambda n: sp_[:, n, :]

                def lead(b, n, i, first=False):
                    q = PER * b + n
                    if n == 0:
                        act.wait_ge(s_w[b], i * 16 + 16)
                    if not first:
                        act.wait_ge(s_lo, i * 2 * PER + (q - 1))
                        act.wait_ge(s_mm, i * 2 * PER + (q - 1))
                    act.activation(split[:, q % 2, 0, :, :], w[:, b, :, n * P:(n + 1) * P], ACT.Copy).then_inc(s_hi, 1)

                def lead_next(q, i):
                    if q < 2 * PER - 2:
                        lead((q + 2) // PER, (q + 2) % PER, i)
                    else:
                        lead(0, q + 2 - 2 * PER, i + 1)

                act.wait_ge(s_wdt, 48)
                act.activation(dt_split[:, 0, :, :], wdt[:, :, :], ACT.Copy).then_inc(s_dts, 1)
                lead(0, 0, 0, True)
                lead(0, 1, 0, True)
                ch.step(act.activation(hcol[:, 2:3], hcol[:, 1:2], ACT.Exp))
                act.wait_ge(s_dt, 1)
                act.activation(sp_[:, 0, :].rearrange("p (a c) -> p a c", c=THIRD), pb[0:2 * HEADS, 3:6, 0:THIRD],
                               ACT.Identity, bias=hcol[:, 0:1]).then_inc(s_dv, 1)
                act.wait_ge(s_dv, 1)
                ch.link(act.activation(S(1), S(0), ACT.Abs))
                ch.link(act.activation(S(2), S(1), ACT.Exp, scale=-1.0))
                act.wait_ge(s_dve, 1)
                ch.step(act.activation(S(3), S(4), ACT.Ln))

                act.wait_ge(s_zero, 6)

                def z_tile(b, n, i):
                    q = PER * b + n
                    act.wait_ge(s_mm, i * 8 + (q + 1))
                    act.wait_ge(s_st[q % 2], i * 64 + 16 * (q // 2))
                    act.activation(out[:, q % 2, 0:TOK].rearrange("p (a c) -> p a c", c=THIRD),
                                   pb[:, bank(q):bank(q) + 3, 0:THIRD], ACT.Silu).then_inc(s_ev, 1)

                def xbc_tile(b, n, i):
                    q = PER * b + n
                    act.wait_ge(s_mm, i * 8 + (q + 1))
                    if q < 2:
                        act.wait_ge(s_cv, i * 8 - 16)
                    else:
                        act.wait_ge(s_cv, i * 8 - 16 + (q - 1))
                    act.activation(pad[:, q % 2, 2:2 + CTX_ROWS], pb[:, bank(q), 0:CTX_ROWS], ACT.Copy)
                    act.activation(pad[:, q % 2, LAT_AT + 2:THIRD + 4], pb[:, bank(q), CTX_ROWS:THIRD], ACT.Copy)
                    act.activation(pad[:, q % 2, THIRD + 4:GAPPED + 2].rearrange("p (a c) -> p a c", c=THIRD),
                                   pb[:, bank(q) + 1:bank(q) + 3, 0:THIRD], ACT.Copy).then_inc(s_ev, 1)
                    act.wait_ge(s_ev, i * 8 + (q + 1))
                    if q < 2:
                        act.wait_ge(s_si, i * 8 - 16)
                    else:
                        act.wait_ge(s_si, i * 8 - 16 + (q - 1))
                    act.activation(mid[:, q % 2, :], pad[:, q % 2, 2:2 + GAPPED], ACT.Identity,
                                   bias=prm[:, 1, bass.ds(i * 8 + (q - 16), 1)],
                                   scale=prm[:, 0, bass.ds(i * 8 + (2 * XBC_TILES - 16 + q), 1)]).then_inc(s_mid, 1)

                def silu(b, n, i):
                    q = PER * b + n
                    act.wait_ge(s_cv, i * 8 + (q - 15))
                    act.wait_ge(s_st[q % 2], i * 128 + (32 * (q // 2) - 256 + 128))
                    act.activation(out[:, q % 2, :], mid[:, q % 2, :], ACT.Silu).then_inc(s_si, 1)

                with act.Fori(0, 2) as i:
                    for b in range(2):
                        for n in range(PER):
                            z_tile(b, n, i)
                            lead_next(PER * b + n, i)
                for n, (slot, back) in enumerate(((R_IN, 0), (R_IN, 1), (None, 0), (None, 1), (R_TOT, 0), (R_TOT, 1))):
                    act.wait_ge(s_cum, n + 3)
                    cols = slice(back * HEADS, (back + 1) * HEADS)
                    dst = eend[:, :, cols] if slot is None else rates[:, :, slot, cols]
                    act.activation(dst, pb[:, 6 + n % 2, 0:TILES * HEADS].rearrange("p (a c) -> p a c", c=HEADS), ACT.Exp
                                   ).then_inc(s_ex, 1)

                def xbc_tiles(i, last):
                    for q in range(2 * PER):
                        xbc_tile(q // PER, q % PER, i)
                        if not last or q < 2 * PER - 2:
                            lead_next(q, i)
                        silu(q // PER, q % PER, i)

                with act.Fori(2, 4) as i:
                    xbc_tiles(i, False)
                xbc_tiles(4, True)

            @block.vector
            def _(dve):
                ch = Chain(dve, s_dve)
                S = lambda n: sp_[:, n, :]

                def rest(b, n, i):
                    q = PER * b + n
                    dve.wait_ge(s_hi, i * 2 * PER + (q + 1))
                    dve.tensor_tensor(split[:, q % 2, 1, :, :], w[:, b, :, n * P:(n + 1) * P],
                                      split[:, q % 2, 0, :, :].bitcast(F32), ALU.subtract).then_inc(s_lo, 1)

                def rest_next(q, i):
                    if q < 2 * PER - 2:
                        rest((q + 2) // PER, (q + 2) % PER, i)
                    else:
                        rest(0, q + 2 - 2 * PER, i + 1)

                dve.wait_ge(s_dts, 1)
                dve.tensor_tensor(dt_split[:, 1, :, :], wdt[:, :, :], dt_split[:, 0, :, :].bitcast(F32), ALU.subtract
                                  ).then_inc(s_dts, 1)
                rest(0, 0, 0)
                rest(0, 1, 0)
                dve.wait_ge(s_act, 3)
                ch.link(dve.tensor_scalar(S(4), S(2), 1.0, None, ALU.add))
                ch.link(dve.tensor_scalar(S(1), S(4), -1.0, 1e-30, ALU.add, ALU.max))
                ch.link(dve.reciprocal(S(5), S(1)))
                dve.wait_ge(s_act, 4)
                ch.link(dve.tensor_tensor(S(5), S(5), S(3), ALU.mult))
                ch.link(dve.tensor_tensor(S(5), S(5), S(2), ALU.mult))
                ch.link(dve.scalar_tensor_tensor(S(4), S(4), 1.0, S(2), ALU.is_equal, ALU.mult))
                ch.link(dve.tensor_tensor(S(5), S(5), S(4), ALU.add))
                ch.link(dve.scalar_tensor_tensor(S(0), S(0), 0.0, S(5), ALU.max, ALU.add))
                ch.link(dve.tensor_scalar(S(1), S(0), hcol[:, 2:3], -1.0, ALU.mult, ALU.mult))
                dve.memset(ones[:, :], 1.0).then_inc(s_rows, 1)
                for b in range(2):
                    for at, width in ((0, 2), (CTX_ROWS + 2, 2), (GAPPED + 2, 2)):
                        dve.memset(pad[:, b, at:at + width], 0.0).then_inc(s_zero, 1)
                with dve.Fori(0, 2) as i:
                    for q in range(2 * PER):
                        rest_next(q, i)
                dve.wait_ge(s_cum, 1)
                for which in range(2):
                    dve.tensor_copy(rates[:, 0:LAST_TILE, which, :],
                                    pb[:, 6 + which, :].rearrange("p (a c) -> p a c", c=64)).then_inc(s_kept, 1)
                dve.wait_ge(s_cum, 2)
                for which in range(2):
                    dve.tensor_copy(rates[:, LAST_TILE, which, :], pb[:, 6, which * 64:(which + 1) * 64]).then_inc(s_kept, 1)
                dve.wait_ge(s_ex, 4)
                dve.wait_ge(s_kept, 4)
                dve.tensor_tensor(rates[:, :, R_W, :], rates[:, :, R_DT, :], eend[:, :, :], ALU.mult)

                def tiles(i, last):
                    for q in range(2 * PER):
                        dve.wait_ge(s_mid, i * 8 + (q + 1))
                        for n, tap in enumerate((0, 1, 3, 4)):
                            ins = dve.scalar_tensor_tensor(mid[:, q % 2, :], pad[:, q % 2, tap:tap + GAPPED],
                                                           prm[:, 0, bass.ds(i * 8 + (tap * XBC_TILES + q), 1)],
                                                           mid[:, q % 2, :], ALU.mult, ALU.add)
                            if n < 3:
                                ins.then_inc(s_cnt, 1)
                                dve.wait_ge(s_cnt, i * 24 + (3 * q + n + 1))
                            else:
                                ins.then_inc(s_cv, 1)
                        if not last or q < 2 * PER - 2:
                            rest_next(q, i + 2)

                with dve.Fori(0, 2) as i:
                    tiles(i, False)
                tiles(2, True)

            @block.gpsimd
            def _(pool):
                with pool.Fori(0, 2) as i:
                    for q in range(8):
                        pool.wait_ge(s_ev, i * 8 + (q + 1))
                        pool.dma_start(io["z_dram"][:, :, i * 8 + q, :].rearrange("t p c -> p t c"),
                                       out[:, q % 2, 0:TOK].rearrange("p (t c) -> p t c", c=P)).then_inc(s_st[q % 2], 16)
                with pool.Fori(0, 3) as i:
                    for q in range(8):
                        pool.wait_ge(s_si, i * 8 + (q + 1))
                        pool.dma_start(io["xbc_dram"][0, :, i * 8 + q, :], out[:, q % 2, 0:P]).then_inc(s_st[q % 2], 16)
                        pool.dma_start(io["xbc_dram"][1:, :, i * 8 + q, :].rearrange("t p c -> p t c"),
                                       out[:, q % 2, LAT_AT:].rearrange("p (t c) -> p t c", c=P)).then_inc(s_st[q % 2], 16)
                for b in range(2):
                    pool.wait_ge(s_st[b], 8 * 16 + 12 * 32)


GW = INNER // GROUPS
GH = HEADS // GROUPS


def per_head(ap):
    return ap.unsqueeze(2).broadcast_to([P, ap.shape[-1], HEAD])


def by_head(ap):
    return ap.rearrange("p (h c) -> p h c", c=HEAD)


def phase_states(nc, io, keep):
    XB = 20 * P
    with ExitStack() as ctx:
        m = Mem(nc, ctx, "st_")
        xb = m.sb("xb", [P, 2, XB])
        init = m.sb("init", [P, 2, 16, P])
        rc = m.sb("rates", [P, 2, 5, 64])
        xrow = m.sb("xrow", [P, 2, INNER])
        brow = m.sb("brow", [P, 2, GROUPS * P])
        xw = m.sb("xw", [P, 2, INNER])
        decayed = m.sb("decayed", [P, INNER])
        sb_ = m.sb("state_back", [P, 2, INNER])
        out = m.sb("ctx_state", [P, 2, 16, P])
        pb = m.psum()
        s_xb = [m.sem(f"chunk_in{b}") for b in range(2)]
        s_init = m.sem("init_in")
        s_rc = m.sem("rates_ready")
        s_tr = m.sem("transposed")
        s_row = m.sem("rows_ready")
        s_xw = m.sem("weighted")
        s_con = m.sem("contributions")
        s_cx = m.sem("ctx_kept")
        s_it = m.sem("init_transposed")
        s_ik = m.sem("init_kept")
        s_dec = m.sem("decayed")
        s_new = m.sem("state_ready")
        s_st = [m.sem(f"state_stored{b}") for b in range(2)]
        s_out = m.sem("ctx_stored")
        state, rates, ident = keep["state"], keep["rates"], keep["ident"]

        with nc.Block() as block:

            @block.sync
            def _(sp):
                sp.dma_start(xb[:, 0, :], io["xbc_dram"][0, :, 0:20, :].rearrange("p a c -> p (a c)")).then_inc(s_xb[0], 16)
                for d in range(2):
                    for h in range(2):
                        sp.dma_start(init[h * HEAD:(h + 1) * HEAD, d, :, :],
                                     io["state_ssd"][0, 0, d].rearrange("(a b) p n -> b p a n", b=2)[h]).then_inc(s_init, 16)
                sp.dma_start(xb[:, 1, :], io["xbc_dram"][8, :, 0:20, :].rearrange("p a c -> p (a c)")).then_inc(s_xb[1], 16)
                with sp.Fori(0, 4) as i:
                    for b in range(2):
                        sp.wait_ge(s_tr, i * 2 + (b + 1))
                        sp.dma_start(xb[:, b, :], io["xbc_dram"][(7 - b) + i * -2, :, 0:20, :].rearrange("p a c -> p (a c)")
                                     ).then_inc(s_xb[b], 16)
                sp.wait_ge(s_xb[1], 80)

            @block.tensor
            def _(pe):
                def turn(b, done):
                    for a in range(20):
                        ins = pe.transpose(pb[:, a // 4, (a % 4) * P:(a % 4 + 1) * P], xb[:, b, a * P:(a + 1) * P], ident)
                    ins.then_inc(s_tr, 1)

                pe.wait_ge(s_xb[0], 16)
                turn(0, 0)
                pe.wait_ge(s_xw, 8)
                pe.wait_ge(s_row, 5)
                for d in range(2):
                    for a in range(16):
                        n = d * 16 + a
                        if n % 4 == 0 and n >= 12:
                            pe.wait_ge(s_cx, n // 4 - 2)
                        ins = pe.matmul(pb[:, 5 + (n // 4) % 3, (a % 4) * P:(a % 4 + 1) * P], xw[:, d, a * P:(a + 1) * P],
                                        brow[:, 0, (a // 4) * P:(a // 4 + 1) * P], start=True, stop=True)
                        if a % 4 == 3:
                            ins.then_inc(s_con, 1)
                pe.wait_ge(s_init, 64)
                for d in range(2):
                    for a in range(16):
                        n = d * 16 + a
                        if n % 4 == 0:
                            if n == 0:
                                pe.wait_ge(s_cx, 8)
                            if n >= 12:
                                pe.wait_ge(s_ik, n // 4 - 2)
                        ins = pe.transpose(pb[:, 5 + (n // 4) % 3, (a % 4) * P:(a % 4 + 1) * P], init[:, d, a, :], ident)
                        if a % 4 == 3:
                            ins.then_inc(s_it, 1)
                pe.wait_ge(s_ik, 8)
                with pe.Fori(0, 4) as i:
                    for b in range(2):
                        pe.wait_ge(s_row, i * 10 + (5 * b + 5))
                        if b == 0:
                            pe.wait_ge(s_xb[1], i * 16 + 16)
                        else:
                            pe.wait_ge(s_xb[0], i * 16 + 32)
                        turn(1 - b, 0)
                        pe.wait_ge(s_row, i * 10 + (5 * b + 10))
                        for g in range(GROUPS):
                            n = 4 * b + g
                            pe.wait_ge(s_xw, i * 8 + (n + 9))
                            pe.wait_ge(s_new, i * 8 + (4 * b + (1 if g == 3 else 0)))
                            pe.matmul(pb[:, 5 + g % 3, :], brow[:, b, g * P:(g + 1) * P], xw[:, b, g * GW:(g + 1) * GW],
                                      start=True, stop=True).then_inc(s_con, 1)

            @block.scalar
            def _(act):
                def rows(b, br):
                    for a in range(4):
                        act.activation(xrow[:, b, a * GW:(a + 1) * GW], pb[:, a, :], ACT.Copy).then_inc(s_row, 1)
                    act.activation(brow[:, br, :], pb[:, 4, :], ACT.Copy).then_inc(s_row, 1)

                act.wait_ge(s_tr, 1)
                rows(0, 0)
                for n in range(8):
                    act.wait_ge(s_con, n + 1)
                    act.activation(out[:, n // 4, 4 * (n % 4):4 * (n % 4) + 4, :].rearrange("p a c -> p (a c)"),
                                   pb[:, 5 + n % 3, :], ACT.Copy).then_inc(s_cx, 1)
                act.wait_ge(s_cx, 8)
                for d in range(2):
                    for h in range(2):
                        act.dma_start(io["new_state"][0, 0, d].rearrange("(a b) p n -> b p a n", b=2)[h],
                                      out[h * HEAD:(h + 1) * HEAD, d, :, :]).then_inc(s_out, 16)
                for n in range(8):
                    act.wait_ge(s_it, n + 1)
                    dst = state if n < 4 else sb_[:, 0, :]
                    act.activation(dst[:, (n % 4) * GW:(n % 4 + 1) * GW], pb[:, 5 + n % 3, :], ACT.Copy).then_inc(s_ik, 1)
                with act.Fori(0, 4) as i:
                    for b in range(2):
                        act.wait_ge(s_tr, i * 2 + (b + 2))
                        act.wait_ge(s_xw, i * 8 + (4 * b + 8))
                        act.wait_ge(s_con, i * 8 + (4 * b + 8) )
                        rows(b, b)
                act.wait_ge(s_out, 64)

            @block.vector
            def _(dve):
                dve.tensor_copy(rc[:, 0, :, :], rates[:, 0, :, :]).then_inc(s_rc, 1)
                dve.wait_ge(s_rc, 1)
                for d in range(2):
                    for g in range(GROUPS):
                        dve.wait_ge(s_row, g + 1)
                        h0 = d * HEADS + g * GH
                        dve.tensor_tensor(by_head(xw[:, d, g * GW:(g + 1) * GW]), by_head(xrow[:, 0, g * GW:(g + 1) * GW]),
                                          per_head(rc[:, 0, R_W, h0:h0 + GH]), ALU.mult).then_inc(s_xw, 1)
                dve.wait_ge(s_ik, 8)
                with dve.Fori(0, 4) as i:
                    for b in range(2):
                        dve.wait_ge(s_new, i * 8 + 4 * b)
                        dve.wait_ge(s_xw, i * 8 + (4 * b + 8))
                        dve.tensor_copy(rc[:, b, :, :], rates[:, bass.ds((8 - b) + i * -2, 1), :, :].rearrange("p a b c -> p (a b) c")
                                        ).then_inc(s_rc, 1)
                        dve.wait_ge(s_rc, i * 2 + (b + 2))
                        for g in range(GROUPS):
                            h0 = HEADS + g * GH
                            cols = slice(g * GW, (g + 1) * GW)
                            dve.wait_ge(s_row, i * 10 + (5 * b + g + 6))
                            if g == 0:
                                dve.wait_ge(s_con, i * 8 + (4 * b + 8))
                            dve.tensor_tensor(by_head(xw[:, b, cols]), by_head(xrow[:, b, cols]),
                                              per_head(rc[:, b, R_W, h0:h0 + GH]), ALU.mult).then_inc(s_xw, 1)
                            dve.tensor_tensor(by_head(decayed[:, cols]), by_head(sb_[:, b, cols]),
                                              per_head(rc[:, b, R_TOT, h0:h0 + GH]), ALU.mult).then_inc(s_dec, 1)
                        dve.wait_ge(s_st[1 - b], i * 16 + 16 * b)
                        for g in range(GROUPS):
                            n = 4 * b + g
                            cols = slice(g * GW, (g + 1) * GW)
                            dve.wait_ge(s_con, i * 8 + (n + 9))
                            dve.wait_ge(s_dec, i * 8 + (n + 1))
                            dve.tensor_tensor(sb_[:, 1 - b, cols], decayed[:, cols], pb[:, 5 + g % 3, :], ALU.add
                                              ).then_inc(s_new, 1)

            @block.gpsimd
            def _(pool):
                pool.wait_ge(s_ik, 8)
                with pool.Fori(0, 4) as i:
                    for b in range(2):
                        pool.wait_ge(s_new, i * 8 + 4 * b)
                        pool.dma_start(io["sb_dram"][(8 - b) + i * -2], sb_[:, b, :]).then_inc(s_st[b], 16)
                for b in range(2):
                    pool.wait_ge(s_st[b], 4 * 16)


def phase_scan(nc, io, keep):
    x_rows = io["x_dram"].rearrange("(t p) d -> t p d", p=P)
    with ExitStack() as ctx:
        m = Mem(nc, ctx, "scan_")
        w = m.sb("w", [P, Z_TILES, D])
        xbc = m.sb("xbc", [P, 2, XBC_TILES, P])
        zt = m.sb("z", [P, Z_TILES, P])
        sbt = m.sb("state_back", [P, INNER])
        xr = m.sb("x", [P, D])
        gate = m.sb("gate", [P, 2, D])
        rc = m.sb("rates", [P, 2, 5, 64])
        tri_by = m.sb("tri_by_rate", [P, 2, GH, P])
        ex = m.sb("exp", [P, 2, GH, P])
        mix = m.sb("mix", [P, GH, P])
        cb = m.sb("cb", [P, 2, GROUPS, P])
        xrow = m.sb("xrow", [P, INNER])
        brow = m.sb("brow", [P, GROUPS * P])
        xw = m.sb("xw", [P, GW])
        tmp = m.sb("tmp", [P, 2, GW])
        y = m.sb("y", [P, INNER])
        yc = m.sb("yc", [P, Z_TILES, P])
        red = m.sb("red", [P, P])
        ones = m.sb("ones", [P, 2])
        st = m.sb("stats", [P, 2])
        sq = y[:, :].rearrange("p (a c) -> p a c", c=P)
        pb = m.psum()
        s_w = m.sem("w_in")
        s_gw = m.sem("w_scaled")
        s_gate = m.sem("gate_in")
        s_c = [m.sem(f"chunk_in{b}") for b in range(2)]
        s_z = m.sem("z_in")
        s_sb = m.sem("state_back_in")
        s_x = m.sem("x_in")
        s_one = m.sem("ones_ready")
        s_rc = m.sem("rates_ready")
        s_tx = m.sem("chunk_transposed")
        s_row = m.sem("rows_ready")
        s_cb = m.sem("cb_done")
        s_cbm = m.sem("cb_masked")
        s_tr = m.sem("tri_by_rate_ready")
        s_seg = m.sem("segments")
        s_ex = m.sem("exp_ready")
        s_dve = m.sem("dve")
        s_mix = m.sem("mix_ready")
        s_y = m.sem("diagonal_done")
        s_off = m.sem("off_done")
        s_xw = m.sem("weighted")
        s_con = m.sem("contribution")
        s_yr = m.sem("y_rows_ready")
        s_new = m.sem("state_ready")
        s_yt = m.sem("y_transposed")
        s_yk = m.sem("y_kept")
        s_zg = m.sem("gated")
        s_sq = m.sem("squared")
        s_red = m.sem("squares_summed")
        s_ss = m.sem("norm_summed")
        s_pj = m.sem("projected")
        s_rt = m.sem("root")
        s_pe = m.sem("projection_kept")
        s_sum = m.sem("x_summed")
        s_st = m.sem("x_stored")
        s_gc = m.sem("gate_changed")
        s_cm = m.sem("combined")
        s_rcp = m.sem("inverse_root")
        state, rates, ident, tri, prm = keep["state"], keep["rates"], keep["ident"], keep["tri"], keep["prm"]
        B_T, C_T = 16, 20

        with nc.Block() as block:

            @block.sync
            def _(sp):
                for c in range(2):
                    sp.dma_start(xbc[:, c, :, :], io["xbc_dram"][c]).then_inc(s_c[c], 16)
                    if c == 0:
                        sp.dma_start(w[:, :, :], io["ssd_out_w"][0].rearrange("(k p) n -> p k n", p=P)).then_inc(s_w, 16)
                        sp.dma_start(sbt[:, :], io["sb_dram"][1]).then_inc(s_sb, 16)
                        for n in range(2):
                            sp.dma_start(gate[:, n, :], io["vec_dram"][1, n, V_G1:V_G1 + 1, :].partition_broadcast(P)
                                         ).then_inc(s_gate, 16)
                        sp.dma_start(zt[:, :, :], io["z_dram"][0]).then_inc(s_z, 16)
                        sp.dma_start(xr[:, :], x_rows[0]).then_inc(s_x, 16)

                for t in range(TILES):
                    sp.wait_ge(s_yk, t * 16 + 16)
                    if t + 2 < TILES:
                        sp.dma_start(xbc[:, t % 2, :, :], io["xbc_dram"][t + 2]).then_inc(s_c[t % 2], 16)
                    if t < LAST_TILE:
                        sp.wait_ge(s_zg, t + 1)
                        sp.dma_start(zt[:, :, :], io["z_dram"][t + 1]).then_inc(s_z, 16)
                    sp.wait_ge(s_sum, t + 1)
                    sp.dma_start(x_rows[t], xr[:, :]).then_inc(s_st, 16)
                    sp.wait_ge(s_st, t * 16 + 16)
                    if t < LAST_TILE:
                        sp.dma_start(xr[:, :], x_rows[t + 1]).then_inc(s_x, 16)
                    if t + 2 < TILES:
                        sp.wait_ge(s_yr, t * 4 + 8)
                        sp.dma_start(sbt[:, :], io["sb_dram"][t + 2]).then_inc(s_sb, 16)

            @block.tensor
            def _(pe):
                def turn_x(b, c, use, ctx_chunk):
                    pe.wait_ge(s_c[b], use * 16 + 16)
                    if not ctx_chunk:
                        pe.wait_ge(s_ex, c * 8)
                    for a in range(16):
                        ins = pe.transpose(pb[:, a // 4, (a % 4) * P:(a % 4 + 1) * P], xbc[:, b, a, :], ident)
                        if a % 4 == 3:
                            ins.then_inc(s_tx, 1)

                def turn_b(b, c, ctx_chunk):
                    if not ctx_chunk:
                        pe.wait_ge(s_yr, c * 4)
                    for a in range(GROUPS):
                        ins = pe.transpose(pb[:, 4, a * P:(a + 1) * P], xbc[:, b, B_T + a, :], ident)
                    ins.then_inc(s_tx, 1)
                    for g in range(GROUPS):
                        ins = pe.matmul(pb[:, 5, g * P:(g + 1) * P], xbc[:, b, B_T + g, :], xbc[:, b, C_T + g, :],
                                        start=True, stop=True)
                    ins.then_inc(s_cb, 1)

                def turn_y(t):
                    pe.wait_ge(s_yr, t * 4 + 4)
                    pe.wait_ge(s_new, t * 4 + 4)
                    for q in range(4):
                        if q >= 2:
                            pe.wait_ge(s_yk, t * 16 + 4 * (q - 1))
                        for a in range(4):
                            ins = pe.transpose(pb[:, 6 + q % 2, a * P:(a + 1) * P], y[:, (4 * q + a) * P:(4 * q + a + 1) * P], ident)
                        ins.then_inc(s_yt, 1)

                def project(t):
                    pe.wait_ge(s_zg, t + 1)
                    for half in range(2):
                        for k in range(Z_TILES):
                            ins = pe.matmul(pb[:, 6 + half, :], yc[:, k, :], w[:, k, half * HALF:(half + 1) * HALF],
                                            start=(k == 0), stop=(k == Z_TILES - 1))
                    ins.then_inc(s_pj, 1)
                    pe.wait_ge(s_red, t + 1)
                    pe.matmul(pb[:, 5, 0:2], red[:, :], ones[:, :], start=True, stop=True).then_inc(s_ss, 1)

                def segments(g, c):
                    n = g
                    pe.wait_ge(s_tr, c * 8 + (2 * n + 2))
                    if g == 0:
                        pe.wait_ge(s_row, c * 5 + 4)
                    else:
                        pe.wait_ge(s_ex, c * 8 + 2 * n)
                    for d, left in enumerate((TRI_GT, TRI_LT)):
                        for half in range(2):
                            ins = pe.matmul(pb[:, 2 * d + half, :], tri[:, left, :],
                                            tri_by[:, d, 4 * half:4 * half + 4, :].rearrange("p a c -> p (a c)"),
                                            start=True, stop=True)
                        ins.then_inc(s_seg, 1)

                def group(g, b, c, ctx_chunk, then=None):
                    if g < 3:
                        segments(g + 1, c)
                    if not ctx_chunk:
                        if g:
                            pe.wait_ge(s_yr, c * 4 + g)
                            pe.wait_ge(s_new, c * 4 + g)
                        else:
                            pe.wait_ge(s_sb, c * 16)
                            pe.wait_ge(s_row, c * 5 + 5)
                            pe.wait_ge(s_new, c * 4)
                            pe.wait_ge(s_pe, c)
                            pe.wait_ge(s_rt, c)
                        cols = slice(g * GW, (g + 1) * GW)
                        pe.matmul(pb[:, 5, :], xbc[:, b, C_T + g, :], state[:, cols], start=True, stop=True)
                        pe.matmul(pb[:, 6, :], xbc[:, b, C_T + g, :], sbt[:, cols], start=True, stop=True).then_inc(s_off, 1)
                        pe.wait_ge(s_xw, c * 4 + (g - 3))
                        pe.matmul(pb[:, 7, :], brow[:, g * P:(g + 1) * P], xw[:, :], start=True, stop=True).then_inc(s_con, 1)
                    else:
                        if g:
                            pe.wait_ge(s_yr, g)
                        else:
                            pe.wait_ge(s_row, 5)
                    if then:
                        then()
                    pe.wait_ge(s_mix, c * 4 + (g + 1))
                    for h in range(GH):
                        ins = pe.matmul(pb[:, 4, h * HEAD:(h + 1) * HEAD], mix[:, h, :],
                                        xrow[:, (g * GH + h) * HEAD:(g * GH + h + 1) * HEAD], start=True, stop=True)
                    ins.then_inc(s_y, 1)

                pe.wait_ge(s_one, 1)
                turn_x(0, 0, 0, True)
                turn_b(0, 0, True)
                segments(0, 0)
                for g in range(GROUPS):
                    group(g, 0, 0, True, (lambda: turn_x(1, 1, 0, False)) if g == 3 else None)

                def chunk(b, c, then):
                    turn_b(b, c, False)
                    pe.wait_ge(s_cbm, c * 2 + 2)
                    turn_y(c - 1)
                    segments(0, c)
                    project(c - 1)
                    for g in range(GROUPS):
                        group(g, b, c, False, then if g == 3 else None)

                pe.wait_ge(s_gw, Z_TILES)
                with pe.Fori(0, 3) as i:
                    chunk(1, i * 2 + 1, lambda: turn_x(0, i * 2 + 2, i + 1, False))
                    chunk(0, i * 2 + 2, lambda: turn_x(1, i * 2 + 3, i + 1, False))
                chunk(1, 7, lambda: turn_x(0, 8, 4, False))
                chunk(0, 8, None)
                turn_y(8)
                pe.wait_ge(s_gate, 32)
                project(8)

            @block.scalar
            def _(act):
                def rows(c, ctx_chunk):
                    for a in range(4):
                        act.wait_ge(s_tx, c * 5 + (a + 1))
                        if a == 0 and not ctx_chunk:
                            act.wait_ge(s_y, c * 4)
                        act.activation(xrow[:, a * GW:(a + 1) * GW], pb[:, a, :], ACT.Copy).then_inc(s_row, 1)
                    act.wait_ge(s_tx, c * 5 + 5)
                    if not ctx_chunk:
                        act.wait_ge(s_new, c * 4)
                    act.activation(brow[:, :], pb[:, 4, :], ACT.Copy).then_inc(s_row, 1)

                def exps(g, c):
                    for d in range(2):
                        act.wait_ge(s_seg, c * 8 + (2 * g + d + 1))
                        if d == 0:
                            act.wait_ge(s_mix, c * 4 + g)
                        act.activation(ex[:, d, :, :].rearrange("p (a h) c -> p a (h c)", a=2), pb[:, 2 * d:2 * d + 2, :], ACT.Exp
                                       ).then_inc(s_ex, 1)

                def square(t):
                    act.wait_ge(s_zg, t + 1)
                    act.wait_ge(s_yt, t * 4 + 4)
                    act.activation(sq, yc[:, :, :], ACT.Square).then_inc(s_sq, 1)

                def root(t):
                    act.wait_ge(s_ss, t + 1)
                    act.activation(st[:, 0:1], pb[:, 5, 0:1], ACT.Sqrt, bias=keep["eps"][:, 0:1], scale=1.0 / INNER
                                   ).then_inc(s_rt, 1)

                rows(0, True)
                for g in range(GROUPS):
                    exps(g, 0)

                def chunk(c):
                    rows(c, False)
                    exps(0, c)
                    square(c - 1)
                    root(c - 1)
                    for g in range(1, GROUPS):
                        exps(g, c)

                with act.Fori(0, 4) as i:
                    chunk(i * 2 + 1)
                    chunk(i * 2 + 2)
                square(8)
                root(8)

            @block.gpsimd
            def _(pool):
                def chunk(b, c):
                    pool.wait_ge(s_rc, c + 1)
                    for g in range(GROUPS):
                        for d, left in enumerate((TRI_LE, TRI_GE)):
                            pool.wait_ge(s_seg, c * 8 + (2 * g + d - 1) if (g or d) else c * 8)
                            h0 = d * HEADS + g * GH
                            pool.tensor_tensor(tri_by[:, d, :, :], tri[:, left:left + 1, :].broadcast_to([P, GH, P]),
                                               rc[:, b, R_DA, h0:h0 + GH].unsqueeze(2).broadcast_to([P, GH, P]), ALU.mult
                                               ).then_inc(s_tr, 1)

                chunk(0, 0)
                with pool.Fori(0, 4) as i:
                    chunk(1, i * 2 + 1)
                    chunk(0, i * 2 + 2)

            @block.vector
            def _(dve):
                dve.memset(ones[:, :], 1.0).then_inc(s_one, 1)

                def get_rates(b, c, ctx_chunk):
                    if not ctx_chunk:
                        dve.wait_ge(s_tr, c * 8 - 8)
                        dve.wait_ge(s_yr, c * 4 - 4)
                        dve.wait_ge(s_new, c * 4 - 4)
                    src = rates[:, 0, :, :] if ctx_chunk else rates[:, bass.ds(c, 1), :, :].rearrange("p a b c -> p (a b) c")
                    dve.tensor_copy(rc[:, b, :, :], src).then_inc(s_rc, 1)

                def masks(c):
                    dve.wait_ge(s_cb, c + 1)
                    dve.wait_ge(s_mix, c * 4)
                    for d, left in enumerate((TRI_LE, TRI_GE)):
                        dve.tensor_tensor(cb[:, d, :, :], pb[:, 5, :].rearrange("p (a c) -> p a c", c=P),
                                          tri[:, left:left + 1, :].broadcast_to([P, GROUPS, P]), ALU.mult).then_inc(s_cbm, 1)

                def mixing(g, b, c):
                    for d in range(2):
                        dve.wait_ge(s_ex, c * 8 + (2 * g + d + 1))
                        if d == 0:
                            dve.wait_ge(s_cbm, c * 2 + 2)
                        for h in range(GH):
                            col = d * HEADS + g * GH + h
                            ins = dve.scalar_tensor_tensor(ex[:, d, h, :], ex[:, d, h, :], rc[:, b, R_DT, col:col + 1],
                                                           cb[:, d, g, :], ALU.mult, ALU.mult)
                        ins.then_inc(s_dve, 1)
                    dve.wait_ge(s_dve, c * 8 + (2 * g + 2))
                    dve.wait_ge(s_y, c * 4 + g)
                    dve.tensor_tensor(mix[:, :, :], ex[:, 0, :, :], ex[:, 1, :, :], ALU.add).then_inc(s_mix, 1)

                def weigh(g, b, c):
                    cols = slice(g * GW, (g + 1) * GW)
                    dve.wait_ge(s_row, c * 5 + (g + 1))
                    if g:
                        dve.wait_ge(s_con, c * 4 + (g - 4))
                    else:
                        dve.wait_ge(s_con, c * 4 - 4)
                    dve.tensor_tensor(by_head(xw[:, :]), by_head(xrow[:, cols]),
                                      per_head(rc[:, b, R_W, g * GH:(g + 1) * GH]), ALU.mult).then_inc(s_xw, 1)

                def combine(g, b, c, ctx_chunk):
                    cols = slice(g * GW, (g + 1) * GW)
                    if ctx_chunk:
                        dve.wait_ge(s_y, g + 1)
                        dve.tensor_copy(y[:, cols], pb[:, 4, :]).then_inc(s_yr, 1)
                        return
                    dve.wait_ge(s_off, c * 4 + (g - 3))
                    dve.wait_ge(s_yr, c * 4 + g)
                    dve.wait_ge(s_sum, c)
                    dve.wait_ge(s_new, c * 4 + g)
                    for d in range(2):
                        h0 = d * HEADS + g * GH
                        dve.tensor_tensor(by_head(tmp[:, d, :]), by_head(pb[:, 5 + d, :]),
                                          per_head(rc[:, b, R_IN, h0:h0 + GH]), ALU.mult).then_inc(s_cm, 1)
                    dve.tensor_tensor(by_head(state[:, cols]), by_head(state[:, cols]),
                                      per_head(rc[:, b, R_TOT, g * GH:(g + 1) * GH]), ALU.mult).then_inc(s_cm, 1)
                    dve.wait_ge(s_cm, c * 16 + (4 * g - 13))
                    dve.tensor_tensor(tmp[:, 0, :], tmp[:, 0, :], tmp[:, 1, :], ALU.add).then_inc(s_cm, 1)
                    dve.wait_ge(s_con, c * 4 + (g - 3))
                    dve.tensor_tensor(state[:, cols], state[:, cols], pb[:, 7, :], ALU.add).then_inc(s_new, 1)
                    dve.wait_ge(s_y, c * 4 + (g + 1))
                    if g == 0:
                        dve.wait_ge(s_red, c)
                    dve.wait_ge(s_cm, c * 16 + (4 * g - 12))
                    dve.tensor_tensor(y[:, cols], tmp[:, 0, :], pb[:, 4, :], ALU.add).then_inc(s_yr, 1)

                def gating(bt, t):
                    for q in range(4):
                        dve.wait_ge(s_yt, t * 4 + (q + 1))
                        if q == 0:
                            dve.wait_ge(s_pj, t)
                            dve.wait_ge(s_sq, t)
                        for a in range(4):
                            k = 4 * q + a
                            dve.scalar_tensor_tensor(yc[:, k, :], xbc[:, bt, k, :], keep["d_skip"][:, k:k + 1],
                                                     pb[:, 6 + q % 2, a * P:(a + 1) * P], ALU.mult, ALU.add).then_inc(s_yk, 1)
                    dve.wait_ge(s_yk, t * 16 + 16)
                    dve.wait_ge(s_z, t * 16 + 16)
                    dve.tensor_tensor(yc[:, :, :], yc[:, :, :], zt[:, :, :], ALU.mult).then_inc(s_zg, 1)

                def reduce(t):
                    dve.wait_ge(s_sq, t + 1)
                    dve.wait_ge(s_ss, t)
                    dve.tensor_reduce(red[:, :], sq.rearrange("p a c -> p c a"), AX.X, ALU.add).then_inc(s_red, 1)

                def residual(t, cond):
                    dve.wait_ge(s_yr, t * 4 + 4)
                    dve.wait_ge(s_new, t * 4 + 4)
                    dve.wait_ge(s_rt, t + 1)
                    dve.reciprocal(st[:, 1:2], st[:, 0:1]).then_inc(s_rcp, 1)
                    dve.wait_ge(s_rcp, t + 1)
                    dve.wait_ge(s_pj, t + 1)
                    dve.wait_ge(s_x, t * 16 + 16)
                    dve.scalar_tensor_tensor(tmp[:, :, :].rearrange("p a c -> p (a c)"), pb[:, 6:8, :].rearrange("p a c -> p (a c)"),
                                             st[:, 1:2], gate[:, cond, :], ALU.mult, ALU.mult).then_inc(s_pe, 1)
                    dve.wait_ge(s_pe, t + 1)
                    dve.tensor_tensor(xr[:, :], xr[:, :], tmp[:, :, :].rearrange("p a c -> p (a c)"), ALU.add).then_inc(s_sum, 1)

                get_rates(0, 0, True)
                dve.wait_ge(s_rc, 1)
                masks(0)
                mixing(0, 0, 0)
                for g in range(GROUPS):
                    if g < 3:
                        mixing(g + 1, 0, 0)
                    combine(g, 0, 0, True)
                for g in range(GROUPS):
                    dve.memset(tmp[0:1, 0, g:g + 1], 0.0).then_inc(s_new, 1)
                dve.wait_ge(s_w, 16)
                for k in range(Z_TILES):
                    dve.tensor_scalar(w[:, k, :], w[:, k, :], prm[:, 1, XBC_TILES + k:XBC_TILES + k + 1], None, ALU.mult
                                      ).then_inc(s_gw, 1)
                dve.wait_ge(s_gate, 32)

                def chunk(b, c, first):
                    get_rates(b, c, False)
                    masks(c)
                    gating(1 - b, c - 1)
                    dve.wait_ge(s_rc, c + 1)
                    mixing(0, b, c)
                    reduce(c - 1)
                    weigh(0, b, c)
                    residual(c - 1, CTX if first else LATENT)
                    if first:
                        dve.wait_ge(s_pe, c)
                        dve.tensor_copy(gate[:, CTX, :], gate[:, LATENT, :]).then_inc(s_gc, 1)
                    for g in range(GROUPS):
                        if g < 3:
                            mixing(g + 1, b, c)
                        combine(g, b, c, False)
                        if g < 3:
                            weigh(g + 1, b, c)

                with dve.Fori(0, 4) as i:
                    dve.wait_ge(s_gc, i)
                    chunk(1, i * 2 + 1, True)
                    chunk(0, i * 2 + 2, False)
                gating(0, 8)
                reduce(8)
                residual(8, LATENT)


def phase_final(nc, io, keep):
    x_rows = io["x_dram"].rearrange("(t p) d -> t p d", p=P)
    with ExitStack() as ctx:
        m = Mem(nc, ctx, "final_")
        x = m.sb("x", [P, TILES, D])
        squares = m.sb("squares", [P, TILES, D])
        g = m.sb("gain", [P, D])
        st = m.sb("stats", [P, TILES, 3])
        s_x = [m.sem(f"x_in{t}") for t in range(TILES)]
        s_g = m.sem("gain_in")
        s_sq = m.sem("squared")
        s_root = m.sem("root_ready")
        s_rcp = m.sem("reciprocal_ready")
        s_y = m.sem("y_ready")
        s_out = m.sem("y_stored")

        with nc.Block() as block:

            @block.sync
            def _(sp):
                sp.dma_start(x[:, 0, :], x_rows[0]).then_inc(s_x[0], 16)
                sp.dma_start(g[:, :], io["final_norm_g"].rearrange("(a d) -> a d", a=1).partition_broadcast(P)).then_inc(s_g, 16)
                for t in range(1, TILES):
                    sp.dma_start(x[:, t, :], x_rows[t]).then_inc(s_x[t], 16)
                for t in range(TILES):
                    sp.wait_ge(s_y, t + 1)
                    dst = io["y_prompt"][0] if t == 0 else io["y_sample"][0, (t - 1) * P:t * P, :]
                    sp.dma_start(dst, x[:, t, :]).then_inc(s_out, 16)
                sp.wait_ge(s_out, 16 * TILES)

            @block.scalar
            def _(act):
                for t in range(TILES):
                    act.wait_ge(s_x[t], 16)
                    act.activation(squares[:, t, :], x[:, t, :], ACT.Square, accum_out=st[:, t, 0:1]).then_inc(s_sq, 1)
                    act.wait_ge(s_sq, t + 1)
                    act.activation(st[:, t, 1:2], st[:, t, 0:1], ACT.Sqrt, bias=keep["eps"][:, 0:1], scale=1.0 / D
                                   ).then_inc(s_root, 1)

            @block.vector
            def _(dve):
                dve.wait_ge(s_g, 16)
                for t in range(TILES):
                    dve.wait_ge(s_root, t + 1)
                    dve.reciprocal(st[:, t, 2:3], st[:, t, 1:2]).then_inc(s_rcp, 1)
                    dve.wait_ge(s_rcp, t + 1)
                    dve.scalar_tensor_tensor(x[:, t, :], x[:, t, :], st[:, t, 2:3], g[:, :], ALU.mult, ALU.mult
                                             ).then_inc(s_y, 1)


def build(nc, io):
    with ExitStack() as ctx:
        m = Mem(nc, ctx)
        tri = m.sb("tri", [P, 5, P])
        keep = {
            "tri": tri, "ident": tri[:, 0, :],
            "eps": m.sb("eps", [P, 1]),
            "prm": m.sb("prm", [P, 4, 120]),
            "mod": m.sb("mod", [P, 2, 96]),
            "gain1": m.sb("gain1", [P, 2, 2, KD]),
            "d_skip": m.sb("d_skip", [P, Z_TILES]),
            "s_const": m.sem("const_in"),
        }
        rows = lambda a: a.rearrange("w (t p) -> (w t) p", p=P)
        keep["param_rows"] = [
            (rows(io["ssd_conv_w"][0]), (0, 0), 120),
            (rows(io["ssd_conv_b"]), (1, 0), 24), (rows(io["ssd_norm_g"]), (1, 24), 16),
            (rows(io["hy_short_w"][0]), (2, 0), 72), (rows(io["hy_in_b"]), (2, 72), 24),
            (rows(io["hy_short_b"]), (2, 96), 24),
            (rows(io["norm_g"][0, 0:1, :]), (3, 0), 8), (rows(io["norm_g"][1, 0:1, :]), (3, 8), 8),
        ]
        keep["param_counts"] = (120, 40, 120, 16)
        with nc.Block() as block:
            @block.sync
            def _(sp):
                sp.dma_start(tri[:, :, :], io["tri"].rearrange("p (a b) -> p a b", b=P)).then_inc(keep["s_const"], 16)
        filt_scope = ctx.enter_context(ExitStack())
        keep["filt"] = filt_scope.enter_context(nc.sbuf_tensor("filt", [HY_HID, TAPS], F32))
        phase_modulation(nc, io, keep)
        with ExitStack() as inner:
            keep["hT"] = [inner.enter_context(nc.sbuf_tensor(f"h0_{part}", [P, KD, TOK], F32R)) for part in ("leading", "trailing")]
            phase_norm(nc, io, keep, 0)
            phase_hyena_in(nc, io, keep)
        phase_long_conv(nc, io, keep)
        filt_scope.close()
        phase_hyena_out(nc, io, keep)
        mixture(nc, io, keep, 0)
        with ExitStack() as ssd:
            keep["rates"] = ssd.enter_context(nc.sbuf_tensor("rates", [P, TILES, 5, 2 * HEADS], F32))
            with ExitStack() as inner:
                keep["hT"] = [inner.enter_context(nc.sbuf_tensor(f"h1_{part}", [P, KD, TOK], F32R)) for part in ("leading", "trailing")]
                phase_norm(nc, io, keep, 1)
                phase_ssd_in(nc, io, keep)
            keep["state"] = ssd.enter_context(nc.sbuf_tensor("state", [P, INNER], F32))
            phase_states(nc, io, keep)
            phase_scan(nc, io, keep)
        mixture(nc, io, keep, 1)
        phase_final(nc, io, keep)


def shape_constants():
    r = np.arange(P)
    tri = np.stack([r[:, None] == r, r[:, None] <= r, r[:, None] > r, r[:, None] >= r, r[:, None] < r], 1)
    q = D // 4
    omega = (1.0 / (10000.0 ** (np.arange(q, dtype=np.float32) / np.float32(q)))).astype(np.float32)
    t = np.arange(LAT)
    er = (t // 64).astype(np.float32)[:, None] * omega
    ec = (t % 64).astype(np.float32)[:, None] * omega
    pos = np.concatenate([np.sin(er), np.cos(er), np.sin(ec), np.cos(ec)], -1)

    def clock(n):
        at = np.concatenate([np.arange(n), n - np.arange(n)])
        at[n] = 0
        tt = np.linspace(0.0, 1.0, n, dtype=np.float32)[:, None]
        w = (2.0 * np.pi * np.arange(n, dtype=np.float32)[:, None] / n).astype(np.float32)
        f = np.linspace(1e-4, 15, 16, dtype=np.float32)[None]
        z = np.concatenate([tt, np.cos(f * w), -np.sin(f * w)], -1)
        return z[at].T, tt[at, 0]

    z1, t1 = clock(LAT)
    z2, t2 = clock(CTX_ROWS)
    zfeat = np.concatenate([z1, z2], 1)
    negt = -np.concatenate([t1, t2]).reshape(18, P).T
    deltas = np.abs(np.linspace(np.log(1e-2) / 1.5, np.log(1e-2) / 0.3, D, dtype=np.float32))[None]

    b = np.arange(256)
    ang = lambda k, r_: 2 * np.pi * ((b[:, None] * (8 * k[None] + r_)) % NFFT) / NFFT
    k1, k2 = np.arange(128), np.arange(256)
    f0 = np.concatenate([np.cos(ang(k1, 0)), -np.sin(ang(k1, 0))], 1)
    f0[:, 128] = (-1.0) ** b
    f4 = np.concatenate([np.cos(ang(k1, 4)), -np.sin(ang(k1, 4))], 1)
    fwd = [f0, f4] + [x for r_ in (2, 1, 3) for x in (np.cos(ang(k2, r_)), np.sin(ang(k2, r_)), -np.sin(ang(k2, r_)))]
    fwd = np.concatenate(fwd, 1).reshape(2, P, -1).transpose(1, 0, 2)
    g0 = np.concatenate([np.cos(ang(k1, 0)), -np.sin(ang(k1, 0))], 1).T * 2
    g0[0] = 1.0
    g0[128] = (-1.0) ** b
    g4 = np.concatenate([np.cos(ang(k1, 4)), -np.sin(ang(k1, 4))], 1).T * 2
    inv04 = np.stack([g0, g4]).reshape(2, 2, P, 256).transpose(2, 0, 1, 3) / NFFT
    inv = []
    for r_ in (2, 1, 3):
        c, s = np.cos(ang(k2, r_)).T, np.sin(ang(k2, r_)).T
        inv.append(np.concatenate([np.concatenate([c, s], 1), np.concatenate([-s, c], 1)], 0).reshape(4, P, 512))
    inv = np.stack(inv).transpose(2, 0, 1, 3) * 2 / NFFT
    f32 = lambda a: np.ascontiguousarray(a, dtype=np.float32)
    return {"tri": f32(tri.reshape(P, -1)), "pos": f32(pos), "zfeat": f32(zfeat), "negt": f32(negt), "deltas": f32(deltas),
            "fwd": f32(fwd.reshape(P, -1)), "inv04": f32(inv04.reshape(P, -1)), "inv": f32(inv.reshape(P, -1))}


INPUTS = ["x_prompt", "x_sample", "state_ssd", "c", "c_ctx", "norm_g", "ada_w", "ada_b",
          "hy_in_w", "hy_in_b", "hy_short_w", "hy_short_b", "hy_f_w1", "hy_f_b1", "hy_f_w2", "hy_f_b2",
          "hy_f_w3", "hy_f_freq", "hy_f_bias", "hy_out_w",
          "ssd_in_w", "ssd_conv_w", "ssd_conv_b", "ssd_dt_bias", "ssd_A_log", "ssd_D", "ssd_norm_g", "ssd_out_w",
          "moe_router", "moe_w_gate", "moe_w_up", "moe_w_down", "final_norm_g"]
OUTPUTS = {"y_prompt": (1, CTX_ROWS, D), "y_sample": (1, LAT, D), "new_state": (1, 1, 2, HEADS, HEAD, 128)}
SCRATCH = {"mod_dram": (2, 12 * D), "vec_dram": (2, 2, 4, D), "x_dram": (TOK, D), "h_dram": (TOK, D),
           "x0_dram": (KD, P, GAPPED), "u_dram": (P, TILES, D), "g_dram": (KD, P, TOK),
           "xbc_dram": (TILES, P, XBC_TILES, P), "z_dram": (TILES, P, Z_TILES, P), "sb_dram": (TILES, P, INNER)}


def lay_out(nc, inputs):
    arrays = {f"in_{n}": np.ascontiguousarray(inputs[n]) for n in INPUTS}
    arrays.update({f"in_{n}": a for n, a in shape_constants().items()})
    io = {n[3:]: nc.dram_tensor(n, a.shape, F32, kind="ExternalInput").ap() for n, a in arrays.items()}
    io.update({n: nc.dram_tensor(f"out_{n}", s, F32, kind="ExternalOutput").ap() for n, s in OUTPUTS.items()})
    io.update({n: nc.dram_tensor(n, s, F32, kind="Internal").ap() for n, s in SCRATCH.items()})
    return arrays, io


def kernel(**inputs):
    import concourse.bacc as bacc
    from concourse.bass_utils import run_bass_kernel_spmd

    nc = bacc.Bacc("TRN2", target_bir_lowering=False, num_devices=1)
    arrays, io = lay_out(nc, inputs)
    build(nc, io)
    r = run_bass_kernel_spmd(nc, [arrays], core_ids=[0])
    return tuple(r.results[0][f"out_{n}"] for n in OUTPUTS)
```
